# Optimizing a Trainium2 kernel written in Bass

```python
import jax, jax.numpy as jnp
from jax import lax
import numpy as np
import jax
import jax.numpy as jnp

D_MODEL = 1024
BATCH = 1
SEQ = 512
DEPTH = 1

CHUNK = 64
N_META = 16
EPS = 1e-6

POOL_GROUPS = 4
POOL_WINDOWS = (2, 4, 8, 16)
POOL_WIDTH = D_MODEL // 4
POOL_GDIM = POOL_WIDTH // POOL_GROUPS
CONV_WIDTH = D_MODEL // 4
CONV_KSIZE = 31
FOX_HEADS = 8
FOX_HEAD_DIM = 64
FOX_WIDTH = FOX_HEADS * FOX_HEAD_DIM
Q_BLOCK = 128
N_BRANCH = 3
IN_SPLITS = (POOL_WIDTH, CONV_WIDTH, CONV_WIDTH, FOX_WIDTH, FOX_WIDTH, FOX_WIDTH, FOX_HEADS, N_BRANCH * D_MODEL)
N_IN = sum(IN_SPLITS)
N_GROUPS = 4
EXPERTS_PER_GROUP = 4
N_EXPERTS = N_GROUPS * EXPERTS_PER_GROUP
TOP_K = 2
EXPERT_HIDDEN = D_MODEL // 4


def rms_norm(x, g):
    xf = x.astype(jnp.float32)
    y = xf * lax.rsqrt(jnp.mean(xf * xf, axis=-1, keepdims=True) + EPS)
    return (y * g.astype(jnp.float32)).astype(x.dtype)

def layer_norm(x, g, b):
    xf = x.astype(jnp.float32)
    mu = jnp.mean(xf, axis=-1, keepdims=True)
    var = jnp.mean(jnp.square(xf - mu), axis=-1, keepdims=True)
    y = (xf - mu) * lax.rsqrt(var + EPS)
    return (y * g.astype(jnp.float32) + b.astype(jnp.float32)).astype(x.dtype)

def pool_mixer(a, pool_w, pool_b, pool_scale):
    B_, L, _ = a.shape
    af = a.astype(jnp.float32).reshape(B_, L, POOL_GROUPS, POOL_GDIM)
    cs = jnp.concatenate([jnp.zeros_like(af[:, :1]), jnp.cumsum(af, axis=1)], axis=1)
    t = jnp.arange(L, dtype=jnp.int32)[:, None]
    win = jnp.array(POOL_WINDOWS, dtype=jnp.int32)[None, :]
    lo = jnp.maximum(t + 1 - win, 0)
    cnt = (t + 1 - lo).astype(jnp.float32)
    grp = jnp.arange(POOL_GROUPS, dtype=jnp.int32)[None, :]
    mean = (cs[:, 1:] - cs[:, lo, grp]) / cnt[None, :, :, None]
    diff = mean - af
    y = jnp.einsum('blgc,gcd->blgd', diff, pool_w.astype(jnp.float32)) + pool_b.astype(jnp.float32)
    y = y.reshape(B_, L, POOL_WIDTH) * pool_scale.astype(jnp.float32)
    return y.astype(a.dtype)

def conv_module(bv, bg, conv_w, conv_b, ln_g, ln_b):
    glu = bv * jax.nn.sigmoid(bg)
    y = lax.conv_general_dilated(
        glu, conv_w.astype(glu.dtype)[:, None, :], window_strides=(1,),
        padding=[(CONV_KSIZE - 1, 0)], dimension_numbers=('NWC', 'WIO', 'NWC'),
        feature_group_count=CONV_WIDTH)
    y = y + conv_b.astype(y.dtype)
    y = layer_norm(y, ln_g, ln_b)
    return jax.nn.silu(y)

def forgetting_attention(q, k, v, logf):
    B_, L, H, dh = q.shape
    n_blk = -(-L // Q_BLOCK)
    Lp = n_blk * Q_BLOCK
    pad = Lp - L
    qh = jnp.pad(q.transpose(0, 2, 1, 3), ((0, 0), (0, 0), (0, pad), (0, 0)))
    kh = jnp.pad(k.transpose(0, 2, 1, 3), ((0, 0), (0, 0), (0, pad), (0, 0)))
    vh = jnp.pad(v.transpose(0, 2, 1, 3), ((0, 0), (0, 0), (0, pad), (0, 0)))
    F = jnp.cumsum(jnp.pad(logf.transpose(0, 2, 1), ((0, 0), (0, 0), (0, pad))), axis=-1)
    qb = qh.reshape(B_, H, n_blk, Q_BLOCK, dh).transpose(2, 0, 1, 3, 4)
    Fq = F.reshape(B_, H, n_blk, Q_BLOCK).transpose(2, 0, 1, 3)
    qpos = jnp.arange(Lp, dtype=jnp.int32).reshape(n_blk, Q_BLOCK)
    kpos = jnp.arange(Lp, dtype=jnp.int32)
    scale = FOX_HEAD_DIM ** -0.5

    def block(args):
        qi, Fi, pi = args
        s = jnp.einsum('bhqd,bhkd->bhqk', qi, kh, preferred_element_type=jnp.float32) * scale
        s = s + Fi[..., None] - F[:, :, None, :]
        s = jnp.where(kpos[None, :] <= pi[:, None], s, -jnp.inf)
        p = jax.nn.softmax(s, axis=-1)
        return jnp.einsum('bhqk,bhkd->bhqd', p.astype(vh.dtype), vh)

    o = lax.map(block, (qb, Fq, qpos))
    o = o.transpose(1, 0, 3, 2, 4).reshape(B_, Lp, H * dh)
    return o[:, :L]

def mixer_layer(u, w_in, b_forget, pool_w, pool_b, pool_scale, conv_w, conv_b, conv_ln_g, conv_ln_b,
                w_out_a, w_out_b, w_out_c, w_o):
    B_, L, D = u.shape
    p = u @ w_in
    a, bv, bg, q, k, v, fg, gates = jnp.split(p, [int(i) for i in np.cumsum(IN_SPLITS)[:-1]], axis=-1)
    ya = pool_mixer(a, pool_w, pool_b, pool_scale) @ w_out_a
    yb = conv_module(bv, bg, conv_w, conv_b, conv_ln_g, conv_ln_b) @ w_out_b
    logf = jax.nn.log_sigmoid((fg + b_forget).astype(jnp.float32))
    heads = lambda z: z.reshape(B_, L, FOX_HEADS, FOX_HEAD_DIM)
    yc = forgetting_attention(heads(q), heads(k), heads(v), logf) @ w_out_c
    g = jax.nn.sigmoid(gates.reshape(B_, L, N_BRANCH, D))
    merged = g[:, :, 0] * ya + g[:, :, 1] * yb + g[:, :, 2] * yc
    return merged @ w_o

def hier_moe(h, router_g, router_g_b, router_e, router_e_b, exp_w1, exp_w3, exp_w2):
    B_, L, D = h.shape
    t = h.reshape(B_ * L, D)
    T = t.shape[0]
    glog = (t @ router_g).astype(jnp.float32) + router_g_b.astype(jnp.float32)
    gprob = jax.nn.softmax(glog, axis=-1)
    _, gsel = lax.top_k(glog, 1)
    gw = jnp.take_along_axis(gprob, gsel, axis=-1)
    elog = ((t @ router_e).astype(jnp.float32) + router_e_b.astype(jnp.float32)).reshape(T, N_GROUPS, EXPERTS_PER_GROUP)
    elog_sel = jnp.take_along_axis(elog, gsel[:, :, None], axis=1)[:, 0]
    eprob = jax.nn.softmax(elog_sel, axis=-1)
    top_p, top_i = lax.top_k(eprob, TOP_K)
    top_p = top_p / jnp.sum(top_p, axis=-1, keepdims=True)
    w_grp = jnp.sum(jax.nn.one_hot(top_i, EXPERTS_PER_GROUP, dtype=jnp.float32) * top_p[..., None], axis=1)
    comb = (jax.nn.one_hot(gsel[:, 0], N_GROUPS, dtype=jnp.float32)[:, :, None] * w_grp[:, None, :] * gw[:, :, None])
    comb = comb.reshape(T, N_EXPERTS).astype(t.dtype)
    y = jnp.zeros_like(t)
    for e in range(N_EXPERTS):
        he = jax.nn.silu(t @ exp_w1[e]) * (t @ exp_w3[e])
        y = y + comb[:, e:e + 1] * (he @ exp_w2[e])
    return y.reshape(B_, L, D)

def first_inputs(seed: int = 0) -> dict:
    key = jax.random.key(seed)
    ks = jax.random.split(key, 32)
    f32 = jnp.float32
    nrm = lambda k, shape, s: (jax.random.normal(k, shape, f32) * s).astype(f32)
    D = D_MODEL
    return {
        "x": nrm(ks[0], (BATCH, SEQ, D), 1.0),
        "meta": nrm(ks[1], (N_META, D), 1.0),
        "norm1_g": 1.0 + nrm(ks[2], (DEPTH, D), 0.02),
        "w_in": nrm(ks[3], (DEPTH, D, N_IN), D ** -0.5),
        "b_forget": jax.random.uniform(ks[4], (DEPTH, FOX_HEADS), f32, 1.0, 6.0),
        "pool_w": nrm(ks[5], (DEPTH, POOL_GROUPS, POOL_GDIM, POOL_GDIM), POOL_GDIM ** -0.5),
        "pool_b": nrm(ks[6], (DEPTH, POOL_GROUPS, POOL_GDIM), 0.01),
        "pool_scale": 1.0 + nrm(ks[7], (DEPTH, POOL_WIDTH), 0.1),
        "conv_w": nrm(ks[8], (DEPTH, CONV_KSIZE, CONV_WIDTH), CONV_KSIZE ** -0.5),
        "conv_b": nrm(ks[9], (DEPTH, CONV_WIDTH), 0.01),
        "conv_ln_g": 1.0 + nrm(ks[10], (DEPTH, CONV_WIDTH), 0.02),
        "conv_ln_b": nrm(ks[11], (DEPTH, CONV_WIDTH), 0.01),
        "w_out_a": nrm(ks[12], (DEPTH, POOL_WIDTH, D), POOL_WIDTH ** -0.5),
        "w_out_b": nrm(ks[13], (DEPTH, CONV_WIDTH, D), CONV_WIDTH ** -0.5),
        "w_out_c": nrm(ks[14], (DEPTH, FOX_WIDTH, D), FOX_WIDTH ** -0.5),
        "w_o": nrm(ks[15], (DEPTH, D, D), D ** -0.5),
        "norm2_g": 1.0 + nrm(ks[16], (DEPTH, D), 0.02),
        "router_g": nrm(ks[17], (DEPTH, D, N_GROUPS), D ** -0.5),
        "router_g_b": nrm(ks[18], (DEPTH, N_GROUPS), 0.01),
        "router_e": nrm(ks[19], (DEPTH, D, N_EXPERTS), D ** -0.5),
        "router_e_b": nrm(ks[20], (DEPTH, N_EXPERTS), 0.01),
        "exp_w1": nrm(ks[21], (DEPTH, N_EXPERTS, D, EXPERT_HIDDEN), D ** -0.5),
        "exp_w3": nrm(ks[22], (DEPTH, N_EXPERTS, D, EXPERT_HIDDEN), D ** -0.5),
        "exp_w2": nrm(ks[23], (DEPTH, N_EXPERTS, EXPERT_HIDDEN, D), EXPERT_HIDDEN ** -0.5),
        "final_g": 1.0 + nrm(ks[24], (D,), 0.02),
    }

def first_block(x, meta, norm1_g, w_in, b_forget, pool_w, pool_b, pool_scale, conv_w, conv_b, conv_ln_g,
              conv_ln_b, w_out_a, w_out_b, w_out_c, w_o, norm2_g, router_g, router_g_b, router_e,
              router_e_b, exp_w1, exp_w3, exp_w2, final_g):
    B_ = x.shape[0]
    m = jnp.broadcast_to(meta.astype(x.dtype)[None], (B_, N_META, D_MODEL))
    h = jnp.concatenate([m, x], axis=1)
    for l in range(DEPTH):
        u = rms_norm(h, norm1_g[l])
        h = h + mixer_layer(u, w_in[l], b_forget[l], pool_w[l], pool_b[l], pool_scale[l], conv_w[l],
                            conv_b[l], conv_ln_g[l], conv_ln_b[l], w_out_a[l], w_out_b[l], w_out_c[l], w_o[l])
        v = rms_norm(h, norm2_g[l])
        h = h + hier_moe(v, router_g[l], router_g_b[l], router_e[l], router_e_b[l], exp_w1[l], exp_w3[l], exp_w2[l])
    return rms_norm(h[:, N_META:], final_g)


DEPTH_2 = 2

HEAD_DIM = 64
N_HEADS = D_MODEL // HEAD_DIM
A_KV_HEADS = 4
CMP_BLOCK = 32
CMP_STRIDE = 16
CMP_HIDDEN = 256
SEL_BLOCK = 64
N_SELECT = 16
WINDOW_A = 512
QUERY_BLOCK = 128
B_KV_HEADS = 2
WINDOW_B = 128
N_A_LAYERS = max(1, DEPTH_2 // 2)
D_FF = 2816
CONV_WIDTH_2 = 3
ROPE_THETA = 10000.0
NEG = -1e30
FORCE = 1e6
A_SPLIT = [N_HEADS * HEAD_DIM] + [A_KV_HEADS * HEAD_DIM] * 6 + [3 * N_HEADS]
A_IN_COLS = sum(A_SPLIT)


def rms_norm_2(x, g):
    xf = x.astype(jnp.float32)
    y = xf * lax.rsqrt(jnp.mean(xf * xf, axis=-1, keepdims=True) + EPS)
    return (y * g.astype(jnp.float32)).astype(x.dtype)

def rope(x, pos):
    half = HEAD_DIM // 2
    inv = jnp.float32(ROPE_THETA) ** (-jnp.arange(half, dtype=jnp.float32) / half)
    ang = pos.astype(jnp.float32)[:, None] * inv[None, :]
    cos = jnp.cos(ang)[None, :, None, :]
    sin = jnp.sin(ang)[None, :, None, :]
    xf = x.astype(jnp.float32)
    x1, x2 = xf[..., :half], xf[..., half:]
    return jnp.concatenate([x1 * cos - x2 * sin, x2 * cos + x1 * sin], axis=-1).astype(x.dtype)

def compress(k, pos_emb, w1, w2):
    b, s, g, dh = k.shape
    nseg = s // CMP_STRIDE
    r = CMP_BLOCK // CMP_STRIDE
    nc = nseg - r + 1
    seg = k.reshape(b, nseg, CMP_STRIDE, g, dh)
    blocks = jnp.concatenate([seg[:, i:i + nc] for i in range(r)], axis=2)
    blocks = blocks + pos_emb[None, None, :, None, :]
    flat = blocks.transpose(0, 1, 3, 2, 4).reshape(b, nc, g, CMP_BLOCK * dh)
    return jax.nn.gelu(flat @ w1) @ w2

def _sel_weights():
    r_c = CMP_BLOCK // CMP_STRIDE
    r_s = SEL_BLOCK // CMP_STRIDE
    ws = []
    for o in range(-(r_c - 1), r_s):
        lo = max(o * CMP_STRIDE, 0)
        hi = min(o * CMP_STRIDE + CMP_BLOCK, SEL_BLOCK)
        ws.append(max(hi - lo, 0) // CMP_STRIDE)
    return ws

def block_importance(p, n_sel):
    r_c = CMP_BLOCK // CMP_STRIDE
    r_s = SEL_BLOCK // CMP_STRIDE
    ws = _sel_weights()
    front = r_c - 1
    span = r_s * (n_sel - 1) + 1
    back = max(len(ws) - 1 + span - front - p.shape[-1], 0)
    pp = jnp.pad(p, [(0, 0)] * (p.ndim - 1) + [(front, back)])
    out = ws[0] * pp[..., 0:span:r_s]
    for i in range(1, len(ws)):
        out = out + ws[i] * pp[..., i:i + span:r_s]
    return out

def nsa_mixer(h, w_in, cmp_pos, cmp_w1, cmp_w2, w_out):
    b, s, _ = h.shape
    g_n = A_KV_HEADS
    r_n = N_HEADS // g_n
    dh = HEAD_DIM
    split_idx = np.cumsum(A_SPLIT)[:-1].tolist()
    q, kc, vc, ks, vs, kw, vw, gl = jnp.split(h @ w_in, split_idx, axis=-1)
    pos = jnp.arange(s)
    q = rope(q.reshape(b, s, N_HEADS, dh), pos)
    kc = kc.reshape(b, s, g_n, dh)
    vc = vc.reshape(b, s, g_n, dh)
    ks = rope(ks.reshape(b, s, g_n, dh), pos)
    vs = vs.reshape(b, s, g_n, dh)
    kw = rope(kw.reshape(b, s, g_n, dh), pos)
    vw = vw.reshape(b, s, g_n, dh)
    kc_c = compress(kc, cmp_pos[0], cmp_w1[0], cmp_w2[0])
    vc_c = compress(vc, cmp_pos[1], cmp_w1[1], cmp_w2[1])
    nc = kc_c.shape[1]
    cmp_end = jnp.arange(nc) * CMP_STRIDE + CMP_BLOCK - 1
    kc_c = rope(kc_c, cmp_end)
    gates = jax.nn.sigmoid(gl.astype(jnp.float32)).astype(h.dtype)
    gh = gates.reshape(b, s, g_n, r_n, 3).transpose(0, 2, 3, 1, 4)
    qh = q.reshape(b, s, g_n, r_n, dh).transpose(0, 2, 3, 1, 4)
    kc_h = kc_c.transpose(0, 2, 1, 3)
    vc_h = vc_c.transpose(0, 2, 1, 3)
    n_sel = s // SEL_BLOCK
    ks_b = ks.transpose(0, 2, 1, 3).reshape(b, g_n, n_sel, SEL_BLOCK, dh)
    vs_b = vs.transpose(0, 2, 1, 3).reshape(b, g_n, n_sel, SEL_BLOCK, dh)
    pad_w = ((0, 0), (0, 0), (WINDOW_A, 0), (0, 0))
    kw_p = jnp.pad(kw.transpose(0, 2, 1, 3), pad_w)
    vw_p = jnp.pad(vw.transpose(0, 2, 1, 3), pad_w)
    top = min(N_SELECT, n_sel)
    scale = dh ** -0.5
    bi = jnp.arange(b)[:, None, None, None]
    gi = jnp.arange(g_n)[None, :, None, None]
    sel_j = jnp.arange(n_sel)
    sel_c = jnp.arange(SEL_BLOCK)

    def one_block(qb):
        start = qb * QUERY_BLOCK
        t = start + jnp.arange(QUERY_BLOCK)
        qq = lax.dynamic_slice_in_dim(qh, start, QUERY_BLOCK, axis=3)
        gg = lax.dynamic_slice_in_dim(gh, start, QUERY_BLOCK, axis=3)
        sc = jnp.einsum('bgrqd,bgnd->bgrqn', qq, kc_h).astype(jnp.float32) * scale
        valid = cmp_end[None, :] <= t[:, None]
        p_c = jax.nn.softmax(jnp.where(valid, sc, NEG), axis=-1) * valid
        o_c = jnp.einsum('bgrqn,bgnd->bgrqd', p_c.astype(vc_h.dtype), vc_h)
        imp = block_importance(p_c.sum(axis=2), n_sel)
        cur = t // SEL_BLOCK
        forced = (sel_j[None, :] == 0) | (sel_j[None, :] == cur[:, None]) | (sel_j[None, :] == cur[:, None] - 1)
        causal_blk = sel_j[None, :] * SEL_BLOCK <= t[:, None]
        imp = jnp.where(forced, FORCE, jnp.where(causal_blk, imp, -FORCE))
        _, idx = lax.top_k(imp, top)
        k_sel = ks_b[bi, gi, idx]
        v_sel = vs_b[bi, gi, idx]
        kpos = idx[..., None] * SEL_BLOCK + sel_c
        m_sel = (kpos <= t[:, None, None])[:, :, None]
        ss = jnp.einsum('bgrqd,bgqkcd->bgrqkc', qq, k_sel).astype(jnp.float32) * scale
        ss = jnp.where(m_sel, ss, NEG).reshape(b, g_n, r_n, QUERY_BLOCK, top * SEL_BLOCK)
        p_s = jax.nn.softmax(ss, axis=-1).reshape(b, g_n, r_n, QUERY_BLOCK, top, SEL_BLOCK)
        o_s = jnp.einsum('bgrqkc,bgqkcd->bgrqd', p_s.astype(v_sel.dtype), v_sel)
        kwb = lax.dynamic_slice_in_dim(kw_p, start, QUERY_BLOCK + WINDOW_A, axis=2)
        vwb = lax.dynamic_slice_in_dim(vw_p, start, QUERY_BLOCK + WINDOW_A, axis=2)
        wpos = start - WINDOW_A + jnp.arange(QUERY_BLOCK + WINDOW_A)
        dist = t[:, None] - wpos[None, :]
        m_w = (dist >= 0) & (dist < WINDOW_A) & (wpos[None, :] >= 0)
        sw = jnp.einsum('bgrqd,bgkd->bgrqk', qq, kwb).astype(jnp.float32) * scale
        p_w = jax.nn.softmax(jnp.where(m_w, sw, NEG), axis=-1)
        o_w = jnp.einsum('bgrqk,bgkd->bgrqd', p_w.astype(vwb.dtype), vwb)
        return gg[..., 0:1] * o_c + gg[..., 1:2] * o_s + gg[..., 2:3] * o_w

    out = lax.map(one_block, jnp.arange(s // QUERY_BLOCK))
    out = out.transpose(1, 0, 4, 2, 3, 5).reshape(b, s, N_HEADS * dh)
    return out @ w_out

def shared_kv(h, kv_norm, w_kv):
    b, s, _ = h.shape
    k, v = jnp.split(rms_norm_2(h, kv_norm) @ w_kv, 2, axis=-1)
    k = rope(k.reshape(b, s, B_KV_HEADS, HEAD_DIM), jnp.arange(s))
    v = v.reshape(b, s, B_KV_HEADS, HEAD_DIM)
    return k, v

def _with_prev_block(xb):
    pad = [(0, 0), (1, 0)] + [(0, 0)] * (xb.ndim - 2)
    return jnp.concatenate([jnp.pad(xb, pad)[:, :-1], xb], axis=2)

def swa_sink_mixer(h, k, v, w_q, sinks, w_out):
    b, s, _ = h.shape
    g_n = B_KV_HEADS
    r_n = N_HEADS // g_n
    w = WINDOW_B
    nb = s // w
    q = rope((h @ w_q).reshape(b, s, N_HEADS, HEAD_DIM), jnp.arange(s))
    qb = q.reshape(b, nb, w, g_n, r_n, HEAD_DIM)
    kk = _with_prev_block(k.reshape(b, nb, w, g_n, HEAD_DIM))
    vv = _with_prev_block(v.reshape(b, nb, w, g_n, HEAD_DIM))
    sc = jnp.einsum('bnqgrd,bnkgd->bgrnqk', qb, kk).astype(jnp.float32) * (HEAD_DIM ** -0.5)
    qi = jnp.arange(w)[:, None]
    ki = jnp.arange(2 * w)[None, :]
    rel = qi + w - ki
    band = (rel >= 0) & (rel < w)
    exists = (jnp.arange(nb)[:, None, None] > 0) | (ki[None] >= w)
    mask = band[None] & exists
    sc = jnp.where(mask, sc, NEG)
    sink = sinks.astype(jnp.float32).reshape(1, g_n, r_n, 1, 1, 1)
    mx = jnp.maximum(sc.max(axis=-1, keepdims=True), sink)
    e = jnp.exp(sc - mx)
    p = e / (e.sum(axis=-1, keepdims=True) + jnp.exp(sink - mx))
    o = jnp.einsum('bgrnqk,bnkgd->bnqgrd', p.astype(vv.dtype), vv)
    return o.reshape(b, s, N_HEADS * HEAD_DIM) @ w_out

def conv_ffn(h, w_in, conv_w, conv_b, w_out):
    s = h.shape[1]
    u = h @ w_in
    up = jnp.pad(u, ((0, 0), (CONV_WIDTH_2 - 1, 0), (0, 0)))
    c = conv_b + conv_w[0] * up[:, 0:s]
    for i in range(1, CONV_WIDTH_2):
        c = c + conv_w[i] * up[:, i:i + s]
    a, gate_in = jnp.split(c, 2, axis=-1)
    return (jax.nn.silu(a) * gate_in) @ w_out

def second_inputs(seed: int = 0) -> dict:
    key = jax.random.key(seed)
    ks = jax.random.split(key, 18)
    d = D_MODEL
    n_a = N_A_LAYERS
    n_b = DEPTH_2 - N_A_LAYERS
    f32 = jnp.float32

    def w(k, shape, fan_in):
        return jax.random.normal(k, shape, f32) * (fan_in ** -0.5)

    def gain(k, shape):
        return 1.0 + 0.02 * jax.random.normal(k, shape, f32)

    return {
        'x': jax.random.normal(ks[0], (BATCH, SEQ, d), f32),
        'norm_attn': gain(ks[1], (DEPTH_2, d)),
        'norm_ffn': gain(ks[2], (DEPTH_2, d)),
        'a_w_in': w(ks[3], (n_a, d, A_IN_COLS), d),
        'a_cmp_pos': 0.1 * jax.random.normal(ks[4], (n_a, 2, CMP_BLOCK, HEAD_DIM), f32),
        'a_cmp_w1': w(ks[5], (n_a, 2, CMP_BLOCK * HEAD_DIM, CMP_HIDDEN), CMP_BLOCK * HEAD_DIM),
        'a_cmp_w2': w(ks[6], (n_a, 2, CMP_HIDDEN, HEAD_DIM), CMP_HIDDEN),
        'a_w_out': w(ks[7], (n_a, d, d), d),
        'kv_norm': gain(ks[8], (d,)),
        'b_w_kv': w(ks[9], (d, 2 * B_KV_HEADS * HEAD_DIM), d),
        'b_w_q': w(ks[10], (n_b, d, d), d),
        'b_sinks': jax.random.normal(ks[11], (n_b, N_HEADS), f32),
        'b_w_out': w(ks[12], (n_b, d, d), d),
        'ffn_w_in': w(ks[13], (DEPTH_2, d, 2 * D_FF), d),
        'ffn_conv_w': w(ks[14], (DEPTH_2, CONV_WIDTH_2, 2 * D_FF), CONV_WIDTH_2),
        'ffn_conv_b': 0.02 * jax.random.normal(ks[15], (DEPTH_2, 2 * D_FF), f32),
        'ffn_w_out': w(ks[16], (DEPTH_2, D_FF, d), D_FF),
        'final_norm': gain(ks[17], (d,)),
    }

def second_block(x, norm_attn, norm_ffn, a_w_in, a_cmp_pos, a_cmp_w1, a_cmp_w2, a_w_out, kv_norm, b_w_kv, b_w_q, b_sinks, b_w_out, ffn_w_in, ffn_conv_w, ffn_conv_b, ffn_w_out, final_norm):
    h = x
    k_sh = None
    v_sh = None
    for layer in range(DEPTH_2):
        hn = rms_norm_2(h, norm_attn[layer])
        if layer < N_A_LAYERS:
            h = h + nsa_mixer(hn, a_w_in[layer], a_cmp_pos[layer], a_cmp_w1[layer], a_cmp_w2[layer], a_w_out[layer])
        else:
            if layer == N_A_LAYERS:
                k_sh, v_sh = shared_kv(h, kv_norm, b_w_kv)
                hn = rms_norm_2(h, norm_attn[layer])
            j = layer - N_A_LAYERS
            h = h + swa_sink_mixer(hn, k_sh, v_sh, b_w_q[j], b_sinks[j], b_w_out[j])
        h = h + conv_ffn(rms_norm_2(h, norm_ffn[layer]), ffn_w_in[layer], ffn_conv_w[layer], ffn_conv_b[layer], ffn_w_out[layer])
    return rms_norm_2(h, final_norm)


def setup_inputs(seed=0):
    out = dict(first_inputs(seed))
    for name, value in second_inputs(seed + 1).items():
        if name != "x":
            out[name + "_2"] = value
    return out


def reference(
    x, meta, norm1_g, w_in, b_forget, pool_w, pool_b, pool_scale, conv_w, conv_b, conv_ln_g,
    conv_ln_b, w_out_a, w_out_b, w_out_c, w_o, norm2_g, router_g, router_g_b, router_e,
    router_e_b, exp_w1, exp_w3, exp_w2, final_g, norm_attn_2, norm_ffn_2, a_w_in_2, a_cmp_pos_2,
    a_cmp_w1_2, a_cmp_w2_2, a_w_out_2, kv_norm_2, b_w_kv_2, b_w_q_2, b_sinks_2, b_w_out_2,
    ffn_w_in_2, ffn_conv_w_2, ffn_conv_b_2, ffn_w_out_2, final_norm_2,
):
    x = first_block(
        x, meta, norm1_g, w_in, b_forget, pool_w, pool_b, pool_scale, conv_w, conv_b, conv_ln_g,
        conv_ln_b, w_out_a, w_out_b, w_out_c, w_o, norm2_g, router_g, router_g_b, router_e,
        router_e_b, exp_w1, exp_w3, exp_w2, final_g,
    )
    return second_block(
        x, norm_attn_2, norm_ffn_2, a_w_in_2, a_cmp_pos_2, a_cmp_w1_2, a_cmp_w2_2, a_w_out_2,
        kv_norm_2, b_w_kv_2, b_w_q_2, b_sinks_2, b_w_out_2, ffn_w_in_2, ffn_conv_w_2,
        ffn_conv_b_2, ffn_w_out_2, final_norm_2,
    )


_drawn_inputs = setup_inputs


def setup_inputs(seed=0):
    import zlib

    import numpy as np

    out = dict(_drawn_inputs(seed))
    spreads = {}
    factors = {'pool_b': 4.098,
     'conv_b': 4.715,
     'conv_ln_g': 3.561,
     'conv_ln_b': 4.772,
     'router_g_b': 3.297,
     'router_e_b': 8.0,
     'norm_attn_2': 7.506,
     'norm_ffn_2': 2.764,
     'kv_norm_2': 8.0,
     'b_sinks_2': 20.997,
     'ffn_conv_b_2': 2.81,
     'final_norm_2': 8.075}
    for name, (base, spread) in spreads.items():
        noise = np.random.default_rng([zlib.crc32(name.encode()), seed]).standard_normal(out[name].shape)
        drawn = base * np.exp(spread * noise) if base else spread * noise
        out[name] = jnp.asarray(drawn.astype(out[name].dtype))
    for name, factor in factors.items():
        out[name] = (out[name] * factor).astype(out[name].dtype)
    return out
```

```python
from contextlib import ExitStack

import numpy as np
import concourse.bass as bass
from concourse import mybir

F32 = mybir.dt.float32
F32R = mybir.dt.float32r
ALU = mybir.AluOpType
ACT = mybir.ActivationFunctionType
AX = mybir.AxisListType.X

P = 128
D = 1024
C = D // P
SEQ, META = 512, 16
T1, T2 = SEQ + META, SEQ
HALF = T1 // 2
QT = SEQ // P
HD = 64
EPS = 1e-6
NEG = -1e30
KC = 8
UNIT = KC * P
POOL_W, CONV_W, FOX_H, KS = 256, 256, 8, 31
FOX_W = FOX_H * HD
N_GRP, PER_GRP = 4, 4
N_EXP, EXP_HID = 16, 256
NH, A_G, B_G = 16, 4, 2
CMP_B, CMP_S, CMP_HID = 32, 16, 256
NC = SEQ // CMP_S - CMP_B // CMP_S + 1
WIN_B = 128
DFF = 2816
FC = DFF // P
SCALE = HD ** -0.5

PARTS = [("pool", 2), ("bv", 2), ("bg", 2), ("q1", 4), ("k1", 4), ("fg", 1), ("v1", 4),
         ("merge", 32), ("wo1", 8), ("router", 1), ("moe", 96),
         ("kc", 2), ("vc", 2), ("gl", 1), ("vs", 2), ("vw", 2), ("cmp", 8), ("ks", 2), ("kw", 2), ("q2", 8), ("wo2", 8),
         ("ffn0_in", 2 * FC), ("ffn0_out", 24),
         ("k3", 1), ("v3", 1), ("q3", 8), ("wo3", 8), ("ffn1_in", 2 * FC), ("ffn1_out", 24)]
U = {}
N_UNITS = 0
for _name, _count in PARTS:
    U[_name] = N_UNITS
    N_UNITS += _count
RAW, SPLIT = 4, 2

VECS = [("norm1", 8), ("norm2", 8), ("final1", 8), ("attn0", 8), ("ffn0", 8), ("kv", 8), ("attn1", 8), ("ffn1", 8),
        ("final2", 8), ("pool_b", 2), ("pool_s", 2), ("conv_b", 2), ("ln_g", 2), ("ln_b", 2), ("conv_w", 2 * KS),
        ("bforget", 1), ("fw0", 2 * FC * 4), ("fw1", 2 * FC * 4), ("sink", NH), ("rbias", N_GRP + N_EXP),
        ("prio", 4), ("eps", 1), ("one", 1), ("cvalid", QT), ("cpos", 2 * CMP_B // 2)]
V0 = {}
N_VEC = 0
for _name, _count in VECS:
    V0[_name] = N_VEC
    N_VEC += _count

CONSTS = [("ident", P), ("ones", P), ("rot", P), ("causal", P), ("band", 2 * P), ("poolw", 2 * P),
          ("cosq", SEQ), ("sinq", SEQ), ("cosc", NC), ("sinc", NC), ("cmask", QT * NC), ("w2k", 4 * P), ("w2v", 2 * HD)]
C0 = {}
N_CONST = 0
for _name, _count in CONSTS:
    C0[_name] = N_CONST
    N_CONST += _count

STAGES = [("n1", 1), ("in1", 6 + 8 + 1 + 4), ("pool", 2), ("ln", 2), ("nf", FOX_H), ("ot1", 4), ("merge", 48), ("wo1", 8),
          ("n2", 1), ("router", 1), ("combT", 1), ("cb", N_EXP), ("moe", 96), ("nf1", 1), ("na0", 1),
          ("kcvc", 4), ("tok2", 5), ("cmp", 7), ("rope2", 24), ("ot2", 8), ("wo2", 8),
          ("nf0", 1), ("ffn0_in", 2 * FC), ("ffn0_out", 8), ("na1", 1), ("k3", 2), ("v3", 1), ("q3", 16), ("ot3", 8), ("wo3", 8),
          ("nf_1", 1), ("ffn1_in", 2 * FC), ("ffn1_out", 8), ("nfin", 1)]
R = {}
N_RES = 0
for _name, _count in STAGES:
    R[_name] = N_RES
    N_RES += _count
PAIRS = 4

STAGED = [("ot1", 4), ("merge", 48), ("wo1", 8), ("moe", 96), ("cmp", 2), ("rope2", 24), ("ot2", 8), ("wo2", 8), ("ffn0_in", 2 * FC),
          ("ffn0_out", 8), ("k3", 2), ("q3", 16), ("ot3", 8), ("wo3", 8), ("ffn1_in", 2 * FC), ("ffn1_out", 8)]
E0 = {}
N_EV = 0
for _name, _count in STAGED:
    E0[_name] = N_EV
    N_EV += _count
EV_SLOTS = 4

FOX_ITEMS = [(h, t) for h in range(FOX_H) for t in range(QT + 1)]
NSA_ITEMS = [(gp, r, g2, t, b) for gp in range(2) for r in range(4) for g2 in range(2) for t in range(QT) for b in range(3)]
SWA_ITEMS = [(r, g, t) for r in range(8) for g in range(B_G) for t in range(QT)]
A0 = {"fox": 0, "nsa": len(FOX_ITEMS), "swa": len(FOX_ITEMS) + len(NSA_ITEMS)}

ALONE = [("pool", 2), ("ln", 1), ("nf", FOX_H), ("ot1", 4), ("merge", 16), ("combT", 1), ("cb", N_EXP), ("cmp", 3), ("rope2", 12),
         ("ot2", 8), ("k3", 1), ("q3", 8), ("ot3", 8)]
L0 = {}
N_ALONE = 0
for _name, _count in ALONE:
    L0[_name] = N_ALONE
    N_ALONE += _count

X0 = {"n1": 0, "n2": C, "na0": 2 * C, "nf0": 3 * C, "kv": 4 * C, "na1": 5 * C, "nf_1": 6 * C}
HID0 = {"pool": 0, "conv": 2, "merge": 4, "moe": 12, "ffn0": 44, "ffn1": 44 + FC}
SQ0 = {"n1": 0, "ln": C, "n2": C + 2, "nf1": 2 * C + 2, "na0": 3 * C + 2, "nf0": 4 * C + 2, "na1": 5 * C + 2, "nf_1": 6 * C + 2,
       "nfin": 7 * C + 2}
ROPE0 = {"rope2": 1, "k3": 13, "q3": 14}
DONE0 = {"fg": 0, "ln": 1, "router": 3, "ffn0": 4, "ffn1": 4 + FC}


def build(nc, stream, x_in, vecs_in, consts_in, invcnt_in, out):
    with ExitStack() as ctx:
        def sb(name, shape, dt=F32):
            return ctx.enter_context(nc.sbuf_tensor(name, shape, dt))

        def sem(name):
            return ctx.enter_context(nc.semaphore(name))

        arena_at = (nc.sbuf_base + 31) // 32 * 32
        sb("arena", [P, 2 * FC * SEQ])
        HIDH = nc.alloc_sbuf_tensor_at("hid_hi", [P, FC * SEQ], F32R, offset=arena_at)
        HIDL = nc.alloc_sbuf_tensor_at("hid_lo", [P, FC * SEQ], F32R, offset=arena_at + FC * SEQ * 4)
        raw = sb("raw", [P, RAW, UNIT])
        w_hi = sb("w_hi", [P, SPLIT, UNIT], F32R)
        w_lo = sb("w_lo", [P, SPLIT, UNIT], F32R)
        XH = sb("x_hi", [P, C, T1], F32R)
        XL = sb("x_lo", [P, C, T1], F32R)
        H = sb("resid", [P, C, T1])
        EV = sb("staged", [P, EV_SLOTS, 2 + T1])
        TS = sb("scratch", [P, 3, T1])
        SQ = sb("squares", [P, 2, T1])
        vecs = sb("vecs", [P, N_VEC])
        consts = sb("consts", [P, N_CONST])
        gate48 = sb("gate48", [P, QT, 3 * NH])
        route = sb("route", [P, 12, QT + 1, 16])
        stat = sb("stat", [P, 16])
        o_bytes, end_bytes = C * T1 * 4, 2 * FC * SEQ * 4 - C * T1 * 4
        low = FC * SEQ - C * T1
        cursor = [o_bytes]

        def over(name, shape, dt=F32, at=None):
            size = 4
            for s in shape[1:]:
                size *= s
            start = cursor[0] if at is None else at
            if at is None:
                cursor[0] += -(-size // 32) * 32
            assert start + size <= end_bytes, (name, start + size, end_bytes)
            return nc.alloc_sbuf_tensor_at(name, shape, dt, offset=arena_at + start)

        Q1 = over("q1", [P, 4, T1])
        K1 = over("k1", [P, 4, T1])
        V1 = over("v1", [P, QT + 1, FOX_W])
        nf_at = cursor[0]
        NF = over("neg_cum_logf", [P, FOX_H, T1])
        OT1 = over("o_tok1", [P, QT + 1, FOX_W])
        cursor[0] = nf_at
        apad = over("a_pad", [P, 2, 16 + T1])
        sum2 = over("sum2", [P, 2, 16 + T1])
        sum4 = over("sum4", [P, 2, 16 + T1])
        sum8 = over("sum8", [P, 16 + T1])
        sig = over("sig", [P, 2, T1])
        glu = over("glu", [P, 2, KS - 1 + T1])
        inv = over("inv_count", [P, 2, T1])
        cursor[0] = o_bytes
        CB = over("comb_rows", [P, N_EXP, T1])
        cursor[0] = o_bytes
        q2_at = cursor[0]
        Q2 = over("q2", [P, 8, SEQ])
        ks_at = cursor[0]
        KSEL = over("k_sel", [P, 2, SEQ])
        KWIN = over("k_win", [P, 2, SEQ])
        VSEL = over("v_sel", [P, QT, 2 * P])
        VWIN = over("v_win", [P, QT, 2 * P])
        KCMP = over("k_cmp", [P, 2, 32])
        VCMP = over("v_cmp", [P, A_G, HD])
        HIDC = over("cmp_hidden", [P, 2, A_G * NC])
        ot_at = cursor[0]
        OT2 = over("o_tok2", [P, QT, D])
        cursor[0] = ot_at
        EO = over("kv_even_odd", [P, 4, 2, SEQ // 2])
        PAIR = over("kv_pairs", [P, 4, 2, SEQ // 2])
        BLK = over("cmp_blocks", [P, CMP_B // 2, A_G * NC], at=ks_at)
        BLKH = over("cmp_blocks_hi", [P, CMP_B // 2, A_G * NC], F32R, at=q2_at)
        BLKL = over("cmp_blocks_lo", [P, CMP_B // 2, A_G * NC], F32R, at=q2_at + CMP_B // 2 * A_G * NC * 4)
        cursor[0] = o_bytes
        Q3 = over("q3", [P, 8, SEQ])
        K3 = over("k3", [P, SEQ])
        V3 = over("v3", [P, QT, P])
        OT3 = over("o_tok3", [P, QT, D])

        PS = ctx.enter_context(nc.psum_tensor("psum", [P, 8, 512], F32))

        raw_loaded = [sem(f"raw_loaded{s}") for s in range(RAW)]
        consts_loaded = sem("consts_loaded")
        x_loaded = sem("x_loaded")
        inv_loaded = sem("inv_loaded")
        pairs_moved = sem("pairs_moved")
        stored = sem("stored")
        pads_zeroed = sem("pads_zeroed")
        hi_split = sem("hi_split")
        split_ready = sem("split_ready")
        unit_used = sem("unit_used")
        lin_done = sem("lin_done")
        lin_free = sem("lin_free")
        ev_used = sem("ev_used")
        x_ready = sem("x_ready")
        h_ready = sem("h_ready")
        hid_ready = sem("hid_ready")
        sq_ready = sem("sq_ready")
        sq_used = sem("sq_used")
        act_asked = sem("act_asked")
        act_done = sem("act_done")
        dve_step = sem("dve_step")
        act_step = sem("act_step")
        dve_ready = sem("dve_ready")
        rope_ready = sem("rope_ready")
        s_done = sem("s_done")
        max_ready = sem("max_ready")
        p_ready = sem("p_ready")
        t_done = sem("t_done")
        pt_ready = sem("pt_ready")
        o_done = sem("o_done")
        o_ready = sem("o_ready")

        def const(name, width=None, rows=P, start=0):
            a = C0[name] + start
            return consts[0:rows, a:a + (width if width else dict(CONSTS)[name])]

        def vec(name, i=0):
            return vecs[:, V0[name] + i:V0[name] + i + 1]

        ident = const("ident")

        def pair(r):
            return PS[:, 2 * (r % PAIRS):2 * (r % PAIRS) + 2, :]

        def halves(ap):
            return ap.rearrange("p (a n) -> p a n", a=2)

        def staged(e, width, shift=2):
            return EV[:, e % EV_SLOTS, shift:shift + width]

        def o_hi(c, t):
            return HIDH[:, c * T1:c * T1 + t]

        def o_lo(c, t):
            return HIDL[:, low + c * T1:low + c * T1 + t]

        def m_hi(c, t):
            return HIDH[:, (C + c) * T1:(C + c) * T1 + t]

        def m_lo(c, t):
            return HIDL[:, low - (C - c) * T1:low - (C - c) * T1 + t]

        def fox_item(n):
            h, t = FOX_ITEMS[n]
            lo = HD * (h % 2)
            rows = META if t == 0 else P
            q0 = 0 if t == 0 else META + P * (t - 1)
            keys = META + P * t
            tiles = [(0, META, V1[0:META, 0, h * HD:(h + 1) * HD])]
            tiles += [(META + P * (j - 1), P, V1[:, j, h * HD:(h + 1) * HD]) for j in range(1, t + 1)]
            return rows, Q1[lo:lo + HD, h // 2, q0:q0 + rows], K1[lo:lo + HD, h // 2, 0:keys], keys, tiles

        def nsa_item(n):
            gp, r, g2, t, b = NSA_ITEMS[n]
            lo, g = HD * g2, 2 * gp + g2
            q = Q2[lo:lo + HD, gp * 4 + r, t * P:(t + 1) * P]
            if b == 0:
                return P, q, KCMP[lo:lo + HD, gp, 0:NC], NC, [(0, NC, VCMP[0:NC, g, :])]
            k, v = (KSEL, VSEL) if b == 1 else (KWIN, VWIN)
            keys = P * (t + 1)
            return P, q, k[lo:lo + HD, gp, 0:keys], keys, [(P * j, P, v[:, j, g * HD:(g + 1) * HD]) for j in range(t + 1)]

        def swa_item(n):
            r, g, t = SWA_ITEMS[n]
            lo = HD * g
            first = max(t - 1, 0)
            keys = P * (t + 1 - first)
            return (P, Q3[lo:lo + HD, r, t * P:(t + 1) * P], K3[lo:lo + HD, first * P:(t + 1) * P], keys,
                    [(P * (j - first), P, V3[:, j, g * HD:(g + 1) * HD]) for j in range(first, t + 1)])

        def scores(a):
            return PS[:, 2 * (a % 2):2 * (a % 2) + 2, :].rearrange("p a n -> p (a n)")

        def turned(a):
            return PS[:, 4 + a % 2, :]

        def outs(a):
            return PS[:, 6 + a % 2, :]

        def probs(a):
            return SQ[:, a % 2, :]

        PTS = [TS[:, :, :].rearrange("p a n -> p (a n)")[:, s * 640:(s + 1) * 640] for s in range(2)]

        def tile_slots(tiles):
            at, got = 0, []
            for col, width, v in tiles:
                if width == META:
                    got.append((col, width, 512, True, v))
                else:
                    got.append((col, width, at, False, v))
                    at += P
            return got, at

        def token_tiles1():
            return [(0, 1, 0, META)] + [(META + P * i, 0, P * i, P) for i in range(QT)]

        block = ctx.enter_context(nc.Block())

        @block.sync
        def _(sp):
            sp.dma_start(H[:, :, :], x_in).then_inc(x_loaded, 16)
            sp.dma_start(vecs[:, :], vecs_in).then_inc(consts_loaded, 16)
            sp.dma_start(consts[:, :], consts_in).then_inc(consts_loaded, 16)
            sp.dma_start(inv[:, :, :], invcnt_in).then_inc(inv_loaded, 16)
            for s in range(RAW):
                sp.dma_start(raw[:, s, :], stream[s, :, :]).then_inc(raw_loaded[s], 16)
            with sp.Fori(1, N_UNITS // RAW) as i:
                for s in range(RAW):
                    sp.wait_ge(split_ready, i * RAW + (s + 1 - RAW))
                    sp.dma_start(raw[:, s, :], stream[i * RAW + s, :, :]).then_inc(raw_loaded[s], 16)
            for n in range(N_UNITS // RAW * RAW, N_UNITS):
                sp.wait_ge(split_ready, n + 1 - RAW)
                sp.dma_start(raw[:, n % RAW, :], stream[n, :, :]).then_inc(raw_loaded[n % RAW], 16)
            sp.wait_ge(h_ready, 2 * C)
            sp.dma_start(out, H[:, :, META:T1]).then_inc(stored, 16)
            sp.wait_ge(stored, 16)

        @block.gpsimd
        def _(pool):
            pool.memset(apad[:, :, 0:16], 0.0).then_inc(pads_zeroed, 1)
            pool.memset(sum2[:, :, 0:16], 0.0).then_inc(pads_zeroed, 1)
            pool.memset(sum4[:, :, 0:16], 0.0).then_inc(pads_zeroed, 1)
            pool.memset(sum8[:, 0:16], 0.0).then_inc(pads_zeroed, 1)
            pool.memset(glu[:, :, 0:KS - 1], 0.0).then_inc(pads_zeroed, 1)
            pool.memset(EV[:, :, 0:2], 0.0).then_inc(pads_zeroed, 1)
            pool.memset(route[:, :, :, :], 0.0).then_inc(pads_zeroed, 1)

            def split_unit(slot, n, loads, free):
                pool.wait_ge(raw_loaded[slot], 16 * loads)
                if free:
                    pool.wait_ge(unit_used, n - (SPLIT - 1))
                pool.tensor_tensor(w_hi[:, slot % SPLIT, :], raw[:, slot, :], vec("one").to_broadcast([P, UNIT]), ALU.mult).then_inc(hi_split, 1)
                pool.wait_ge(hi_split, n + 1)
                pool.tensor_tensor(w_lo[:, slot % SPLIT, :], raw[:, slot, :], w_hi[:, slot % SPLIT, :].bitcast(F32),
                                   ALU.subtract).then_inc(split_ready, 1)

            pool.wait_ge(consts_loaded, 32)
            for s in range(RAW):
                split_unit(s, s, 1, s >= SPLIT)
            with pool.Fori(1, N_UNITS // RAW) as i:
                for s in range(RAW):
                    split_unit(s, i * RAW + s, i + 1, True)
            for n in range(N_UNITS // RAW * RAW, N_UNITS):
                split_unit(n % RAW, n, n // RAW + 1, True)

        @block.tensor
        def _(pe):
            def take_pair(r):
                if not isinstance(r, int) or r >= PAIRS:
                    pe.wait_ge(lin_free, r - (PAIRS - 1))

            def three(outs_, slot, k, moving, start, stop):
                for p, (wt, part) in enumerate(((w_hi, 0), (w_hi, 1), (w_lo, 0))):
                    for o, m in zip(outs_, moving):
                        last = pe.matmul(o, wt[:, slot, k * P:(k + 1) * P], m[part], start=start and p == 0, stop=stop and p == 2,
                                         skip_group_check=True)
                return last

            def moving_of(hi, lo, t):
                if t == T1:
                    return [(hi[:, 0:HALF], lo[:, 0:HALF]), (hi[:, HALF:T1], lo[:, HALF:T1])]
                return [(hi, lo)]

            def out_of(rslot, t):
                return [PS[:, 2 * rslot, 0:HALF], PS[:, 2 * rslot + 1, 0:HALF]] if t == T1 else [PS[:, 2 * rslot, :]]

            def unit(n, slot, r, rslot, t, src, ready=None, chunks=range(KC), first=True, last=True, ends=True):
                pe.wait_ge(split_ready, n + 1)
                if first:
                    take_pair(r)
                chunks = list(chunks)
                for j, k in enumerate(chunks):
                    if ready is not None:
                        pe.wait_ge(ready[0], ready[1] + (j + 1))
                    hi, lo = src(j)
                    mm = three(out_of(rslot, t), slot, k, moving_of(hi, lo, t), first and j == 0, last and j == len(chunks) - 1)
                mm.then_inc(unit_used if ends else lin_done, 1)

            def x_of(t):
                return lambda k: (XH[:, k, T1 - t:T1], XL[:, k, T1 - t:T1])

            def token_unit(n, r, t, src):
                pe.wait_ge(split_ready, n + 1)
                take_pair(r)
                tiles = token_tiles1() if t == T1 else [(P * i, 0, P * i, P) for i in range(QT)]
                for first, bank, col, _ in tiles:
                    o = pair(r)[:, bank, col:col + P]
                    for k in range(KC):
                        hi, lo = src(k)
                        for p, (xs, ws) in enumerate(((hi, w_hi), (hi, w_lo), (lo, w_hi))):
                            mm = pe.matmul(o, xs[:, first:first + P], ws[:, n % SPLIT, k * P:(k + 1) * P],
                                           start=k == 0 and p == 0, stop=k == KC - 1 and p == 2, skip_group_check=True)
                mm.then_inc(unit_used, 1)

            def norm_sum(stage, r, t, chunks=C):
                take_pair(r)
                for c in range(chunks):
                    s = SQ0[stage] + c
                    pe.wait_ge(sq_ready, s + 1)
                    for o, a in ((0, 0), (1, HALF)) if t == T1 else ((0, 0),):
                        w = HALF if t == T1 else T2
                        mm = pe.matmul(pair(r)[:, o, 0:w], const("ones"), SQ[:, s % 2, a:a + w],
                                       start=c == 0, stop=c == chunks - 1, skip_group_check=True)
                    mm.then_inc(sq_used, 1)

            def rotate(e, r, width=T2):
                take_pair(r)
                pe.matmul(pair(r)[:, 0, 0:width], const("rot"), staged(e, width), start=True, stop=True).then_inc(lin_done, 1)

            def rope_chunks(n0, r0, e0, count, src):
                for c in range(count + 1):
                    if c < count:
                        r = r0 + 2 * c - (1 if c else 0)
                        unit(n0 + c, (n0 + c) % SPLIT, r, r % PAIRS, T2, src)
                    if c:
                        before = 2 * (c - 1) - (1 if c > 1 else 0)
                        pe.wait_ge(lin_free, r0 + before + 1)
                        rotate(e0 + before, r0 + 2 * c if c < count else r0 + 2 * count - 1)

            def attention(kind, items, item, results):
                a0, n_items = A0[kind], len(items)
                pe.wait_ge(lin_free, results)
                for n in range(n_items + 2):
                    if n < n_items:
                        a = a0 + n
                        rows, q, k, keys, tiles = item(n)
                        if a >= 2:
                            pe.wait_ge(p_ready, a - 1)
                        for c in range(0, keys, 512):
                            w = min(512, keys - c)
                            mm = pe.matmul(scores(a)[0:rows, c:c + w], q, k[:, c:c + w], start=True, stop=True)
                        mm.then_inc(s_done, 1)
                    if 1 <= n <= n_items:
                        a = a0 + n - 1
                        rows, q, k, keys, tiles = item(n - 1)
                        pe.wait_ge(p_ready, a + 1)
                        if a >= 2:
                            pe.wait_ge(pt_ready, a - 1)
                            pe.wait_ge(o_ready, a - 1)
                        got, _ = tile_slots(tiles)
                        for col, width, at, small, v in got:
                            dst = outs(a)[0:width, P:P + rows] if small else turned(a)[0:width, at:at + rows]
                            mm = pe.transpose(dst, probs(a)[0:rows, col:col + width], ident[0:rows, 0:rows])
                        mm.then_inc(t_done, 1)
                    if n >= 2:
                        a = a0 + n - 2
                        rows, q, k, keys, tiles = item(n - 2)
                        pe.wait_ge(pt_ready, a + 1)
                        got, _ = tile_slots(tiles)
                        for j, (col, width, at, small, v) in enumerate(got):
                            mm = pe.matmul(outs(a)[0:rows, 0:HD], PTS[a % 2][0:width, at:at + rows], v,
                                           start=j == 0, stop=j == len(got) - 1)
                        mm.then_inc(o_done, 1)
                pe.wait_ge(o_ready, a0 + n_items)

            def turn_outputs(r0, count, ot, t):
                for c in range(count):
                    take_pair(r0 + c)
                    if t == T1:
                        pe.transpose(pair(r0 + c)[:, 1, 0:META], ot[0:META, 0, c * P:(c + 1) * P], ident[0:META, 0:META])
                    for i in range(QT):
                        mm = pe.transpose(pair(r0 + c)[:, 0, i * P:(i + 1) * P], ot[:, i + (t == T1), c * P:(c + 1) * P], ident)
                    mm.then_inc(lin_done, 1)

            def residual_loop(n0, r0, t, src):
                with pe.Fori(0, 2) as i:
                    for j in range(4):
                        unit(n0 + i * 4 + j, (n0 + j) % SPLIT, r0 + i * 4 + j, (r0 + j) % PAIRS, t, src)

            def hidden_of(part):
                return lambda k: (HIDH[:, (part * KC + k) * SEQ:(part * KC + k + 1) * SEQ],
                                  HIDL[:, (part * KC + k) * SEQ:(part * KC + k + 1) * SEQ])

            def ffn(layer, norm):
                n0, r0 = U[f"ffn{layer}_in"], R[f"ffn{layer}_in"]
                pe.wait_ge(x_ready, X0[norm] + C)
                with pe.Fori(0, FC // 2) as i:
                    for j in range(4):
                        unit(n0 + i * 4 + j, (n0 + j) % SPLIT, r0 + i * 4 + j, (r0 + j) % PAIRS, T2, x_of(T2))
                n0, r0 = U[f"ffn{layer}_out"], R[f"ffn{layer}_out"]
                pe.wait_ge(hid_ready, HID0[f"ffn{layer}"] + FC)
                with pe.Fori(0, 2) as i:
                    for j in range(4):
                        for part in range(3):
                            m = 3 * j + part
                            unit(n0 + i * 12 + m, (n0 + m) % SPLIT, r0 + i * 4 + j, (r0 + j) % PAIRS, T2, hidden_of(part),
                                 chunks=range(min(KC, FC - part * KC)), first=part == 0, last=part == 2)

            pe.wait_ge(consts_loaded, 32)
            norm_sum("n1", R["n1"], T1)
            r = R["in1"]
            for n in range(U["pool"], U["v1"]):
                unit(n, n % SPLIT, r, r % PAIRS, T1, x_of(T1), ready=(x_ready, X0["n1"]) if n == U["pool"] else None)
                r += 1
            for n in range(U["v1"], U["v1"] + 4):
                token_unit(n, r, T1, x_of(T1))
                r += 1
            for c in range(2):
                r = R["pool"] + c
                take_pair(r)
                pe.wait_ge(dve_ready, c + 1)
                for o in range(2):
                    mm = pe.matmul(pair(r)[:, o, 0:HALF], const("poolw", P, start=c * P), TS[:, c, o * HALF:(o + 1) * HALF],
                                   start=True, stop=True)
                mm.then_inc(lin_done, 1)
            take_pair(R["ln"])
            for c in range(2):
                pe.wait_ge(dve_ready, 3 + c)
                for o in range(2):
                    mm = pe.matmul(pair(R["ln"])[:, o, 0:HALF], const("ones"), sig[:, c, o * HALF:(o + 1) * HALF],
                                   start=c == 0, stop=c == 1, skip_group_check=True)
            mm.then_inc(lin_done, 1)
            norm_sum("ln", R["ln"] + 1, T1, chunks=2)
            pe.wait_ge(dve_ready, 5)
            for h in range(FOX_H):
                r = R["nf"] + h
                take_pair(r)
                for o in range(2):
                    mm = pe.matmul(pair(r)[:, o, 0:HALF], ident[0:FOX_H, h:h + 1].to_broadcast([FOX_H, P]),
                                   staged(2, T1)[0:FOX_H, o * HALF:(o + 1) * HALF], start=True, stop=True)
                mm.then_inc(lin_done, 1)
            attention("fox", FOX_ITEMS, fox_item, R["ot1"])
            turn_outputs(R["ot1"], 4, OT1, T1)
            pe.wait_ge(hid_ready, HID0["merge"])
            pe.wait_ge(ev_used, E0["merge"])
            with pe.Fori(0, 4) as i:
                for m in range(2):
                    n, r = U["merge"] + 4 * m, R["merge"] + 6 * m
                    for g in range(3):
                        unit(n + i * 8 + g, (n + g) % SPLIT, r + i * 12 + g, (r + g) % PAIRS, T1, x_of(T1))
                    for b, (k0, k1) in enumerate(((0, 2), (2, 4), (4, 8))):
                        unit(n + i * 8 + 3, (n + 3) % SPLIT, r + i * 12 + 3 + b, (r + 3 + b) % PAIRS, T1,
                             lambda k: (o_hi(k0 + k, T1), o_lo(k0 + k, T1)), chunks=range(k0, k1), ends=b == 2)
            pe.wait_ge(hid_ready, HID0["merge"] + C)
            residual_loop(U["wo1"], R["wo1"], T1, lambda k: (m_hi(k, T1), m_lo(k, T1)))
            norm_sum("n2", R["n2"], T1)
            pe.wait_ge(x_ready, X0["n2"] + C)
            token_unit(U["router"], R["router"], T1, x_of(T1))
            take_pair(R["combT"])
            pe.wait_ge(dve_ready, 6)
            for i, (first, bank, col, rows) in enumerate(token_tiles1()):
                mm = pe.transpose(pair(R["combT"])[0:N_EXP, bank, col:col + rows], route[0:rows, 11, i, :], ident[0:rows, 0:rows])
            mm.then_inc(lin_done, 1)
            pe.wait_ge(lin_free, R["combT"] + 1)
            for e in range(N_EXP):
                r = R["cb"] + e
                take_pair(r)
                for o in range(2):
                    mm = pe.matmul(pair(r)[:, o, 0:HALF], ident[0:N_EXP, e:e + 1].to_broadcast([N_EXP, P]),
                                   SQ[0:N_EXP, 0, o * HALF:(o + 1) * HALF], start=True, stop=True)
                mm.then_inc(lin_done, 1)
            with pe.Fori(0, N_GRP) as i:
                n, r = U["moe"], R["moe"]
                for j in range(16):
                    unit(n + i * 24 + j, (n + j) % SPLIT, r + i * 24 + j, (r + j) % PAIRS, T1, x_of(T1))
                for j in range(16, 24):
                    unit(n + i * 24 + j, (n + j) % SPLIT, r + i * 24 + j, (r + j) % PAIRS, T1,
                         lambda k: (o_hi(k, T1), o_lo(k, T1)), ready=(hid_ready, i * C + HID0["moe"]) if j == 16 else None)
            norm_sum("nf1", R["nf1"], T1)
            norm_sum("na0", R["na0"], T2)
            r = R["kcvc"]
            for n in range(U["kc"], U["gl"]):
                unit(n, n % SPLIT, r, r % PAIRS, T2, x_of(T2), ready=(x_ready, X0["na0"]) if n == U["kc"] else None)
                r += 1
            for n in range(U["gl"], U["cmp"]):
                token_unit(n, r, T2, x_of(T2))
                r += 1
            for kv in range(2):
                pe.wait_ge(dve_ready, 7 + kv)
                r = R["cmp"] + 3 * kv
                for m in range(2):
                    take_pair(r + m)
                    for part in range(2):
                        n = U["cmp"] + 4 * kv + 2 * m + part
                        pe.wait_ge(split_ready, n + 1)
                        for k in range(KC):
                            b = part * KC + k
                            mm = three([pair(r + m)[:, 0, 0:A_G * NC]], n % SPLIT, k, [(BLKH[:, b, :], BLKL[:, b, :])],
                                       part == 0 and k == 0, part == 1 and k == KC - 1)
                        mm.then_inc(unit_used, 1)
                take_pair(r + 2)
                pe.wait_ge(lin_free, r + 2)
                if kv == 0:
                    for gp in range(2):
                        for odd in range(2):
                            g = 2 * gp + odd
                            for j in range(2):
                                mm = pe.matmul(pair(r + 2)[:, 0, gp * NC:(gp + 1) * NC], const("w2k", P, start=(2 * j + odd) * P),
                                               HIDC[:, j, g * NC:(g + 1) * NC], start=odd == 0 and j == 0, stop=odd == 1 and j == 1)
                else:
                    for g in range(A_G):
                        for j in range(2):
                            mm = pe.matmul(pair(r + 2)[0:NC, 0, g * HD:(g + 1) * HD], HIDC[:, j, g * NC:(g + 1) * NC],
                                           const("w2v", HD, start=j * HD), start=j == 0, stop=j == 1)
                mm.then_inc(lin_done, 1)
            rotate(E0["cmp"], R["cmp"] + 6, 2 * NC)
            rope_chunks(U["ks"], R["rope2"], E0["rope2"], 12, x_of(T2))
            pe.wait_ge(rope_ready, ROPE0["k3"])
            attention("nsa", NSA_ITEMS, nsa_item, R["ot2"])
            turn_outputs(R["ot2"], C, OT2, T2)
            pe.wait_ge(ev_used, E0["wo2"])
            residual_loop(U["wo2"], R["wo2"], T2, lambda k: (o_hi(k, T2), o_lo(k, T2)))
            norm_sum("nf0", R["nf0"], T2)
            ffn(0, "nf0")
            norm_sum("na1", R["na1"], T2)
            kv_of = lambda k: (o_hi(k, T2), o_lo(k, T2))
            pe.wait_ge(x_ready, X0["kv"] + C)
            rope_chunks(U["k3"], R["k3"], E0["k3"], 1, kv_of)
            token_unit(U["v3"], R["v3"], T2, kv_of)
            pe.wait_ge(x_ready, X0["na1"] + C)
            rope_chunks(U["q3"], R["q3"], E0["q3"], 8, x_of(T2))
            pe.wait_ge(rope_ready, ROPE0["k3"] + 9)
            attention("swa", SWA_ITEMS, swa_item, R["ot3"])
            turn_outputs(R["ot3"], C, OT3, T2)
            pe.wait_ge(ev_used, E0["wo3"])
            residual_loop(U["wo3"], R["wo3"], T2, lambda k: (o_hi(k, T2), o_lo(k, T2)))
            norm_sum("nf_1", R["nf_1"], T2)
            ffn(1, "nf_1")
            norm_sum("nfin", R["nfin"], T2)

        @block.scalar
        def _(act):
            def by_unit(n):
                act.wait_ge(unit_used, n + 1)

            def alone(l):
                act.wait_ge(lin_done, l + 1)

            def result(rslot, t):
                return PS[:, 2 * rslot:2 * rslot + 2, 0:HALF] if t == T1 else PS[:, 2 * rslot, :]

            def shaped(ap, t):
                return halves(ap) if t == T1 else ap

            def evacuate(rslot, dst, t, func=ACT.Copy, **more):
                act.activation(shaped(dst, t), result(rslot, t), func, **more).then_inc(lin_free, 1)

            def stage(rslot, e, eslot, t, func=ACT.Copy, back=EV_SLOTS - 1, **more):
                if not isinstance(e, int) or e - back > 0:
                    act.wait_ge(ev_used, e - back)
                evacuate(rslot, EV[:, eslot, 2:2 + t], t, func, **more)

            def squares(stage_, src, ready, count=C):
                for c in range(count):
                    s = SQ0[stage_] + c
                    if ready is not None:
                        act.wait_ge(ready[0], ready[1] + c + 1)
                    if s >= 2:
                        act.wait_ge(sq_used, s - 1)
                    ap = src(c)
                    act.activation(SQ[:, s % 2, 0:ap.shape[1]], ap, ACT.Square).then_inc(sq_ready, 1)

            def root(stage_, r, t, width):
                act.wait_ge(sq_used, SQ0[stage_] + width // P)
                act.activation(shaped(TS[:, 2, 0:t], t), result(r % PAIRS, t), ACT.Sqrt, bias=vec("eps"), scale=1.0 / width)\
                   .then_inc(lin_free, 1)

            def h_of(t):
                return lambda c: H[:, c, T1 - t:T1]

            def attention(kind, items, item, extra=0):
                a0, n_items = A0[kind], len(items)
                for n in range(n_items + 1):
                    if n < n_items:
                        a = a0 + n
                        rows, _, _, keys, _ = item(n)
                        act.wait_ge(max_ready, a + 1)
                        if a >= 2:
                            act.wait_ge(t_done, a - 1)
                        act.activation(probs(a)[0:rows, 0:keys + extra], scores(a)[0:rows, 0:keys + extra], ACT.Exp,
                                       bias=stat[0:rows, a % 4:a % 4 + 1],
                                       accum_out=stat[0:rows, 4 + a % 4:5 + a % 4]).then_inc(p_ready, 1)
                    if n:
                        a = a0 + n - 1
                        rows, _, _, _, tiles = item(n - 1)
                        act.wait_ge(t_done, a + 1)
                        if a >= 2:
                            act.wait_ge(o_done, a - 1)
                        got, wide = tile_slots(tiles)
                        height = max([g[1] for g in got if not g[3]], default=0)
                        if got[0][3]:
                            cp = act.activation(PTS[a % 2][0:META, 512:512 + rows], outs(a)[0:META, P:P + rows], ACT.Copy)
                        if wide:
                            cp = act.activation(PTS[a % 2][0:height, 0:wide], turned(a)[0:height, 0:wide], ACT.Copy)
                        cp.then_inc(pt_ready, 1)

            def turned_outputs(stage_, count, t):
                for c in range(count):
                    r, e = R[stage_] + c, E0[stage_] + c
                    alone(L0[stage_] + c)
                    if e >= EV_SLOTS:
                        act.wait_ge(ev_used, e - (EV_SLOTS - 1))
                    if t == T1:
                        act.activation(staged(e, META), pair(r)[:, 1, 0:META], ACT.Copy)
                    act.activation(staged(e, T2, 2 + t - T2), pair(r)[:, 0, :], ACT.Copy).then_inc(lin_free, 1)

            def residual_loop(name, t, units=1):
                n0, r0, e0 = U[name], R[name], E0[name]
                with act.Fori(0, 2) as i:
                    for j in range(4):
                        by_unit(n0 + i * (4 * units) + units * j + units - 1)
                        stage((r0 + j) % PAIRS, e0 + i * 4 + j, (e0 + j) % EV_SLOTS, t)

            def ffn(layer):
                n0, r0, e0 = U[f"ffn{layer}_in"], R[f"ffn{layer}_in"], E0[f"ffn{layer}_in"]
                with act.Fori(0, FC // 2) as i:
                    for j in range(2):
                        for m in (2 * j, 2 * j + 1):
                            by_unit(n0 + i * 4 + m)
                            stage((r0 + m) % PAIRS, e0 + i * 4 + m, (e0 + m) % EV_SLOTS, T2)
                        act.wait_ge(ev_used, e0 + i * 4 + 2 * j + 1)
                        act.activation(SQ[:, j, 0:T2], SQ[:, j, 0:T2], ACT.Silu).then_inc(act_done, 1)
                residual_loop(f"ffn{layer}_out", T2, 3)

            def rope_results(name, n0, count, scale_from):
                r0, e0 = R[name], E0[name]
                order = [(0, False)]
                for c in range(1, count):
                    order += [(c, False), (c - 1, True)]
                order.append((count - 1, True))
                for n, (c, turned_) in enumerate(order):
                    if turned_:
                        alone(L0[name] + c)
                        stage((r0 + n) % PAIRS, e0 + n, (e0 + n) % EV_SLOTS, T2, back=3 if c < count - 1 else 2)
                    else:
                        by_unit(n0 + c)
                        stage((r0 + n) % PAIRS, e0 + n, (e0 + n) % EV_SLOTS, T2, back=1 if n else 0,
                              scale=SCALE if c >= scale_from else 1.0)

            act.wait_ge(consts_loaded, 32)
            act.wait_ge(x_loaded, 16)
            act.wait_ge(pads_zeroed, 7)
            squares("n1", h_of(T1), None)
            root("n1", R["n1"], T1, D)
            r, n = R["in1"], U["pool"]
            for c in range(14):
                by_unit(n + c)
                if c < 2:
                    evacuate((r + c) % PAIRS, apad[:, c, 16:16 + T1], T1)
                elif c < 4:
                    evacuate((r + c) % PAIRS, glu[:, c - 2, KS - 1:KS - 1 + T1], T1)
                elif c < 6:
                    evacuate((r + c) % PAIRS, sig[:, c - 4, :], T1, ACT.Sigmoid)
                elif c < 10:
                    evacuate((r + c) % PAIRS, Q1[:, c - 6, :], T1, scale=SCALE)
                else:
                    evacuate((r + c) % PAIRS, K1[:, c - 10, :], T1)
            by_unit(n + 14)
            act.activation(halves(staged(0, T1)[0:FOX_H, :]), pair(r + 14)[0:FOX_H, :, 0:HALF], ACT.Identity,
                           bias=vec("bforget")[0:FOX_H, :]).then_inc(lin_free, 1)
            for c in range(4):
                rr = r + 15 + c
                by_unit(n + 15 + c)
                act.activation(V1[0:META, 0, c * P:(c + 1) * P], pair(rr)[0:META, 1, 0:P], ACT.Copy)
                act.activation(V1[:, 1:QT + 1, c * P:(c + 1) * P], pair(rr)[:, 0, :].rearrange("p (i n) -> p i n", i=QT), ACT.Copy)\
                   .then_inc(lin_free, 1)
            act.wait_ge(lin_free, r + 15)
            act.activation(staged(1, T1)[0:FOX_H, :], staged(0, T1)[0:FOX_H, :], ACT.Abs).then_inc(act_step, 1)
            act.wait_ge(act_step, 1)
            act.activation(staged(3, T1)[0:FOX_H, :], staged(1, T1)[0:FOX_H, :], ACT.Exp, scale=-1.0).then_inc(act_step, 1)
            act.wait_ge(act_step, 2)
            act.activation(staged(1, T1)[0:FOX_H, :], staged(3, T1)[0:FOX_H, :], ACT.Ln, bias=vec("one")[0:FOX_H, :])\
               .then_inc(act_done, 1)
            for c in range(2):
                alone(L0["pool"] + c)
                evacuate((R["pool"] + c) % PAIRS, apad[:, c, 16:16 + T1], T1, ACT.Identity, bias=vec("pool_b", c))
            alone(L0["ln"])
            evacuate(R["ln"] % PAIRS, TS[:, 2, :], T1, scale=-1.0 / CONV_W)
            squares("ln", lambda c: sig[:, c, :], (act_asked, 0), 2)
            root("ln", R["ln"] + 1, T1, CONV_W)
            for c in range(2):
                act.wait_ge(act_asked, 3 + c)
                act.activation(sig[:, c, :], sig[:, c, :], ACT.Silu, bias=vec("ln_b", c)).then_inc(act_done, 1)
            act.wait_ge(hid_ready, HID0["merge"])
            for h in range(FOX_H):
                alone(L0["nf"] + h)
                evacuate((R["nf"] + h) % PAIRS, NF[:, h, :], T1)
            attention("fox", FOX_ITEMS, fox_item)
            turned_outputs("ot1", 4, T1)
            with act.Fori(0, 4) as i:
                n, r, e = U["merge"], R["merge"], E0["merge"]
                for j in range(12):
                    m, k = j // 6, j % 6
                    if k in (3, 4):
                        alone(L0["merge"] + i * 4 + 2 * m + k - 3)
                    else:
                        by_unit(n + i * 8 + 4 * m + min(k, 3))
                    stage((r + j) % PAIRS, e + i * 12 + j, (e + j) % EV_SLOTS, T1, ACT.Sigmoid if k < 3 else ACT.Copy)
            residual_loop("wo1", T1)
            squares("n2", h_of(T1), (ev_used, E0["wo1"]))
            root("n2", R["n2"], T1, D)
            r = R["router"]
            by_unit(U["router"])
            for slot, a, w in ((0, 0, N_GRP), (1, N_GRP, N_EXP)):
                act.activation(route[0:META, slot, 0, 0:w], pair(r)[0:META, 1, a:a + w], ACT.Copy)
                cp = act.activation(route[:, slot, 1:QT + 1, 0:w],
                                    pair(r)[:, 0, :].rearrange("p (i n) -> p i n", i=QT)[:, :, a:a + w], ACT.Copy)
            cp.then_inc(lin_free, 1)
            act.wait_ge(act_asked, 5)
            act.activation(route[:, 4, :, 0:8], route[:, 3, :, 0:8], ACT.Exp).then_inc(act_done, 1)
            r = R["combT"]
            alone(L0["combT"])
            act.activation(SQ[0:N_EXP, 0, 0:META], pair(r)[0:N_EXP, 1, 0:META], ACT.Copy)
            act.activation(SQ[0:N_EXP, 0, META:T1], pair(r)[0:N_EXP, 0, :], ACT.Copy).then_inc(lin_free, 1)
            for e in range(N_EXP):
                alone(L0["cb"] + e)
                evacuate((R["cb"] + e) % PAIRS, CB[:, e, :], T1)
            with act.Fori(0, N_GRP) as i:
                n, r, e = U["moe"], R["moe"], E0["moe"]
                for j in range(24):
                    by_unit(n + i * 24 + j)
                    stage((r + j) % PAIRS, e + i * 24 + j, (e + j) % EV_SLOTS, T1, ACT.Silu if j < 16 and j % 2 == 0 else ACT.Copy)
            squares("nf1", h_of(T1), (ev_used, E0["moe"] + 3 * 24 + 16))
            root("nf1", R["nf1"], T1, D)
            squares("na0", h_of(T2), (h_ready, 0))
            root("na0", R["na0"], T2, D)
            for c in range(4):
                r = R["kcvc"] + c
                by_unit(U["kc"] + c)
                act.activation(EO[:, c, :, :], pair(r)[:, 0, :].rearrange("p (n a) -> p a n", a=2), ACT.Copy).then_inc(lin_free, 1)
            act.wait_ge(lin_free, R["kcvc"] + 4)
            for par in range(2):
                for g2 in range(2):
                    act.dma_start(PAIR[par * HD:(par + 1) * HD, :, g2, :], EO[g2 * HD:(g2 + 1) * HD, :, par, :])\
                       .then_inc(pairs_moved, 16)
            r = R["tok2"]
            by_unit(U["gl"])
            act.activation(gate48[:, :, :], pair(r)[:, 0, :].rearrange("p (i n) -> p i n", i=QT)[:, :, 0:3 * NH], ACT.Sigmoid)\
               .then_inc(lin_free, 1)
            for c, v in enumerate((VSEL, VSEL, VWIN, VWIN)):
                by_unit(U["vs"] + c)
                act.activation(v[:, :, (c % 2) * P:(c % 2 + 1) * P], pair(r + 1 + c)[:, 0, :].rearrange("p (i n) -> p i n", i=QT),
                               ACT.Copy).then_inc(lin_free, 1)
            for kv in range(2):
                r = R["cmp"] + 3 * kv
                for m in range(2):
                    by_unit(U["cmp"] + 4 * kv + 2 * m + 1)
                    act.activation(HIDC[:, m, :], pair(r + m)[:, 0, 0:A_G * NC], ACT.Gelu_apprx_tanh).then_inc(lin_free, 1)
                alone(L0["cmp"] + kv)
                if kv == 0:
                    act.wait_ge(ev_used, E0["cmp"])
                    act.activation(staged(E0["cmp"], 2 * NC), pair(r + 2)[:, 0, 0:2 * NC], ACT.Copy).then_inc(lin_free, 1)
                else:
                    act.activation(VCMP[0:NC, :, :], pair(r + 2)[0:NC, 0, 0:A_G * HD].rearrange("p (g d) -> p g d", g=A_G), ACT.Copy)\
                       .then_inc(lin_free, 1)
            alone(L0["cmp"] + 2)
            act.activation(staged(E0["cmp"] + 1, 2 * NC), pair(R["cmp"] + 6)[:, 0, 0:2 * NC], ACT.Copy).then_inc(lin_free, 1)
            rope_results("rope2", U["ks"], 12, 4)
            attention("nsa", NSA_ITEMS, nsa_item)
            turned_outputs("ot2", C, T2)
            residual_loop("wo2", T2)
            squares("nf0", h_of(T2), (ev_used, E0["wo2"]))
            root("nf0", R["nf0"], T2, D)
            ffn(0)
            squares("na1", h_of(T2), (ev_used, E0["ffn0_out"]))
            root("na1", R["na1"], T2, D)
            rope_results("k3", U["k3"], 1, 1)
            by_unit(U["v3"])
            act.activation(V3[:, :, :], pair(R["v3"])[:, 0, :].rearrange("p (i n) -> p i n", i=QT), ACT.Copy).then_inc(lin_free, 1)
            rope_results("q3", U["q3"], 8, 0)
            attention("swa", SWA_ITEMS, swa_item, 1)
            turned_outputs("ot3", C, T2)
            residual_loop("wo3", T2)
            squares("nf_1", h_of(T2), (ev_used, E0["wo3"]))
            root("nf_1", R["nf_1"], T2, D)
            ffn(1)
            squares("nfin", h_of(T2), (ev_used, E0["ffn1_out"]))
            root("nfin", R["nfin"], T2, D)

        @block.vector
        def _(dve):
            steps = [0]

            def then(ins):
                steps[0] = steps[0] + 1
                ins.then_inc(dve_step, 1)
                dve.wait_ge(dve_step, steps[0])

            def parts(src, hi, lo):
                then(dve.tensor_copy(hi, src))
                return dve.tensor_tensor(lo, src, hi.bitcast(F32), ALU.subtract)

            def reciprocal_root(r, t):
                dve.wait_ge(lin_free, r + 1)
                then(dve.reciprocal(TS[:, 2, 0:t], TS[:, 2, 0:t]))

            def normed(gain, t, hi, lo, used):
                dve.wait_ge(unit_used, used)
                for c in range(C):
                    y = TS[:, c % 2, 0:t]
                    then(dve.scalar_tensor_tensor(out=y, in0=H[:, c, T1 - t:T1], scalar=vec(gain, c), in1=TS[:, 2, 0:t],
                                                  op0=ALU.mult, op1=ALU.mult))
                    parts(y, hi(c), lo(c)).then_inc(x_ready, 1)

            def normed_in_place(gain, root_):
                for c in range(C):
                    dve.scalar_tensor_tensor(out=H[:, c, META:T1], in0=H[:, c, META:T1], scalar=vec(gain, c), in1=root_,
                                             op0=ALU.mult, op1=ALU.mult).then_inc(h_ready, 1)

            def x_hi(t):
                return lambda c: XH[:, c, T1 - t:T1]

            def x_lo(t):
                return lambda c: XL[:, c, T1 - t:T1]

            def residual_loop(name, t):
                r0, e0 = R[name], E0[name]
                with dve.Fori(0, 2) as i:
                    for j in range(4):
                        dve.wait_ge(lin_free, r0 + i * 4 + j + 1)
                        h = H[:, i * 4 + j, T1 - t:T1]
                        dve.tensor_tensor(h, h, EV[:, (e0 + j) % EV_SLOTS, 2:2 + t], ALU.add).then_inc(ev_used, 1)

            def attention(kind, items, item, masked, kept, extra=0):
                a0, n_items = A0[kind], len(items)
                for n in range(n_items + 2):
                    if n < n_items:
                        a = a0 + n
                        rows, _, _, keys, _ = item(n)
                        dve.wait_ge(s_done, a + 1)
                        masked(n, scores(a), rows, keys)
                        dve.tensor_reduce(stat[0:rows, a % 4:a % 4 + 1], scores(a)[0:rows, 0:keys + extra], AX, ALU.max, negate=True)\
                           .then_inc(max_ready, 1)
                    if n >= 2:
                        a = a0 + n - 2
                        rows = item(n - 2)[0]
                        dve.wait_ge(o_done, a + 1)
                        rs = stat[0:rows, 8 + a % 4:9 + a % 4]
                        then(dve.reciprocal(rs, stat[0:rows, 4 + a % 4:5 + a % 4]))
                        kept(n - 2, a, outs(a)[0:rows, 0:HD], rs, rows).then_inc(o_ready, 1)

            def add_mask(s, mask):
                then(dve.tensor_tensor(s, s, mask, ALU.add))

            def feature_parts(stage_, count, t, first):
                for c in range(count):
                    dve.wait_ge(lin_free, R[stage_] + c + 1)
                    parts(staged(E0[stage_] + c, t), o_hi(first + c, t), o_lo(first + c, t)).then_inc(ev_used, 1)

            def rotated(stage_, count, dest):
                r0, e0 = R[stage_], E0[stage_]
                for c in range(count):
                    at = 2 * c - (1 if c else 0)
                    rot = 2 * c + 2 if c < count - 1 else 2 * count - 1
                    dve.wait_ge(lin_free, r0 + rot + 1)
                    if ROPE0[stage_] + c:
                        dve.wait_ge(rope_ready, ROPE0[stage_] + c)
                    dve.tensor_tensor(TS[:, 0, 0:T2], staged(e0 + at, T2), const("cosq"), ALU.mult).then_inc(ev_used, 1)
                    dve.tensor_tensor(TS[:, 1, 0:T2], staged(e0 + rot, T2), const("sinq"), ALU.mult).then_inc(ev_used, 1)
                    dve.wait_ge(ev_used, e0 + 2 * c + 2)
                    dve.tensor_tensor(dest(c), TS[:, 0, 0:T2], TS[:, 1, 0:T2], ALU.add).then_inc(rope_ready, 1)

            def ffn(layer):
                r0, e0 = R[f"ffn{layer}_in"], E0[f"ffn{layer}_in"]
                w0 = V0[f"fw{layer}"]
                before, per = steps[0], 2 * 6
                with dve.Fori(0, FC // 2) as i:
                    steps[0] = i * per + before
                    for j in range(2):
                        for m in (2 * j, 2 * j + 1):
                            slot = (e0 + m) % EV_SLOTS
                            w = [vecs[:, bass.ds(i * 16 + (w0 + 4 * m + q), 1)] for q in range(4)]
                            y = SQ[:, j, 0:T2] if m == 2 * j else TS[:, j, 0:T2]
                            dve.wait_ge(lin_free, r0 + i * 4 + m + 1)
                            then(dve.tensor_scalar(y, EV[:, slot, 2:2 + T2], w[2], w[3], ALU.mult, ALU.add))
                            then(dve.scalar_tensor_tensor(out=y, in0=EV[:, slot, 1:1 + T2], scalar=w[1], in1=y, op0=ALU.mult, op1=ALU.add))
                            dve.scalar_tensor_tensor(out=y, in0=EV[:, slot, 0:T2], scalar=w[0], in1=y, op0=ALU.mult, op1=ALU.add)\
                               .then_inc(ev_used, 1)
                        dve.wait_ge(act_done, DONE0[f"ffn{layer}"] + i * 2 + j + 1)
                        dve.wait_ge(ev_used, e0 + i * 4 + 2 * j + 2)
                        y = TS[:, j, 0:T2]
                        then(dve.tensor_tensor(y, y, SQ[:, j, 0:T2], ALU.mult))
                        parts(y, HIDH[:, bass.ds(i * (2 * SEQ) + j * SEQ, SEQ)], HIDL[:, bass.ds(i * (2 * SEQ) + j * SEQ, SEQ)])\
                            .then_inc(hid_ready, 1)
                steps[0] = before + per * (FC // 2)
                residual_loop(f"ffn{layer}_out", T2)

            dve.wait_ge(consts_loaded, 32)
            dve.wait_ge(x_loaded, 16)
            dve.wait_ge(pads_zeroed, 7)
            reciprocal_root(R["n1"], T1)
            for c in range(C):
                y = TS[:, c % 2, :]
                then(dve.scalar_tensor_tensor(out=y, in0=H[:, c, :], scalar=vec("norm1", c), in1=TS[:, 2, :], op0=ALU.mult, op1=ALU.mult))
                parts(y, XH[:, c, :], XL[:, c, :]).then_inc(x_ready, 1)
            a, b = 16, 16 + T1
            dve.wait_ge(inv_loaded, 16)
            dve.wait_ge(lin_free, R["in1"] + 2)
            then(dve.tensor_tensor(sum2[:, :, a:b], apad[:, :, a:b], apad[:, :, a - 1:b - 1], ALU.add))
            then(dve.tensor_tensor(sum4[:, :, a:b], sum2[:, :, a:b], sum2[:, :, a - 2:b - 2], ALU.add))
            then(dve.tensor_tensor(sum8[:, a:b], sum4[:, 1, a:b], sum4[:, 1, a - 4:b - 4], ALU.add))
            then(dve.tensor_tensor(sum2[:, 1, a:b], sum8[:, a:b], sum8[:, a - 8:b - 8], ALU.add))
            for c, (low_, high) in enumerate(((sum2[0:HD, 0, a:b], sum4[HD:P, 0, a:b]), (sum8[0:HD, a:b], sum2[HD:P, 1, a:b]))):
                then(dve.tensor_tensor(TS[0:HD, c, :], low_, inv[0:HD, c, :], ALU.mult))
                then(dve.tensor_tensor(TS[HD:P, c, :], high, inv[HD:P, c, :], ALU.mult))
                dve.tensor_tensor(TS[:, c, :], TS[:, c, :], apad[:, c, a:b], ALU.subtract).then_inc(dve_ready, 1)
            dve.wait_ge(lin_free, R["in1"] + 6)
            g0 = KS - 1
            then(dve.tensor_tensor(glu[:, :, g0:g0 + T1], glu[:, :, g0:g0 + T1], sig[:, :, :], ALU.mult))
            for c in range(2):
                y = sig[:, c, :]
                then(dve.tensor_scalar(y, glu[:, c, 0:T1], vec("conv_w", c * KS), vec("conv_b", c), ALU.mult, ALU.add))
                for k in range(1, KS):
                    ins = dve.scalar_tensor_tensor(out=y, in0=glu[:, c, k:k + T1], scalar=vec("conv_w", c * KS + k), in1=y,
                                                   op0=ALU.mult, op1=ALU.add)
                    if k < KS - 1:
                        then(ins)
                ins.then_inc(dve_ready, 1)
            dve.wait_ge(act_done, DONE0["fg"] + 1)
            z, soft, total = (staged(e, T1)[0:FOX_H, :] for e in (0, 1, 2))
            then(dve.tensor_scalar(z, z, 0.0, None, ALU.min))
            then(dve.tensor_tensor(soft, soft, z, ALU.subtract))
            dve.tensor_tensor_scan(total, consts[0:FOX_H, C0["ones"]:C0["ones"] + 1].to_broadcast([FOX_H, T1]), soft, 0.0,
                                   ALU.mult, ALU.add).then_inc(dve_ready, 1)
            for c in range(2):
                dve.wait_ge(lin_free, R["pool"] + c + 1)
                then(dve.tensor_scalar(apad[:, c, a:b], apad[:, c, a:b], vec("pool_s", c), None, ALU.mult))
                parts(apad[:, c, a:b], o_hi(c, T1), o_lo(c, T1)).then_inc(hid_ready, 1)
            dve.wait_ge(lin_free, R["ln"] + 1)
            for c in range(2):
                dve.tensor_tensor(sig[:, c, :], sig[:, c, :], TS[:, 2, :], ALU.add).then_inc(act_asked, 1)
            reciprocal_root(R["ln"] + 1, T1)
            for c in range(2):
                dve.scalar_tensor_tensor(out=sig[:, c, :], in0=sig[:, c, :], scalar=vec("ln_g", c), in1=TS[:, 2, :],
                                         op0=ALU.mult, op1=ALU.mult).then_inc(act_asked, 1)
            for c in range(2):
                dve.wait_ge(act_done, DONE0["ln"] + c + 1)
                parts(sig[:, c, :], o_hi(2 + c, T1), o_lo(2 + c, T1)).then_inc(hid_ready, 1)
            dve.wait_ge(lin_free, R["nf"] + FOX_H)

            def masked_fox(n, s, rows, keys):
                h, t = FOX_ITEMS[n]
                add_mask(s[0:rows, 0:keys], NF[0:rows, h, 0:keys])
                add_mask(s[0:rows, keys - rows:keys], const("causal", rows, rows))

            def kept_fox(n, a, o, rs, rows):
                h, t = FOX_ITEMS[n]
                return dve.tensor_scalar(OT1[0:rows, t, h * HD:(h + 1) * HD], o, rs, None, ALU.mult)

            attention("fox", FOX_ITEMS, fox_item, masked_fox, kept_fox)
            feature_parts("ot1", 4, T1, 4)
            with dve.Fori(0, 4) as i:
                for m in range(2):
                    r, e = R["merge"] + 6 * m, E0["merge"] + 6 * m
                    dve.wait_ge(hid_ready, HID0["merge"] + i * 2 + m)
                    for g in range(3):
                        dve.wait_ge(lin_free, r + i * 12 + 4 + g)
                        dve.tensor_tensor(TS[:, g, :], staged(e + g, T1), staged(e + 3 + g, T1), ALU.mult).then_inc(ev_used, 1)
                    dve.wait_ge(ev_used, e + i * 12 + 3)
                    dve.tensor_tensor(TS[:, 0, :], TS[:, 0, :], TS[:, 1, :], ALU.add).then_inc(ev_used, 1)
                    dve.wait_ge(ev_used, e + i * 12 + 4)
                    dve.tensor_tensor(TS[:, 0, :], TS[:, 0, :], TS[:, 2, :], ALU.add).then_inc(ev_used, 1)
                    dve.wait_ge(ev_used, e + i * 12 + 5)
                    hi = HIDH[:, bass.ds(i * (2 * T1) + (C + m) * T1, T1)]
                    lo = HIDL[:, bass.ds(i * (2 * T1) + (low - (C - m) * T1), T1)]
                    dve.tensor_copy(hi, TS[:, 0, :]).then_inc(ev_used, 1)
                    dve.wait_ge(ev_used, e + i * 12 + 6)
                    dve.tensor_tensor(lo, TS[:, 0, :], hi.bitcast(F32), ALU.subtract).then_inc(hid_ready, 1)
            residual_loop("wo1", T1)
            reciprocal_root(R["n2"], T1)
            normed("norm2", T1, x_hi(T1), x_lo(T1), U["router"])
            dve.wait_ge(lin_free, R["router"] + 1)
            NTT = QT + 1

            def wide(ap, n=4):
                return ap.unsqueeze(2).to_broadcast([P, NTT, n])

            def vec_rows(name, a, n):
                return vecs[:, V0[name] + a:V0[name] + a + n].unsqueeze(1).to_broadcast([P, NTT, n])

            glog, elog = route[:, 0, :, 0:4], route[:, 1, :, :]
            val = [route[:, 2, :, k] for k in range(10)]
            less, ex = route[:, 3, :, :], route[:, 4, :, :]
            prio = vec_rows("prio", 0, 4)

            def first_of(out_, src, top, best):
                then(dve.tensor_tensor(out_, src, wide(top), ALU.is_equal))
                then(dve.tensor_tensor(out_, out_, prio, ALU.mult))
                then(dve.tensor_reduce(best, out_, AX, ALU.max))
                then(dve.tensor_tensor(out_, out_, wide(best), ALU.is_equal))

            group, top1, top2, rest, w = (route[:, k, :, 0:4] for k in (5, 7, 8, 9, 10))
            then(dve.tensor_tensor(glog, glog, vec_rows("rbias", 0, 4), ALU.add))
            then(dve.tensor_tensor(elog, elog, vec_rows("rbias", 4, 16), ALU.add))
            then(dve.tensor_reduce(val[0], glog, AX, ALU.max))
            then(dve.tensor_tensor(less[:, :, 0:4], glog, wide(val[0]), ALU.subtract))
            first_of(group, glog, val[0], val[1])
            grid = route[:, 6, :, :].rearrange("p t (g e) -> p t g e", g=N_GRP)
            then(dve.tensor_tensor(grid, elog.rearrange("p t (g e) -> p t g e", g=N_GRP),
                                   group.unsqueeze(3).to_broadcast([P, NTT, N_GRP, PER_GRP]), ALU.mult))
            then(dve.tensor_reduce(rest, route[:, 6, :, :].rearrange("p t (g e) -> p t e g", g=N_GRP), AX, ALU.add))
            then(dve.tensor_reduce(val[2], rest, AX, ALU.max))
            dve.tensor_tensor(less[:, :, 4:8], rest, wide(val[2]), ALU.subtract).then_inc(act_asked, 1)
            dve.wait_ge(act_done, DONE0["router"] + 1)
            then(dve.tensor_reduce(val[3], ex[:, :, 0:4], AX, ALU.add))
            then(dve.tensor_reduce(val[4], ex[:, :, 4:8], AX, ALU.max))
            first_of(top1, ex[:, :, 4:8], val[4], val[5])
            then(dve.scalar_tensor_tensor(out=rest, in0=top1, scalar=-2.0, in1=ex[:, :, 4:8], op0=ALU.mult, op1=ALU.add))
            then(dve.tensor_reduce(val[6], rest, AX, ALU.max))
            first_of(top2, rest, val[6], val[7])
            then(dve.tensor_tensor(val[8], val[4], val[6], ALU.add))
            then(dve.tensor_tensor(val[8], val[8], val[3], ALU.mult))
            then(dve.reciprocal(val[9], val[8]))
            then(dve.tensor_tensor(w, top1, top2, ALU.add))
            then(dve.tensor_tensor(w, w, ex[:, :, 4:8], ALU.mult))
            then(dve.tensor_tensor(w, w, wide(val[9]), ALU.mult))
            dve.tensor_tensor(route[:, 11, :, :].rearrange("p t (g e) -> p t g e", g=N_GRP),
                              w.unsqueeze(2).to_broadcast([P, NTT, N_GRP, PER_GRP]),
                              group.unsqueeze(3).to_broadcast([P, NTT, N_GRP, PER_GRP]), ALU.mult).then_inc(dve_ready, 1)
            dve.wait_ge(lin_free, R["cb"] + N_EXP)
            before, per = steps[0], 8
            with dve.Fori(0, N_GRP) as i:
                steps[0] = i * per + before
                r, e = R["moe"], E0["moe"]
                for j in range(C):
                    y = TS[:, j % 2, :]
                    dve.wait_ge(lin_free, r + i * 24 + 2 * j + 2)
                    dve.tensor_tensor(y, staged(e + 2 * j, T1), staged(e + 2 * j + 1, T1), ALU.mult).then_inc(ev_used, 1)
                    dve.wait_ge(ev_used, e + i * 24 + 2 * j + 1)
                    dve.tensor_tensor(y, y, CB[:, i * PER_GRP + j // 2, :], ALU.mult).then_inc(ev_used, 1)
                    dve.wait_ge(ev_used, e + i * 24 + 2 * j + 2)
                    if j == 0:
                        dve.wait_ge(unit_used, U["moe"] + i * 24)
                    parts(y, o_hi(j, T1), o_lo(j, T1)).then_inc(hid_ready, 1)
                for j in range(C):
                    dve.wait_ge(lin_free, r + i * 24 + 16 + j + 1)
                    dve.tensor_tensor(H[:, j, :], H[:, j, :], staged(e + 16 + j, T1), ALU.add).then_inc(ev_used, 1)
            steps[0] = before + per * N_GRP
            reciprocal_root(R["nf1"], T1)
            normed_in_place("final1", TS[:, 2, META:T1])
            reciprocal_root(R["na0"], T2)
            normed("attn0", T2, x_hi(T2), x_lo(T2), U["kc"])
            dve.wait_ge(lin_free, R["tok2"] + 1)
            for t in range(QT):
                g = gate48[:, t, 0:3 * NH:3]
                ins = dve.tensor_scalar(g, g, vec("cvalid", t), None, ALU.mult)
                then(ins)
            dve.wait_ge(pairs_moved, 64)
            for kv in range(2):
                if kv:
                    dve.wait_ge(dve_ready, 7)
                for b in range(CMP_B // 2):
                    ins = dve.tensor_scalar(BLK[:, b, :].rearrange("p (g n) -> p g n", g=A_G),
                                            PAIR[:, 2 * kv:2 * kv + 2, :, b:b + 8 * (NC - 1) + 1:8].rearrange("p q g n -> p (q g) n"),
                                            vec("cpos", kv * (CMP_B // 2) + b), None, ALU.add)
                    if b == CMP_B // 2 - 1:
                        then(ins)
                if kv:
                    dve.wait_ge(unit_used, U["cmp"] + 4)
                parts(BLK[:, :, :], BLKH[:, :, :], BLKL[:, :, :]).then_inc(dve_ready, 1)
            dve.wait_ge(lin_free, R["cmp"] + 7)
            k_, kr = (staged(E0["cmp"] + x, 2 * NC).rearrange("p (g n) -> p g n", g=2) for x in range(2))
            cosc, sinc = (const(x).unsqueeze(1).to_broadcast([P, 2, NC]) for x in ("cosc", "sinc"))
            ta, tb = (TS[:, x, 0:2 * NC].rearrange("p (g n) -> p g n", g=2) for x in range(2))
            dve.tensor_tensor(ta, k_, cosc, ALU.mult).then_inc(ev_used, 1)
            dve.tensor_tensor(tb, kr, sinc, ALU.mult).then_inc(ev_used, 1)
            dve.wait_ge(ev_used, E0["cmp"] + 2)
            dve.tensor_tensor(KCMP[:, :, 0:NC], ta, tb, ALU.add).then_inc(rope_ready, 1)
            rotated("rope2", 12, lambda c: KSEL[:, c, :] if c < 2 else KWIN[:, c - 2, :] if c < 4 else Q2[:, c - 4, :])

            def masked_nsa(n, s, rows, keys):
                gp, r, g2, t, b = NSA_ITEMS[n]
                if b == 0:
                    add_mask(s[:, 0:NC], const("cmask", NC, start=t * NC))
                else:
                    add_mask(s[:, keys - P:keys], const("causal"))

            def kept_nsa(n, a, o, rs, rows):
                gp, r, g2, t, b = NSA_ITEMS[n]
                h = (2 * gp + g2) * 4 + r
                then(dve.tensor_tensor(rs, rs, gate48[:, t, 3 * h + b:3 * h + b + 1], ALU.mult))
                ot = OT2[:, t, h * HD:(h + 1) * HD]
                if b == 0:
                    return dve.tensor_scalar(ot, o, rs, None, ALU.mult)
                dve.wait_ge(o_ready, a)
                return dve.scalar_tensor_tensor(out=ot, in0=o, scalar=rs, in1=ot, op0=ALU.mult, op1=ALU.add)

            attention("nsa", NSA_ITEMS, nsa_item, masked_nsa, kept_nsa)
            feature_parts("ot2", C, T2, 0)
            residual_loop("wo2", T2)
            reciprocal_root(R["nf0"], T2)
            normed("ffn0", T2, x_hi(T2), x_lo(T2), U["wo2"])
            ffn(0)
            reciprocal_root(R["na1"], T2)
            normed("kv", T2, lambda c: o_hi(c, T2), lambda c: o_lo(c, T2), U["k3"])
            normed("attn1", T2, x_hi(T2), x_lo(T2), U["k3"])
            dve.wait_ge(x_ready, X0["nf_1"])
            rotated("k3", 1, lambda c: K3[:, :])
            rotated("q3", 8, lambda c: Q3[:, c, :])

            def masked_swa(n, s, rows, keys):
                r, g, t = SWA_ITEMS[n]
                h = g * 8 + r
                then(dve.tensor_copy(s[:, keys:keys + 1], vec("sink", h)))
                add_mask(s[:, 0:keys], const("causal") if t == 0 else const("band"))

            def kept_swa(n, a, o, rs, rows):
                r, g, t = SWA_ITEMS[n]
                h = g * 8 + r
                return dve.tensor_scalar(OT3[:, t, h * HD:(h + 1) * HD], o, rs, None, ALU.mult)

            attention("swa", SWA_ITEMS, swa_item, masked_swa, kept_swa, 1)
            feature_parts("ot3", C, T2, 0)
            residual_loop("wo3", T2)
            reciprocal_root(R["nf_1"], T2)
            normed("ffn1", T2, x_hi(T2), x_lo(T2), U["wo3"])
            ffn(1)
            reciprocal_root(R["nfin"], T2)
            normed_in_place("final2", TS[:, 2, 0:T2])


def units_of(w):
    rows, cols = w.shape
    w = w.reshape(rows // UNIT, KC, P, cols // P, P).transpose(3, 0, 2, 1, 4)
    return w.reshape(-1, P, UNIT)


def padded(w, cols):
    out = np.zeros((w.shape[0], cols), np.float32)
    out[:, :w.shape[1]] = w
    return out


def lay_stream(a):
    w = np.asarray(a["w_in"])[0]
    cut = np.cumsum([POOL_W, CONV_W, CONV_W, FOX_W, FOX_W, FOX_W, FOX_H])
    pool, bv, bg, q, k, v, fg, gates = np.split(w, cut, axis=1)
    seq = [units_of(x) for x in (pool, bv, bg, q, k, padded(fg, P), v)]
    branch = units_of(np.concatenate([np.asarray(a[n])[0] for n in ("w_out_a", "w_out_b", "w_out_c")], axis=0))
    gate = units_of(gates).reshape(3, C, P, UNIT)
    seq.append(np.concatenate([gate, branch[None]], axis=0).transpose(1, 0, 2, 3).reshape(-1, P, UNIT))
    seq.append(units_of(np.asarray(a["w_o"])[0]))
    seq.append(units_of(padded(np.concatenate([np.asarray(a["router_g"])[0], np.asarray(a["router_e"])[0]], axis=1), P)))
    w1, w3, w2 = (np.asarray(a[n])[0] for n in ("exp_w1", "exp_w3", "exp_w2"))
    for g in range(N_GRP):
        for e in range(g * PER_GRP, (g + 1) * PER_GRP):
            seq.append(np.stack([units_of(w1[e]), units_of(w3[e])], axis=1).reshape(-1, P, UNIT))
        seq.append(units_of(w2[g * PER_GRP:(g + 1) * PER_GRP].reshape(PER_GRP * EXP_HID, D)))
    w = np.asarray(a["a_w_in_2"])[0]
    q, kc, vc, ks, vs, kw, vw, gl = np.split(w, np.cumsum([NH * HD] + [A_G * HD] * 6), axis=1)
    q = q.reshape(D, 2, 2, 4, HD).transpose(0, 1, 3, 2, 4).reshape(D, D)
    seq += [units_of(x) for x in (kc, vc, padded(gl, P), vs, vw)]
    c1 = np.asarray(a["a_cmp_w1_2"])[0]
    seq += [units_of(c1[0]), units_of(c1[1])]
    seq += [units_of(x) for x in (ks, kw, q, np.asarray(a["a_w_out_2"])[0])]

    def ffn(layer):
        w = units_of(np.asarray(a["ffn_w_in_2"])[layer]).reshape(2, FC, P, UNIT).transpose(1, 0, 2, 3).reshape(-1, P, UNIT)
        o = np.zeros((3 * UNIT, D), np.float32)
        o[:DFF] = np.asarray(a["ffn_w_out_2"])[layer]
        return [w, units_of(o)]

    seq += ffn(0)
    k, v = np.split(np.asarray(a["b_w_kv_2"]), 2, axis=1)
    q = np.asarray(a["b_w_q_2"])[0].reshape(D, B_G, 8, HD).transpose(0, 2, 1, 3).reshape(D, D)
    seq += [units_of(x) for x in (k, v, q, np.asarray(a["b_w_out_2"])[0])]
    seq += ffn(1)
    out = np.concatenate(seq, axis=0)
    assert out.shape == (N_UNITS, P, UNIT), out.shape
    return np.ascontiguousarray(out)


def lay_vecs(a):
    def cols(x):
        return np.asarray(x).reshape(-1, P).T

    def rows(x):
        return np.tile(np.asarray(x).reshape(1, -1), (P, 1))

    out = {"norm1": cols(a["norm1_g"]), "norm2": cols(a["norm2_g"]), "final1": cols(a["final_g"]),
           "attn0": cols(np.asarray(a["norm_attn_2"])[0]), "attn1": cols(np.asarray(a["norm_attn_2"])[1]),
           "ffn0": cols(np.asarray(a["norm_ffn_2"])[0]), "ffn1": cols(np.asarray(a["norm_ffn_2"])[1]),
           "kv": cols(a["kv_norm_2"]), "final2": cols(a["final_norm_2"]), "pool_b": cols(a["pool_b"]), "pool_s": cols(a["pool_scale"]),
           "conv_b": cols(a["conv_b"]), "ln_g": cols(a["conv_ln_g"]), "ln_b": cols(a["conv_ln_b"]),
           "conv_w": np.asarray(a["conv_w"])[0].T.reshape(2, P, KS).transpose(1, 0, 2).reshape(P, 2 * KS),
           "bforget": np.concatenate([np.asarray(a["b_forget"]).reshape(-1, 1), np.zeros((P - FOX_H, 1), np.float32)]),
           "sink": rows(a["b_sinks_2"]),
           "rbias": np.concatenate([rows(a["router_g_b"]), rows(a["router_e_b"])], axis=1),
           "prio": rows(np.arange(4, 0, -1, dtype=np.float32)), "eps": np.full((P, 1), EPS), "one": np.ones((P, 1)),
           "cpos": np.asarray(a["a_cmp_pos_2"])[0].reshape(2, CMP_B // 2, P).transpose(2, 0, 1).reshape(P, -1)}
    valid = (np.arange(SEQ) >= CMP_B - 1).astype(np.float32)
    out["cvalid"] = valid.reshape(QT, P).T
    for layer in range(2):
        w = np.concatenate([np.asarray(a["ffn_conv_w_2"])[layer], np.asarray(a["ffn_conv_b_2"])[layer][None]], axis=0)
        out[f"fw{layer}"] = w.reshape(4, 2, FC, P).transpose(3, 2, 1, 0).reshape(P, -1)
    return np.ascontiguousarray(np.concatenate([out[n].astype(np.float32) for n, _ in VECS], axis=1))


def lay_consts(a):
    f = np.float32
    rot = np.zeros((P, P), f)
    half = HD // 2
    for h in range(2):
        for d in range(half):
            rot[h * HD + d + half, h * HD + d] = -1.0
            rot[h * HD + d, h * HD + d + half] = 1.0
    i, j = np.arange(P)[:, None], np.arange(P)[None, :]
    causal = np.where(j <= i, 0.0, NEG)
    band = np.concatenate([np.where(j > i, 0.0, NEG), causal], axis=1)
    ends = np.arange(NC) * CMP_S + CMP_B - 1
    cmask = np.where(ends[None, :] <= np.arange(SEQ)[:, None], 0.0, NEG).reshape(QT, P, NC).transpose(1, 0, 2).reshape(P, -1)
    angle = f(10000.0) ** (-np.arange(half, dtype=f) / f(half))

    def table(fn, pos):
        t = fn((pos.astype(f)[:, None] * angle[None, :]).astype(f)).T
        return np.concatenate([t] * 4, axis=0)

    pw = np.asarray(a["pool_w"])[0]
    poolw = np.zeros((P, 2 * P), f)
    for g in range(4):
        lo = HD * (g % 2)
        poolw[lo:lo + HD, (g // 2) * P + lo:(g // 2) * P + lo + HD] = pw[g]
    w2 = np.asarray(a["a_cmp_w2_2"])[0].reshape(2, 2, P, HD)
    w2k = np.zeros((P, 2, 2, P), f)
    for j in range(2):
        w2k[:, j, 0, 0:HD] = w2[0, j]
        w2k[:, j, 1, HD:P] = w2[0, j]
    pos = np.arange(SEQ)
    out = {"ident": np.eye(P), "ones": np.ones((P, P)), "rot": rot, "causal": causal, "band": band, "poolw": poolw,
           "cosq": table(np.cos, pos), "sinq": table(np.sin, pos), "cosc": table(np.cos, ends), "sinc": table(np.sin, ends),
           "cmask": cmask, "w2k": w2k.reshape(P, -1), "w2v": w2[1].transpose(1, 0, 2).reshape(P, -1)}
    return np.ascontiguousarray(np.concatenate([out[n].astype(f) for n, _ in CONSTS], axis=1))


def lay_inverse_counts():
    out = np.zeros((P, 2, T1), np.float32)
    for g, window in enumerate((2, 4, 8, 16)):
        lo = HD * (g % 2)
        out[lo:lo + HD, g // 2, :] = 1.0 / np.minimum(np.arange(T1) + 1, window)
    return out


def kernel(**inputs):
    import concourse.bacc as bacc
    from concourse.bass_utils import run_bass_kernel_spmd

    h = np.concatenate([np.asarray(inputs["meta"]), np.asarray(inputs["x"])[0]], axis=0)
    arrays = {"stream": lay_stream(inputs), "x_fm": np.ascontiguousarray(h.T.reshape(C, P, T1).transpose(1, 0, 2)),
              "vecs_in": lay_vecs(inputs), "consts_in": lay_consts(inputs), "inv_counts": lay_inverse_counts()}
    nc = bacc.Bacc("TRN2", target_bir_lowering=False, num_devices=1)
    aps = [nc.dram_tensor(n, x.shape, F32, kind="ExternalInput").ap() for n, x in arrays.items()]
    out = nc.dram_tensor("out_fm", [P, C, SEQ], F32, kind="ExternalOutput").ap()
    build(nc, *aps, out)
    got = run_bass_kernel_spmd(nc, [arrays], core_ids=[0]).results[0]["out_fm"]
    return np.ascontiguousarray(got.transpose(1, 0, 2).reshape(D, SEQ).T)[None]
```

```python
from contextlib import ExitStack

import numpy as np
import concourse.bass as bass
from concourse import mybir

F32 = mybir.dt.float32
F32R = mybir.dt.float32r
ALU = mybir.AluOpType
ACT = mybir.ActivationFunctionType
AX = mybir.AxisListType.X

P = 128
D = 1024
C = D // P
SEQ, META = 512, 16
T1, T2 = SEQ + META, SEQ
HALF = T1 // 2
QT = SEQ // P
HD = 64
EPS = 1e-6
NEG = -1e30
KC = 8
UNIT = KC * P
POOL_W, CONV_W, FOX_H, KS = 256, 256, 8, 31
FOX_W = FOX_H * HD
N_GRP, PER_GRP = 4, 4
N_EXP, EXP_HID = 16, 256
NH, A_G, B_G = 16, 4, 2
CMP_B, CMP_S, CMP_HID = 32, 16, 256
NC = SEQ // CMP_S - CMP_B // CMP_S + 1
WIN_B = 128
DFF = 2816
FC = DFF // P
SCALE = HD ** -0.5

PARTS = [("pool", 2), ("bv", 2), ("bg", 2), ("fg", 1), ("q1", 4), ("v1", 4), ("k1", 4),
         ("merge", 32), ("wo1", 8), ("router", 1), ("moe", 96),
         ("kc", 2), ("vc", 2), ("gl", 1), ("vs", 2), ("vw", 2), ("cmp", 8), ("ks", 2), ("kw", 2), ("q2", 8), ("wo2", 8),
         ("ffn0_in", 2 * FC), ("ffn0_out", 24),
         ("k3", 1), ("v3", 1), ("q3", 8), ("wo3", 8), ("ffn1_in", 2 * FC), ("ffn1_out", 24)]
U = {}
N_UNITS = 0
for _name, _count in PARTS:
    U[_name] = N_UNITS
    N_UNITS += _count
RAW, SPLIT = 4, 2

VECS = [("norm1", 8), ("norm2", 8), ("final1", 8), ("attn0", 8), ("ffn0", 8), ("kv", 8), ("attn1", 8), ("ffn1", 8),
        ("final2", 8), ("pool_b", 2), ("pool_s", 2), ("conv_b", 2), ("ln_g", 2), ("ln_b", 2), ("conv_w", 2 * KS),
        ("bforget", 1), ("fw0", 2 * FC * 4), ("fw1", 2 * FC * 4), ("sink", NH), ("rbias", N_GRP + N_EXP),
        ("prio", 4), ("eps", 1), ("one", 1), ("cvalid", QT), ("cpos", 2 * CMP_B // 2)]
V0 = {}
N_VEC = 0
for _name, _count in VECS:
    V0[_name] = N_VEC
    N_VEC += _count

CONSTS = [("ident", P), ("ones", P), ("rot", P), ("causal", P), ("band", 2 * P), ("poolw", 2 * P),
          ("cosq", SEQ), ("sinq", SEQ), ("cosc", NC), ("sinc", NC), ("cmask", QT * NC), ("w2k", 4 * P), ("w2v", 2 * HD)]
C0 = {}
N_CONST = 0
for _name, _count in CONSTS:
    C0[_name] = N_CONST
    N_CONST += _count

STAGES = [("n1", 1), ("in1", 11), ("pool", 2), ("v1", 8), ("ln", 1), ("k1a", 1), ("lnv", 1), ("k1b", 3), ("ot1", 4), ("merge", 48), ("wo1", 8),
          ("n2", 1), ("router", 1), ("moe_a", 1), ("routerT", 1), ("moe_b", 3), ("combT", 1), ("cb", N_EXP), ("moe", 92), ("nf1", 1), ("na0", 1),
          ("kcvc", 4), ("tok2", 10), ("cmp", 7), ("rope2", 24), ("ot2", 8), ("wo2", 8),
          ("nf0", 1), ("ffn0_in", 2 * FC), ("ffn0_out", 8), ("na1", 1), ("kv3", 4), ("q3", 16), ("ot3", 8), ("wo3", 8),
          ("nf_1", 1), ("ffn1_in", 2 * FC), ("ffn1_out", 8), ("nfin", 1)]
R = {}
N_RES = 0
for _name, _count in STAGES:
    R[_name] = N_RES
    N_RES += _count
HEAD = 4
PAIRS = 4

STAGED = [("ot1", 4), ("merge", 48), ("wo1", 8), ("moe", 96), ("cmp", 2), ("rope2", 24), ("ot2", 8), ("wo2", 8), ("ffn0_in", 2 * FC),
          ("ffn0_out", 8), ("k3", 2), ("q3", 16), ("ot3", 8), ("wo3", 8), ("ffn1_in", 2 * FC), ("ffn1_out", 8)]
E0 = {}
N_EV = 0
for _name, _count in STAGED:
    E0[_name] = N_EV
    N_EV += _count
EV_SLOTS = 4

FOX_ITEMS = [(half, t) for half in range(2) for t in range(QT + 1)]
NSA_ITEMS = [(half, t, b) for half in range(2) for t in range(QT) for b in range(3)]
SWA_ITEMS = [(half, t) for half in range(2) for t in range(QT)]
ITEMS = {"fox": FOX_ITEMS, "nsa0": NSA_ITEMS, "nsa1": NSA_ITEMS, "swa": SWA_ITEMS}
CHUNKS = {"fox": 4, "nsa0": 4, "nsa1": 4, "swa": 8}
DEPTH = {"fox": 3, "nsa0": 4, "nsa1": 4, "swa": 4}
LAG = {"fox": 3, "nsa0": 3, "nsa1": 3, "swa": 3}
FOX_BANK = [0, 1, 2, 3, 0, 2, 3, 0, 1, 2]
FOX_PROBS = [0, 1, 2, 0, 1, 2, 0, 1, 2, 3]
MASKS = {"fox": 1, "nsa0": 1, "nsa1": 1, "swa": 2}
A0, Q0, O0, M0 = {}, {}, {}, {}
W0 = {"nsa0": 0, "nsa1": 4 * len(NSA_ITEMS)}
_a = _q = _o = _m = 0
for _name, _items in ITEMS.items():
    A0[_name], Q0[_name], O0[_name], M0[_name] = _a, _q, _o, _m
    _n = len(_items) * CHUNKS[_name]
    _a, _q, _m = _a + _n, _q + CHUNKS[_name], _m + _n * MASKS[_name]
    _o += _n // 3 if _items is NSA_ITEMS else _n


def at(i, stride, base=0):
    return i * stride + base


ALONE = [("pool", 2), ("v1", 4), ("ln", 1), ("ot1", 4), ("merge", 16), ("routerT", 1), ("combT", 1), ("cb", N_EXP), ("tok2", 5), ("cmp", 3),
         ("rope2", 12), ("ot2", 8), ("k3", 1), ("v3", 1), ("q3", 8), ("ot3", 8)]
L0 = {}
N_ALONE = 0
for _name, _count in ALONE:
    L0[_name] = N_ALONE
    N_ALONE += _count

X0 = {"n1": 0, "n2": C, "na0": 2 * C, "nf0": 3 * C, "kv": 4 * C, "na1": 5 * C, "nf_1": 6 * C}
HID0 = {"pool": 0, "conv": 2, "merge": 4, "moe": 12, "ffn0": 44, "ffn1": 44 + FC}
SQ0 = {"n1": 0, "ln": C, "n2": C + 2, "nf1": 2 * C + 2, "na0": 3 * C + 2, "nf0": 4 * C + 2, "na1": 5 * C + 2, "nf_1": 6 * C + 2,
       "nfin": 7 * C + 2}
SUMS = {"n1": C, "ln": 2, "n2": 2, "nf1": C, "na0": C, "nf0": 2, "na1": 2, "nf_1": 2, "nfin": 2}
S0 = {_name: sum(list(SUMS.values())[:_i]) for _i, _name in enumerate(SUMS)}
ADD0 = {_name: _i * (C - 2) for _i, _name in enumerate(("n2", "nf0", "na1", "nf_1", "nfin"))}
ROPE0 = {"rope2": 1, "k3": 13, "q3": 14}
DONE0 = {"fg": 0, "ln": 1, "router": 3, "ffn0": 4, "ffn1": 4 + FC}


def build(nc, stream, x_in, vecs_in, consts_in, invcnt_in, out):
    with ExitStack() as ctx:
        def sb(name, shape, dt=F32):
            return ctx.enter_context(nc.sbuf_tensor(name, shape, dt))

        def sem(name):
            return ctx.enter_context(nc.semaphore(name))

        arena_at = (nc.sbuf_base + 31) // 32 * 32
        sb("arena", [P, 2 * FC * SEQ])
        HIDH = nc.alloc_sbuf_tensor_at("hid_hi", [P, FC * SEQ], F32R, offset=arena_at)
        HIDL = nc.alloc_sbuf_tensor_at("hid_lo", [P, FC * SEQ], F32R, offset=arena_at + FC * SEQ * 4)
        SPARE = nc.alloc_sbuf_tensor_at("spare", [P, C * T1], F32, offset=arena_at)
        raw = sb("raw", [P, RAW, UNIT])
        w_hi = sb("w_hi", [P, SPLIT, UNIT], F32R)
        w_lo = sb("w_lo", [P, SPLIT, UNIT], F32R)
        XH = sb("x_hi", [P, C, T1], F32R)
        XL = sb("x_lo", [P, C, T1], F32R)
        H = sb("resid", [P, C, T1])
        EV = sb("staged", [P, EV_SLOTS, 2 + T1])
        TS = sb("scratch", [P, 3, T1])
        SQ = sb("squares", [P, 2, T1])
        vecs = sb("vecs", [P, N_VEC])
        consts = sb("consts", [P, N_CONST])
        gate48 = sb("gate48", [P, QT, 3 * NH])
        route = sb("route", [P, 12, QT + 1, 16])
        ones2 = sb("ones2", [2, P], F32R)
        one_root = sb("one_root", [P, 1])
        one_exp = sb("one_exp", [P, 1])
        stat = sb("stat", [P, 3, len(NSA_ITEMS)])
        o_bytes, end_bytes = C * T1 * 4, 2 * FC * SEQ * 4 - C * T1 * 4
        low = FC * SEQ - C * T1
        cursor = [o_bytes]

        def over(name, shape, dt=F32, at=None):
            size = 4
            for s in shape[1:]:
                size *= s
            start = cursor[0] if at is None else at
            if at is None:
                cursor[0] += -(-size // 32) * 32
            assert start + size <= end_bytes, (name, start + size, end_bytes)
            return nc.alloc_sbuf_tensor_at(name, shape, dt, offset=arena_at + start)

        Q1 = over("q1", [P, 4, T1])
        K1 = over("k1", [P, 4, T1])
        V1 = over("v1", [P, QT + 1, FOX_W])
        nf_at = cursor[0]
        NF = over("neg_cum_logf", [P, FOX_H, T1], F32R)
        OT1 = over("o_tok1", [P, QT + 1, FOX_W])
        cursor[0] = nf_at
        apad = over("a_pad", [P, 2, 16 + T1])
        sum2 = over("sum2", [P, 2, 16 + T1])
        sum4 = over("sum4", [P, 2, 16 + T1])
        sum8 = over("sum8", [P, 16 + T1])
        sig = over("sig", [P, 2, T1])
        glu = over("glu", [P, 2, KS - 1 + T1])
        inv = over("inv_count", [P, 2, T1])
        cursor[0] = o_bytes
        CB = over("comb_rows", [P, N_EXP, T1])
        cursor[0] = o_bytes
        q2_at = cursor[0]
        Q2 = over("q2", [P, 8, SEQ])
        ks_at = cursor[0]
        KSEL = over("k_sel", [P, 2, SEQ])
        KWIN = over("k_win", [P, 2, SEQ])
        VSEL = over("v_sel", [P, QT, 2 * P])
        VWIN = over("v_win", [P, QT, 2 * P])
        KCMP = over("k_cmp", [P, 2, 32])
        VCMP = over("v_cmp", [P, A_G, HD])
        HIDC = over("cmp_hidden", [P, 2, A_G * NC])
        ot_at = cursor[0]
        OT2 = over("o_tok2", [P, QT, D])
        cursor[0] = ot_at
        EO = over("kv_even_odd", [P, 4, 2, SEQ // 2])
        PAIR = over("kv_pairs", [P, 4, 2, SEQ // 2])
        BLK = over("cmp_blocks", [P, CMP_B // 2, A_G * NC], at=ks_at)
        BLKH = over("cmp_blocks_hi", [P, CMP_B // 2, A_G * NC], F32R, at=q2_at)
        BLKL = over("cmp_blocks_lo", [P, CMP_B // 2, A_G * NC], F32R, at=q2_at + CMP_B // 2 * A_G * NC * 4)
        cursor[0] = o_bytes
        Q3 = over("q3", [P, 8, SEQ])
        K3 = over("k3", [P, SEQ])
        V3 = over("v3", [P, QT, P])
        OT3 = over("o_tok3", [P, QT, D])

        PS = ctx.enter_context(nc.psum_tensor("psum", [P, 8, 512], F32))

        raw_loaded = [sem(f"raw_loaded{s}") for s in range(RAW)]
        consts_loaded = sem("consts_loaded")
        x_loaded = [sem(f"x_loaded{i}") for i in range(4)]
        inv_loaded = sem("inv_loaded")
        pairs_moved = sem("pairs_moved")
        stored = sem("stored")
        pads_zeroed = sem("pads_zeroed")
        hi_split = sem("hi_split")
        split_ready = sem("split_ready")
        unit_used = sem("unit_used")
        lin_done = sem("lin_done")
        lin_free = sem("lin_free")
        ev_used = sem("ev_used")
        y_ready = sem("y_ready")
        hi_ready = sem("hi_ready")
        x_ready = sem("x_ready")
        h_ready = sem("h_ready")
        hid_ready = sem("hid_ready")
        sq_ready = sem("sq_ready")
        sq_added = sem("sq_added")
        sq_used = sem("sq_used")
        act_asked = sem("act_asked")
        act_done = sem("act_done")
        dve_step = sem("dve_step")
        act_step = sem("act_step")
        dve_ready = sem("dve_ready")
        rope_ready = sem("rope_ready")
        q_staged = sem("q_staged")
        zeros_written = sem("zeros_written")
        rows_moved = sem("rows_moved")
        masked = sem("masked")
        sum_inverted = sem("sum_inverted")
        weigh_ready = sem("weigh_ready")
        s_done = sem("s_done")
        max_ready = sem("max_ready")
        p_ready = sem("p_ready")
        t_done = sem("t_done")
        pt_ready = sem("pt_ready")
        o_done = sem("o_done")
        o_ready = sem("o_ready")

        def const(name, width=None, rows=P, start=0):
            a = C0[name] + start
            return consts[0:rows, a:a + (width if width else dict(CONSTS)[name])]

        def vec(name, i=0):
            return vecs[:, V0[name] + i:V0[name] + i + 1]

        ident = const("ident")

        def pair(r):
            return PS[:, 2 * (r % PAIRS):2 * (r % PAIRS) + 2, :]

        def halves(ap):
            return ap.rearrange("p (a n) -> p a n", a=2)

        def staged(e, width, shift=2):
            return EV[:, e % EV_SLOTS, shift:shift + width]

        def o_hi(c, t):
            return HIDH[:, c * T1:c * T1 + t]

        def o_lo(c, t):
            return HIDL[:, low + c * T1:low + c * T1 + t]

        def spare(c, t):
            return SPARE[:, c * T1:c * T1 + t]

        def m_hi(c, t):
            return HIDH[:, (C + c) * T1:(C + c) * T1 + t]

        def m_lo(c, t):
            return HIDL[:, low - (C - c) * T1:low - (C - c) * T1 + t]

        QSTAGE = SQ

        def home(kind, i, n):
            return (i, n) if n >= 0 else (i - 1 if isinstance(i, int) else i + -1, n + len(ITEMS[kind]))

        def exists(kind, i, n):
            return n < len(ITEMS[kind]) and (n >= 0 or not isinstance(i, int) or i > 0)

        def number(kind, i, n, per=1, count=A0):
            return at(i, len(ITEMS[kind]) * per, count[kind] + n * per)

        def chunk_queries(kind, i):
            if kind == "fox":
                return Q1[:, i, :]
            if kind == "swa":
                return Q3[:, i, :]
            return Q2[:, at(i, 1, 4 * int(kind[3])), :]

        def queries(kind, n):
            half, t = ITEMS[kind][n][0:2]
            q0 = P * t if kind != "fox" else META + P * (t - 1) if t else 0
            return QSTAGE[:, half, q0:q0 + P]

        def keys_of(kind, i, n):
            half, t = ITEMS[kind][n][0:2]
            if kind == "fox":
                return K1[:, i, 0:META + P * t], META + P * t
            if kind == "swa":
                first = max(t - 1, 0)
                return K3[:, first * P:(t + 1) * P], P * (t + 1 - first)
            gp, b = int(kind[3]), ITEMS[kind][n][2]
            if b == 0:
                return KCMP[:, gp, 0:NC], NC
            return (KSEL if b == 1 else KWIN)[:, gp, 0:P * (t + 1)], P * (t + 1)

        def key_tiles(kind, n):
            t = ITEMS[kind][n][1]
            if kind == "fox":
                return [(META + P * j, P, P * j, j + 1) for j in range(t)] + [(0, META, None, 0)]
            if kind == "swa":
                first = max(t - 1, 0)
                return [(P * (j - first), P, P * (j - first), j) for j in range(first, t + 1)]
            if ITEMS[kind][n][2] == 0:
                return [(0, NC, 0, 0)]
            return [(P * j, P, P * j, j) for j in range(t + 1)]

        def values(kind, i, n, width, j):
            half = ITEMS[kind][n][0]
            if kind == "fox":
                return V1[0:width, j, bass.ds(at(i, P, half * HD), HD)]
            if kind == "swa":
                return V3[:, j, half * HD:(half + 1) * HD]
            g, b = 2 * int(kind[3]) + half, ITEMS[kind][n][2]
            return VCMP[0:NC, g, :] if b == 0 else (VSEL if b == 1 else VWIN)[:, j, g * HD:(g + 1) * HD]

        def scores(kind, n):
            if kind == "fox":
                return PS[:, 0:4, :].rearrange("p a n -> p (a n)")[:, 512 * FOX_BANK[n]:512 * FOX_BANK[n] + (528 if n % 5 == 4 else 512)]
            return PS[:, n % 4, :]

        def probs(kind, n):
            return EV[:, FOX_PROBS[n] if kind == "fox" else n % 4, 2:2 + T1]

        def turned(n):
            return PS[:, 4 + n % 2, :]

        def meta_turned(n):
            t = n % (QT + 1)
            return turned(n)[0:META, t * P:(t + 1) * P] if t < QT else PS[0:META, FOX_BANK[n] + 1, P:2 * P]

        def outs(kind, n):
            return PS[:, 6 + (n // 3 if kind in ("nsa0", "nsa1") else n) % 2, :]

        def turned_copy(n, rows, col):
            return TS[:, 2, (n % 2) * P:(n % 2) * P + rows] if col is None else TS[:, n % 2, col:col + rows]

        def weights(n):
            return TS[:, 2, (n % 4) * P:(n % 4 + 1) * P]

        def token_tiles1():
            return [(0, 1, 0, META)] + [(META + P * i, 0, P * i, P) for i in range(QT)]

        def turning_order(count):
            order = [(0, False)]
            for c in range(1, count):
                order += [(c, False), (c - 1, True)]
            return order + [(count - 1, True)]

        block = ctx.enter_context(nc.Block())

        @block.sync
        def _(sp):
            for i in range(4):
                sp.dma_start(H[:, 2 * i:2 * i + 2, :], x_in[:, 2 * i:2 * i + 2, :]).then_inc(x_loaded[i], 16)
            sp.dma_start(vecs[:, :], vecs_in).then_inc(consts_loaded, 16)
            sp.dma_start(consts[:, :], consts_in).then_inc(consts_loaded, 16)
            sp.dma_start(inv[:, :, :], invcnt_in).then_inc(inv_loaded, 16)
            for s in range(RAW):
                sp.dma_start(raw[:, s, :], stream[s, :, :]).then_inc(raw_loaded[s], 16)
            with sp.Fori(1, N_UNITS // RAW) as i:
                for s in range(RAW):
                    sp.wait_ge(split_ready, i * RAW + (s + 1 - RAW))
                    sp.dma_start(raw[:, s, :], stream[i * RAW + s, :, :]).then_inc(raw_loaded[s], 16)
            for n in range(N_UNITS // RAW * RAW, N_UNITS):
                sp.wait_ge(split_ready, n + 1 - RAW)
                sp.dma_start(raw[:, n % RAW, :], stream[n, :, :]).then_inc(raw_loaded[n % RAW], 16)
            for c in range(0, C, 2):
                sp.wait_ge(h_ready, C + c + 2)
                sp.dma_start(out[:, c:c + 2, :], H[:, c:c + 2, META:T1]).then_inc(stored, 16)
            sp.wait_ge(stored, 16 * C // 2)

        @block.gpsimd
        def _(pool):
            pool.memset(apad[:, :, 0:16], 0.0).then_inc(pads_zeroed, 1)
            pool.memset(sum2[:, :, 0:16], 0.0).then_inc(pads_zeroed, 1)
            pool.memset(sum4[:, :, 0:16], 0.0).then_inc(pads_zeroed, 1)
            pool.memset(sum8[:, 0:16], 0.0).then_inc(pads_zeroed, 1)
            pool.memset(glu[:, :, 0:KS - 1], 0.0).then_inc(pads_zeroed, 1)
            pool.memset(EV[:, :, 0:2], 0.0).then_inc(pads_zeroed, 1)
            pool.memset(route[:, :, :, :], 0.0).then_inc(pads_zeroed, 1)

            def split_unit(slot, n, loads, free):
                pool.wait_ge(raw_loaded[slot], 16 * loads)
                if free:
                    pool.wait_ge(unit_used, n - (SPLIT - 1))
                pool.tensor_tensor(w_hi[:, slot % SPLIT, :], raw[:, slot, :], vec("one").to_broadcast([P, UNIT]), ALU.mult).then_inc(hi_split, 1)
                pool.wait_ge(hi_split, n + 1)
                pool.tensor_tensor(w_lo[:, slot % SPLIT, :], raw[:, slot, :], w_hi[:, slot % SPLIT, :].bitcast(F32),
                                   ALU.subtract).then_inc(split_ready, 1)

            pool.wait_ge(consts_loaded, 32)
            for s in range(RAW):
                split_unit(s, s, 1, s >= SPLIT)
            with pool.Fori(1, N_UNITS // RAW) as i:
                for s in range(RAW):
                    split_unit(s, i * RAW + s, i + 1, True)
            for n in range(N_UNITS // RAW * RAW, N_UNITS):
                split_unit(n % RAW, n, n // RAW + 1, True)

        @block.tensor
        def _(pe):
            def take_pair(r):
                if not isinstance(r, int) or r >= PAIRS:
                    pe.wait_ge(lin_free, r - (PAIRS - 1))

            def three(outs_, slot, k, moving, start, stop):
                for p, (wt, part) in enumerate(((w_hi, 0), (w_hi, 1), (w_lo, 0))):
                    for o, m in zip(outs_, moving):
                        last = pe.matmul(o, wt[:, slot, k * P:(k + 1) * P], m[part], start=start and p == 0, stop=stop and p == 2,
                                         skip_group_check=True)
                return last

            def moving_of(hi, lo, t):
                if t == T1:
                    return [(hi[:, 0:HALF], lo[:, 0:HALF]), (hi[:, HALF:T1], lo[:, HALF:T1])]
                return [(hi, lo)]

            def out_of(rslot, t):
                return [PS[:, 2 * rslot, 0:HALF], PS[:, 2 * rslot + 1, 0:HALF]] if t == T1 else [PS[:, 2 * rslot, :]]

            def unit(n, slot, r, rslot, t, src, ready=None, chunks=range(KC), first=True, last=True, ends=True):
                pe.wait_ge(split_ready, n + 1)
                if first:
                    take_pair(r)
                chunks = list(chunks)
                for j, k in enumerate(chunks):
                    if ready is not None:
                        pe.wait_ge(ready[0], ready[1] + (j + 1))
                    hi, lo = src(j)
                    mm = three(out_of(rslot, t), slot, k, moving_of(hi, lo, t), first and j == 0, last and j == len(chunks) - 1)
                mm.then_inc(unit_used if ends else lin_done, 1)

            def two_units(n, r, t, src, ready):
                pe.wait_ge(split_ready, n + 2)
                take_pair(r)
                take_pair(r + 1)
                for k in range(KC):
                    pe.wait_ge(ready[0], ready[1] + (k + 1))
                    hi, lo = src(k)
                    for u in range(2):
                        mm = three(out_of((r + u) % PAIRS, t), (n + u) % SPLIT, k, moving_of(hi, lo, t), k == 0, k == KC - 1)
                        if k == KC - 1:
                            mm.then_inc(unit_used, 1)

            def x_of(t):
                return lambda k: (XH[:, k, T1 - t:T1], XL[:, k, T1 - t:T1])

            def turn(r, source, t):
                take_pair(r)
                tiles = token_tiles1() if t == T1 else [(P * i, 0, P * i, P) for i in range(QT)]
                for first, bank, col, rows in tiles:
                    mm = pe.transpose(pair(r)[0:rows, bank, col:col + P], source[:, first:first + rows], ident)
                mm.then_inc(lin_done, 1)

            def token_units(n0, r0, count, t, src, spare0):
                for x, (c, turned_) in enumerate(turning_order(count)):
                    r = r0 + x
                    if turned_:
                        pe.wait_ge(lin_free, r0 + turning_order(count).index((c, False)) + 1)
                        turn(r, spare(spare0 + c, t), t)
                    else:
                        unit(n0 + c, (n0 + c) % SPLIT, r, r % PAIRS, t, src)

            def norm_sum(stage, r, t, chunks=C):
                take_pair(r)
                for c in range(chunks):
                    s = SQ0[stage] + c
                    pe.wait_ge(sq_ready, s + 1)
                    for o, a in ((0, 0), (1, HALF)) if t == T1 else ((0, 0),):
                        w = HALF if t == T1 else T2
                        mm = pe.matmul(pair(r)[:, o, 0:w], const("ones"), SQ[:, s % 2, a:a + w],
                                       start=c == 0, stop=c == chunks - 1, skip_group_check=True)
                    mm.then_inc(sq_used, 1)

            def rotate(e, r, width=T2):
                take_pair(r)
                pe.matmul(pair(r)[:, 0, 0:width], const("rot"), staged(e, width), start=True, stop=True).then_inc(lin_done, 1)

            def rope_chunks(n0, r0, e0, count, src, ready=None):
                for c in range(count + 1):
                    if ready is not None and c < 2:
                        if c == 0:
                            two_units(n0, r0, T2, src, ready)
                    elif c < count:
                        r = r0 + 2 * c - (1 if c else 0)
                        unit(n0 + c, (n0 + c) % SPLIT, r, r % PAIRS, T2, src)
                    if c:
                        before = 2 * (c - 1) - (1 if c > 1 else 0)
                        pe.wait_ge(lin_free, r0 + before + 1)
                        rotate(e0 + before, r0 + 2 * c if c < count else r0 + 2 * count - 1)

            def attention(kind, results):
                body, depth, lag = len(ITEMS[kind]), DEPTH[kind], LAG[kind]
                nsa = kind in ("nsa0", "nsa1")

                def step(i, n):
                    if exists(kind, i, n):
                        a = number(kind, i, n)
                        q = queries(kind, n)
                        k, keys = keys_of(kind, i, n)
                        if n % (body // 2) == 0:
                            pe.wait_ge(q_staged, at(i, 2, 2 * Q0[kind] + 1 + n // (body // 2)))
                        if exists(kind, i, n - depth):
                            pe.wait_ge(p_ready, a + (1 - depth))
                        if kind == "fox" and n % (QT + 1) == QT - 1 and exists(kind, i, n - QT):
                            pe.wait_ge(pt_ready, a + (1 - QT))
                        for c in range(0, keys, 512):
                            w = min(512, keys - c)
                            mm = pe.matmul(scores(kind, n)[:, c:c + w], q, k[:, c:c + w], start=True, stop=kind != "fox",
                                           skip_group_check=kind == "fox")
                            if kind == "fox":
                                mm = pe.matmul(scores(kind, n)[:, c:c + w], ones2[:, :], NF[0:2, at(i, 2, ITEMS[kind][n][0]), c:c + w],
                                               start=False, stop=True, skip_group_check=True)
                        mm.then_inc(s_done, 1)
                    if exists(kind, i, n - lag):
                        a = number(kind, i, n - lag)
                        _, m = home(kind, i, n - lag)
                        pe.wait_ge(p_ready, a + 1)
                        if exists(kind, i, n - lag - 2):
                            pe.wait_ge(pt_ready, a + -1)
                        by = ident
                        if nsa:
                            pe.wait_ge(weigh_ready, number(kind, i, n - lag + 1, 1, W0))
                            by = weights(m)
                        for col, width, dst, _ in key_tiles(kind, m):
                            o = meta_turned(m) if dst is None else turned(m)[0:width, dst:dst + P]
                            e = probs(kind, m)[:, col:col + width]
                            mm = pe.matmul(o, e, by, start=True, stop=True) if nsa else pe.transpose(o, e, by)
                        mm.then_inc(t_done, 1)
                    if exists(kind, i, n - lag - 1) and not (kind == "fox" and home(kind, i, n - lag - 1)[1] % (QT + 1) == 0):
                        a = number(kind, i, n - lag - 1)
                        c, m = home(kind, i, n - lag - 1)
                        pe.wait_ge(pt_ready, a + 1)
                        if nsa and m % 3 == 0 and exists(kind, i, n - lag - 1 - 6):
                            pe.wait_ge(o_ready, at(i, body // 3, O0[kind] + (n - lag - 1) // 3 - 1))
                        if not nsa and exists(kind, i, n - lag - 3):
                            pe.wait_ge(o_ready, number(kind, i, n - lag - 2, 1, O0))

                        def output(m, j, first, last):
                            _, width, src, tile = key_tiles(kind, m)[j]
                            return pe.matmul(outs(kind, m)[:, 0:HD], turned_copy(m, P, src)[0:width, :], values(kind, c, m, width, tile),
                                             start=first, stop=last, skip_group_check=nsa)

                        tiles = len(key_tiles(kind, m))
                        for j in range(tiles):
                            if kind == "fox" and m % (QT + 1) == 1 and j == 1:
                                output(m - 1, 0, True, True).then_inc(o_done, 1)
                            mm = output(m, j, j == 0 and not (nsa and m % 3), j == tiles - 1 and not (nsa and m % 3 < 2))
                        mm.then_inc(o_done, 1)

                pe.wait_ge(lin_free, results)
                for n in range(body):
                    step(0, n)
                with pe.Fori(1, CHUNKS[kind]) as i:
                    for n in range(body):
                        step(i, n)
                for n in range(body, body + lag + 1):
                    step(CHUNKS[kind] - 1, n)
                pe.wait_ge(o_ready, O0[kind] + CHUNKS[kind] * body // (3 if nsa else 1))

            def turn_outputs(r0, count, ot, t):
                for c in range(count):
                    take_pair(r0 + c)
                    if t == T1:
                        pe.transpose(pair(r0 + c)[:, 1, 0:META], ot[0:META, 0, c * P:(c + 1) * P], ident[0:META, 0:META])
                    for i in range(QT):
                        mm = pe.transpose(pair(r0 + c)[:, 0, i * P:(i + 1) * P], ot[:, i + (t == T1), c * P:(c + 1) * P], ident)
                    mm.then_inc(lin_done, 1)

            def residual(name, t, src, ready):
                n0, r0 = U[name], R[name]
                two_units(n0, r0, t, src, ready)
                for c in range(2, C):
                    unit(n0 + c, (n0 + c) % SPLIT, r0 + c, (r0 + c) % PAIRS, t, src)

            def gathered_sum(stage, t):
                take_pair(R[stage])
                for x in range(2):
                    if x == 0:
                        pe.wait_ge(sq_added, ADD0[stage] + C - 2)
                    else:
                        pe.wait_ge(sq_ready, SQ0[stage] + C)
                    for o, a in ((0, 0), (1, HALF)) if t == T1 else ((0, 0),):
                        w = HALF if t == T1 else T2
                        mm = pe.matmul(pair(R[stage])[:, o, 0:w], const("ones"), SQ[:, x, a:a + w],
                                       start=x == 0, stop=x == 1, skip_group_check=True)
                    mm.then_inc(sq_used, 1)

            def hidden_of(part):
                return lambda k: (HIDH[:, (part * KC + k) * SEQ:(part * KC + k + 1) * SEQ],
                                  HIDL[:, (part * KC + k) * SEQ:(part * KC + k + 1) * SEQ])

            def ffn(layer, norm):
                n0, r0 = U[f"ffn{layer}_in"], R[f"ffn{layer}_in"]
                two_units(n0, r0, T2, x_of(T2), (x_ready, X0[norm]))
                for j in range(2, 4):
                    unit(n0 + j, (n0 + j) % SPLIT, r0 + j, (r0 + j) % PAIRS, T2, x_of(T2))
                with pe.Fori(1, FC // 2) as i:
                    for j in range(4):
                        unit(n0 + i * 4 + j, (n0 + j) % SPLIT, r0 + i * 4 + j, (r0 + j) % PAIRS, T2, x_of(T2))
                n0, r0 = U[f"ffn{layer}_out"], R[f"ffn{layer}_out"]
                pe.wait_ge(hid_ready, HID0[f"ffn{layer}"] + FC)
                with pe.Fori(0, 2) as i:
                    for j in range(4):
                        for part in range(3):
                            m = 3 * j + part
                            unit(n0 + i * 12 + m, (n0 + m) % SPLIT, r0 + i * 4 + j, (r0 + j) % PAIRS, T2, hidden_of(part),
                                 chunks=range(min(KC, FC - part * KC)), first=part == 0, last=part == 2)

            pe.wait_ge(consts_loaded, 32)
            norm_sum("n1", R["n1"], T1)
            r = R["in1"]
            two_units(U["pool"], r, T1, x_of(T1), (x_ready, X0["n1"]))
            for n in range(U["bv"], U["v1"]):
                unit(n, n % SPLIT, r + n - U["pool"], (r + n - U["pool"]) % PAIRS, T1, x_of(T1))
            for c in range(2):
                r = R["pool"] + c
                take_pair(r)
                pe.wait_ge(dve_ready, c + 1)
                for o in range(2):
                    mm = pe.matmul(pair(r)[:, o, 0:HALF], const("poolw", P, start=c * P), TS[:, c, o * HALF:(o + 1) * HALF],
                                   start=True, stop=True)
                mm.then_inc(lin_done, 1)
            token_units(U["v1"], R["v1"], 4, T1, x_of(T1), 4)
            take_pair(R["ln"])
            for c in range(2):
                pe.wait_ge(dve_ready, 3 + c)
                for o in range(2):
                    mm = pe.matmul(pair(R["ln"])[:, o, 0:HALF], const("ones"), sig[:, c, o * HALF:(o + 1) * HALF],
                                   start=c == 0, stop=c == 1, skip_group_check=True)
            mm.then_inc(lin_done, 1)
            unit(U["k1"], U["k1"] % SPLIT, R["k1a"], R["k1a"] % PAIRS, T1, x_of(T1))
            norm_sum("ln", R["lnv"], T1, chunks=2)
            for c in range(1, 4):
                n, r = U["k1"] + c, R["k1b"] + c - 1
                unit(n, n % SPLIT, r, r % PAIRS, T1, x_of(T1))
            pe.wait_ge(rows_moved, 32)
            pe.wait_ge(dve_ready, 6)
            attention("fox", R["ot1"])
            turn_outputs(R["ot1"], 4, OT1, T1)
            with pe.Fori(0, 4) as i:
                for m in range(2):
                    n, r = U["merge"] + 4 * m, R["merge"] + 6 * m
                    for g in range(3):
                        unit(n + i * 8 + g, (n + g) % SPLIT, r + i * 12 + g, (r + g) % PAIRS, T1, x_of(T1))
                    pe.wait_ge(hid_ready, HID0["merge"])
                    pe.wait_ge(ev_used, E0["merge"])
                    for b, (k0, k1) in enumerate(((0, 2), (2, 4), (4, 8))):
                        unit(n + i * 8 + 3, (n + 3) % SPLIT, r + i * 12 + 3 + b, (r + 3 + b) % PAIRS, T1,
                             lambda k: (o_hi(k0 + k, T1), o_lo(k0 + k, T1)), chunks=range(k0, k1), ends=b == 2)
            residual("wo1", T1, lambda k: (m_hi(k, T1), m_lo(k, T1)), (hid_ready, HID0["merge"]))
            gathered_sum("n2", T1)
            two_units(U["router"], R["router"], T1, x_of(T1), (x_ready, X0["n2"]))
            pe.wait_ge(lin_free, R["router"] + 1)
            turn(R["routerT"], spare(0, T1), T1)
            for j in range(1, HEAD):
                n, r = U["moe"] + j, R["moe_b"] + j - 1
                unit(n, n % SPLIT, r, r % PAIRS, T1, x_of(T1))
            take_pair(R["combT"])
            pe.wait_ge(dve_ready, 7)
            for i, (first, bank, col, rows) in enumerate(token_tiles1()):
                mm = pe.transpose(pair(R["combT"])[0:N_EXP, bank, col:col + rows], route[0:rows, 11, i, :], ident[0:rows, 0:rows])
            mm.then_inc(lin_done, 1)
            pe.wait_ge(lin_free, R["combT"] + 1)
            for e in range(N_EXP):
                r = R["cb"] + e
                take_pair(r)
                for o in range(2):
                    mm = pe.matmul(pair(r)[:, o, 0:HALF], ident[0:N_EXP, e:e + 1].to_broadcast([N_EXP, P]),
                                   SQ[0:N_EXP, 0, o * HALF:(o + 1) * HALF], start=True, stop=True)
                mm.then_inc(lin_done, 1)
            def group_units(i, first):
                n, r = U["moe"], R["moe"] - HEAD
                for j in range(first, 16):
                    unit(n + i * 24 + j, (n + j) % SPLIT, r + i * 24 + j, (r + j) % PAIRS, T1, x_of(T1))
                for j in range(16, 24):
                    unit(n + i * 24 + j, (n + j) % SPLIT, r + i * 24 + j, (r + j) % PAIRS, T1,
                         lambda k: (o_hi(k, T1), o_lo(k, T1)), ready=(hid_ready, i * C + HID0["moe"]) if j == 16 else None)

            group_units(0, HEAD)
            with pe.Fori(1, N_GRP) as i:
                group_units(i, 0)
            norm_sum("nf1", R["nf1"], T1)
            norm_sum("na0", R["na0"], T2)
            r = R["kcvc"]
            two_units(U["kc"], r, T2, x_of(T2), (x_ready, X0["na0"]))
            for n in range(U["vc"], U["gl"]):
                unit(n, n % SPLIT, r + n - U["kc"], (r + n - U["kc"]) % PAIRS, T2, x_of(T2))
            token_units(U["gl"], R["tok2"], 5, T2, x_of(T2), 0)
            for kv in range(2):
                pe.wait_ge(dve_ready, 8 + kv)
                r = R["cmp"] + 3 * kv
                for m in range(2):
                    take_pair(r + m)
                    for part in range(2):
                        n = U["cmp"] + 4 * kv + 2 * m + part
                        pe.wait_ge(split_ready, n + 1)
                        for k in range(KC):
                            b = part * KC + k
                            mm = three([pair(r + m)[:, 0, 0:A_G * NC]], n % SPLIT, k, [(BLKH[:, b, :], BLKL[:, b, :])],
                                       part == 0 and k == 0, part == 1 and k == KC - 1)
                        mm.then_inc(unit_used, 1)
                take_pair(r + 2)
                pe.wait_ge(lin_free, r + 2)
                if kv == 0:
                    for gp in range(2):
                        for odd in range(2):
                            g = 2 * gp + odd
                            for j in range(2):
                                mm = pe.matmul(pair(r + 2)[:, 0, gp * NC:(gp + 1) * NC], const("w2k", P, start=(2 * j + odd) * P),
                                               HIDC[:, j, g * NC:(g + 1) * NC], start=odd == 0 and j == 0, stop=odd == 1 and j == 1)
                else:
                    for g in range(A_G):
                        for j in range(2):
                            mm = pe.matmul(pair(r + 2)[0:NC, 0, g * HD:(g + 1) * HD], HIDC[:, j, g * NC:(g + 1) * NC],
                                           const("w2v", HD, start=j * HD), start=j == 0, stop=j == 1)
                mm.then_inc(lin_done, 1)
            rotate(E0["cmp"], R["cmp"] + 6, 2 * NC)
            rope_chunks(U["ks"], R["rope2"], E0["rope2"], 12, x_of(T2))
            pe.wait_ge(rope_ready, ROPE0["k3"])
            attention("nsa0", R["ot2"])
            attention("nsa1", R["ot2"])
            turn_outputs(R["ot2"], C, OT2, T2)
            residual("wo2", T2, lambda k: (o_hi(k, T2), o_lo(k, T2)), (ev_used, E0["ot2"]))
            gathered_sum("nf0", T2)
            ffn(0, "nf0")
            gathered_sum("na1", T2)
            kv_of = lambda k: (o_hi(k, T2), o_lo(k, T2))
            r = R["kv3"]
            two_units(U["k3"], r, T2, kv_of, (x_ready, X0["kv"]))
            pe.wait_ge(lin_free, r + 1)
            rotate(E0["k3"], r + 2)
            pe.wait_ge(lin_free, r + 2)
            turn(r + 3, Q3[:, 7, :], T2)
            rope_chunks(U["q3"], R["q3"], E0["q3"], 8, x_of(T2), (x_ready, X0["na1"]))
            pe.wait_ge(rope_ready, ROPE0["k3"] + 9)
            attention("swa", R["ot3"])
            turn_outputs(R["ot3"], C, OT3, T2)
            residual("wo3", T2, lambda k: (o_hi(k, T2), o_lo(k, T2)), (ev_used, E0["ot3"]))
            gathered_sum("nf_1", T2)
            ffn(1, "nf_1")
            gathered_sum("nfin", T2)

        @block.scalar
        def _(act):
            def by_unit(n):
                act.wait_ge(unit_used, n + 1)

            def alone(l):
                act.wait_ge(lin_done, l + 1)

            def result(rslot, t):
                return PS[:, 2 * rslot:2 * rslot + 2, 0:HALF] if t == T1 else PS[:, 2 * rslot, :]

            def shaped(ap, t):
                return halves(ap) if t == T1 else ap

            def evacuate(rslot, dst, t, func=ACT.Copy, **more):
                act.activation(shaped(dst, t), result(rslot, t), func, **more).then_inc(lin_free, 1)

            def stage(rslot, e, eslot, t, func=ACT.Copy, back=EV_SLOTS - 1, **more):
                if not isinstance(e, int) or e - back > 0:
                    act.wait_ge(ev_used, e - back)
                evacuate(rslot, EV[:, eslot, 2:2 + t], t, func, **more)

            def squares(stage_, src, ready, count=C):
                for c in range(count):
                    s = SQ0[stage_] + c
                    if ready is not None:
                        act.wait_ge(ready[0], ready[1] + c + 1)
                    if s >= 2:
                        act.wait_ge(sq_used, S0[stage_] + c - 1)
                    ap = src(c)
                    act.activation(SQ[:, s % 2, 0:ap.shape[1]], ap, ACT.Square).then_inc(sq_ready, 1)

            def root_table():
                act.activation(one_root[:, :], vec("one"), ACT.Sqrt)

            def exp_table():
                act.activation(one_exp[:, :], vec("one"), ACT.Exp)

            def root(stage_, r, t, width):
                act.wait_ge(sq_used, S0[stage_] + SUMS[stage_])
                act.activation(shaped(TS[:, 2, 0:t], t), result(r % PAIRS, t), ACT.Sqrt, bias=vec("eps"), scale=1.0 / width)\
                   .then_inc(lin_free, 1)

            def high_parts(count0, t, hi):
                for c in range(C):
                    act.wait_ge(y_ready, count0 + c + 1)
                    act.activation(hi(c), TS[:, c % 2, 0:t], ACT.Copy).then_inc(hi_ready, 1)

            def x_hi(t):
                return lambda c: XH[:, c, T1 - t:T1]

            def token_results(n0, r0, l0, count, t, spare0, keep):
                for x, (c, turned_) in enumerate(turning_order(count)):
                    if turned_:
                        alone(l0 + c)
                        keep(c, pair(r0 + x))
                    else:
                        by_unit(n0 + c)
                        evacuate((r0 + x) % PAIRS, spare(spare0 + c, t), t)

            def h_of(t):
                return lambda c: H[:, c, T1 - t:T1]

            def stage_queries(kind, i, half):
                body = len(ITEMS[kind])
                if exists(kind, i, -1) or kind == "nsa1":
                    act.wait_ge(s_done, number(kind, i, half * body // 2 - body // 2))
                q = chunk_queries(kind, i)
                rows = slice(half * HD, (half + 1) * HD)
                act.activation(QSTAGE[rows, half, 0:q.shape[-1]], q[rows, :], ACT.Copy).then_inc(q_staged, 1)

            def attention(kind, following=None):
                body, depth, lag = len(ITEMS[kind]), DEPTH[kind], LAG[kind]
                extra = 1 if kind == "swa" else 0

                last = CHUNKS[kind] - 1

                def step(i, n):
                    if n == body // 2 - 2:
                        stage_queries(kind, i, 1)
                    if n == body // 2 + 1 and not (isinstance(i, int) and i == last):
                        stage_queries(kind, i + 1, 0)
                    if n == body // 2 + 1 and isinstance(i, int) and i == last and following:
                        stage_queries(following, 0, 0)
                    if exists(kind, i, n - 1):
                        a = number(kind, i, n - 1)
                        c, m = home(kind, i, n - 1)
                        keys = keys_of(kind, c, m)[1]
                        act.wait_ge(max_ready, a + 1)
                        if exists(kind, i, n - 1 - depth):
                            act.wait_ge(t_done, a + (1 - depth))
                        act.activation(probs(kind, m)[:, 0:keys + extra], scores(kind, m)[:, 0:keys + extra], ACT.Exp,
                                       bias=stat[:, 0, m:m + 1], accum_out=stat[:, 1, m:m + 1]).then_inc(p_ready, 1)
                    if exists(kind, i, n - lag):
                        a = number(kind, i, n - lag)
                        _, m = home(kind, i, n - lag)
                        act.wait_ge(t_done, a + 1)
                        if exists(kind, i, n - lag - 2):
                            act.wait_ge(o_done, a + -1)
                        tiles = key_tiles(kind, m)
                        if tiles[-1][2] is None:
                            cp = act.activation(turned_copy(m, P, None)[0:META, :], meta_turned(m), ACT.Copy)
                            tiles = tiles[:-1]
                        if tiles:
                            height, wide = tiles[0][1], len(tiles) * P
                            cp = act.activation(turned_copy(m, wide, 0)[0:height, :], turned(m)[0:height, 0:wide], ACT.Copy)
                        cp.then_inc(pt_ready, 1)

                for n in range(body):
                    step(0, n)
                with act.Fori(1, last) as i:
                    for n in range(body):
                        step(i, n)
                for n in range(body + lag + 1):
                    step(last, n)

            def turned_outputs(stage_, count, t):
                for c in range(count):
                    r, e = R[stage_] + c, E0[stage_] + c
                    alone(L0[stage_] + c)
                    if e >= EV_SLOTS:
                        act.wait_ge(ev_used, e - (EV_SLOTS - 1))
                    if t == T1:
                        act.activation(staged(e, META), pair(r)[:, 1, 0:META], ACT.Copy)
                    act.activation(staged(e, T2, 2 + t - T2), pair(r)[:, 0, :], ACT.Copy).then_inc(lin_free, 1)

            def residual(name, t, norm, units=1):
                root_table()
                for c in range(C):
                    by_unit(U[name] + units * c + units - 1)
                    stage((R[name] + c) % PAIRS, E0[name] + c, (E0[name] + c) % EV_SLOTS, t)
                    act.wait_ge(ev_used, E0[name] + c + 1)
                    if c >= 2:
                        act.wait_ge(sq_added, ADD0[norm] + c - 1)
                    act.activation(SQ[:, min(c, 1), 0:t], H[:, c, T1 - t:T1], ACT.Square).then_inc(sq_ready, 1)

            def ffn(layer):
                n0, r0, e0 = U[f"ffn{layer}_in"], R[f"ffn{layer}_in"], E0[f"ffn{layer}_in"]
                with act.Fori(0, FC // 2) as i:
                    for j in range(2):
                        for m in (2 * j, 2 * j + 1):
                            by_unit(n0 + i * 4 + m)
                            stage((r0 + m) % PAIRS, e0 + i * 4 + m, (e0 + m) % EV_SLOTS, T2)
                        act.wait_ge(ev_used, e0 + i * 4 + 2 * j + 1)
                        act.activation(SQ[:, j, 0:T2], SQ[:, j, 0:T2], ACT.Silu).then_inc(act_done, 1)
                residual(f"ffn{layer}_out", T2, ("na1", "nfin")[layer], 3)

            def rope_results(name, n0, count, scale_from):
                r0, e0 = R[name], E0[name]
                order = [(0, False)]
                for c in range(1, count):
                    order += [(c, False), (c - 1, True)]
                order.append((count - 1, True))
                for n, (c, turned_) in enumerate(order):
                    if turned_:
                        alone(L0[name] + c)
                        stage((r0 + n) % PAIRS, e0 + n, (e0 + n) % EV_SLOTS, T2, back=3 if c < count - 1 else 2)
                    else:
                        by_unit(n0 + c)
                        stage((r0 + n) % PAIRS, e0 + n, (e0 + n) % EV_SLOTS, T2, back=1 if n else 0,
                              scale=SCALE if c >= scale_from else 1.0)

            act.wait_ge(consts_loaded, 32)
            act.wait_ge(pads_zeroed, 7)
            root_table()
            for c in range(C):
                act.wait_ge(x_loaded[c // 2], 16)
                if c >= 2:
                    act.wait_ge(sq_used, c - 1)
                act.activation(SQ[:, c % 2, :], H[:, c, :], ACT.Square).then_inc(sq_ready, 1)
            root("n1", R["n1"], T1, D)
            high_parts(X0["n1"], T1, x_hi(T1))
            r, n = R["in1"], U["pool"]
            for c in range(6):
                by_unit(n + c)
                if c < 2:
                    evacuate((r + c) % PAIRS, apad[:, c, 16:16 + T1], T1)
                elif c < 4:
                    evacuate((r + c) % PAIRS, glu[:, c - 2, KS - 1:KS - 1 + T1], T1)
                else:
                    evacuate((r + c) % PAIRS, sig[:, c - 4, :], T1, ACT.Sigmoid)
            by_unit(U["fg"])
            act.activation(halves(staged(0, T1)[0:FOX_H, :]), pair(r + 6)[0:FOX_H, :, 0:HALF], ACT.Identity,
                           bias=vec("bforget")[0:FOX_H, :]).then_inc(lin_free, 1)
            act.wait_ge(lin_free, r + 7)
            act.activation(staged(1, T1)[0:FOX_H, :], staged(0, T1)[0:FOX_H, :], ACT.Abs).then_inc(act_step, 1)
            act.wait_ge(act_step, 1)
            act.activation(staged(3, T1)[0:FOX_H, :], staged(1, T1)[0:FOX_H, :], ACT.Exp, scale=-1.0).then_inc(act_step, 1)
            act.wait_ge(act_step, 2)
            act.activation(staged(1, T1)[0:FOX_H, :], staged(3, T1)[0:FOX_H, :], ACT.Ln, bias=vec("one")[0:FOX_H, :])\
               .then_inc(act_done, 1)
            for c in range(4):
                by_unit(U["q1"] + c)
                evacuate((r + 7 + c) % PAIRS, Q1[:, c, :], T1, scale=SCALE)
            for c in range(2):
                alone(L0["pool"] + c)
                evacuate((R["pool"] + c) % PAIRS, apad[:, c, 16:16 + T1], T1, ACT.Identity, bias=vec("pool_b", c))

            def keep_v1(c, ps):
                act.activation(V1[0:META, 0, c * P:(c + 1) * P], ps[0:META, 1, 0:P], ACT.Copy)
                act.activation(V1[:, 1:QT + 1, c * P:(c + 1) * P], ps[:, 0, :].rearrange("p (i n) -> p i n", i=QT), ACT.Copy)\
                   .then_inc(lin_free, 1)

            token_results(U["v1"], R["v1"], L0["v1"], 4, T1, 4, keep_v1)
            alone(L0["ln"])
            evacuate(R["ln"] % PAIRS, TS[:, 2, :], T1, scale=-1.0 / CONV_W)
            squares("ln", lambda c: sig[:, c, :], (act_asked, 0), 2)
            by_unit(U["k1"])
            evacuate(R["k1a"] % PAIRS, K1[:, 0, :], T1)
            root("ln", R["lnv"], T1, CONV_W)
            by_unit(U["k1"] + 1)
            evacuate(R["k1b"] % PAIRS, K1[:, 1, :], T1)
            for c in range(2):
                act.wait_ge(act_asked, 3 + c)
                act.activation(sig[:, c, :], sig[:, c, :], ACT.Silu, bias=vec("ln_b", c)).then_inc(act_done, 1)
            act.wait_ge(hid_ready, HID0["merge"])
            act.wait_ge(dve_ready, 5)
            for part in range(2):
                act.dma_start(NF[part:part + 1, :, :].bitcast(F32), staged(part, T1)[0:FOX_H, :]).then_inc(rows_moved, 16)
            exp_table()
            act.wait_ge(zeros_written, 2)
            stage_queries("fox", 0, 0)
            for c in range(2, 4):
                by_unit(U["k1"] + c)
                evacuate((R["k1b"] + c - 1) % PAIRS, K1[:, c, :], T1)
            attention("fox")
            turned_outputs("ot1", 4, T1)
            with act.Fori(0, 4) as i:
                n, r, e = U["merge"], R["merge"], E0["merge"]
                for j in range(12):
                    m, k = j // 6, j % 6
                    if k in (3, 4):
                        alone(L0["merge"] + i * 4 + 2 * m + k - 3)
                    else:
                        by_unit(n + i * 8 + 4 * m + min(k, 3))
                    stage((r + j) % PAIRS, e + i * 12 + j, (e + j) % EV_SLOTS, T1, ACT.Sigmoid if k < 3 else ACT.Copy)
            residual("wo1", T1, "n2")
            root("n2", R["n2"], T1, D)
            high_parts(X0["n2"], T1, x_hi(T1))
            by_unit(U["router"])
            evacuate(R["router"] % PAIRS, spare(0, T1), T1)

            def stage_expert(i, j, rslot):
                by_unit(U["moe"] + i * 24 + j)
                e = E0["moe"]
                stage(rslot, e + i * 24 + j, (e + j) % EV_SLOTS, T1, ACT.Silu if j < 16 and j % 2 == 0 else ACT.Copy)

            stage_expert(0, 0, R["moe_a"] % PAIRS)
            alone(L0["routerT"])
            r = R["routerT"]
            for slot, a, w in ((0, 0, N_GRP), (1, N_GRP, N_EXP)):
                act.activation(route[0:META, slot, 0, 0:w], pair(r)[0:META, 1, a:a + w], ACT.Copy)
                cp = act.activation(route[:, slot, 1:QT + 1, 0:w],
                                    pair(r)[:, 0, :].rearrange("p (i n) -> p i n", i=QT)[:, :, a:a + w], ACT.Copy)
            cp.then_inc(lin_free, 1)
            stage_expert(0, 1, R["moe_b"] % PAIRS)
            act.wait_ge(act_asked, 5)
            act.activation(route[:, 4, :, 0:8], route[:, 3, :, 0:8], ACT.Exp).then_inc(act_done, 1)
            for j in range(2, HEAD):
                stage_expert(0, j, (R["moe_b"] + j - 1) % PAIRS)
            r = R["combT"]
            alone(L0["combT"])
            act.activation(SQ[0:N_EXP, 0, 0:META], pair(r)[0:N_EXP, 1, 0:META], ACT.Copy)
            act.activation(SQ[0:N_EXP, 0, META:T1], pair(r)[0:N_EXP, 0, :], ACT.Copy).then_inc(lin_free, 1)
            for e in range(N_EXP):
                alone(L0["cb"] + e)
                evacuate((R["cb"] + e) % PAIRS, CB[:, e, :], T1)
            for j in range(HEAD, 24):
                stage_expert(0, j, (R["moe"] - HEAD + j) % PAIRS)
            with act.Fori(1, N_GRP) as i:
                for j in range(24):
                    stage_expert(i, j, (R["moe"] - HEAD + j) % PAIRS)
            root_table()
            squares("nf1", h_of(T1), (ev_used, E0["moe"] + 3 * 24 + 16))
            root("nf1", R["nf1"], T1, D)
            squares("na0", h_of(T2), (h_ready, 0))
            root("na0", R["na0"], T2, D)
            high_parts(X0["na0"], T2, x_hi(T2))
            for c in range(4):
                r = R["kcvc"] + c
                by_unit(U["kc"] + c)
                act.activation(EO[:, c, :, :], pair(r)[:, 0, :].rearrange("p (n a) -> p a n", a=2), ACT.Copy).then_inc(lin_free, 1)
            act.wait_ge(lin_free, R["kcvc"] + 4)
            for par in range(2):
                for g2 in range(2):
                    act.dma_start(PAIR[par * HD:(par + 1) * HD, :, g2, :], EO[g2 * HD:(g2 + 1) * HD, :, par, :])\
                       .then_inc(pairs_moved, 16)

            def keep_tok2(c, ps):
                tiles = ps[:, 0, :].rearrange("p (i n) -> p i n", i=QT)
                if c == 0:
                    act.activation(gate48[:, :, :], tiles[:, :, 0:3 * NH], ACT.Sigmoid).then_inc(lin_free, 1)
                else:
                    v, half = (VSEL, VWIN)[(c - 1) // 2], (c - 1) % 2
                    act.activation(v[:, :, half * P:(half + 1) * P], tiles, ACT.Copy).then_inc(lin_free, 1)

            token_results(U["gl"], R["tok2"], L0["tok2"], 5, T2, 0, keep_tok2)
            for kv in range(2):
                r = R["cmp"] + 3 * kv
                for m in range(2):
                    by_unit(U["cmp"] + 4 * kv + 2 * m + 1)
                    act.activation(HIDC[:, m, :], pair(r + m)[:, 0, 0:A_G * NC], ACT.Gelu_apprx_tanh).then_inc(lin_free, 1)
                alone(L0["cmp"] + kv)
                if kv == 0:
                    act.wait_ge(ev_used, E0["cmp"])
                    act.activation(staged(E0["cmp"], 2 * NC), pair(r + 2)[:, 0, 0:2 * NC], ACT.Copy).then_inc(lin_free, 1)
                else:
                    act.activation(VCMP[0:NC, :, :], pair(r + 2)[0:NC, 0, 0:A_G * HD].rearrange("p (g d) -> p g d", g=A_G), ACT.Copy)\
                       .then_inc(lin_free, 1)
            alone(L0["cmp"] + 2)
            act.activation(staged(E0["cmp"] + 1, 2 * NC), pair(R["cmp"] + 6)[:, 0, 0:2 * NC], ACT.Copy).then_inc(lin_free, 1)
            rope_results("rope2", U["ks"], 12, 4)
            exp_table()
            act.wait_ge(zeros_written, 4)
            act.wait_ge(rope_ready, ROPE0["k3"])
            stage_queries("nsa0", 0, 0)
            attention("nsa0", "nsa1")
            attention("nsa1")
            turned_outputs("ot2", C, T2)
            residual("wo2", T2, "nf0")
            root("nf0", R["nf0"], T2, D)
            high_parts(X0["nf0"], T2, x_hi(T2))
            ffn(0)
            root("na1", R["na1"], T2, D)
            high_parts(X0["kv"], T2, lambda c: o_hi(c, T2))
            high_parts(X0["na1"], T2, x_hi(T2))
            r, e = R["kv3"], E0["k3"]
            by_unit(U["k3"])
            stage(r % PAIRS, e, e % EV_SLOTS, T2, back=0)
            by_unit(U["v3"])
            evacuate((r + 1) % PAIRS, Q3[:, 7, :], T2)
            alone(L0["k3"])
            stage((r + 2) % PAIRS, e + 1, (e + 1) % EV_SLOTS, T2, back=1)
            alone(L0["v3"])
            act.activation(V3[:, :, :], pair(r + 3)[:, 0, :].rearrange("p (i n) -> p i n", i=QT), ACT.Copy).then_inc(lin_free, 1)
            rope_results("q3", U["q3"], 8, 0)
            exp_table()
            act.wait_ge(zeros_written, 6)
            act.wait_ge(rope_ready, ROPE0["q3"] + 8)
            stage_queries("swa", 0, 0)
            attention("swa")
            turned_outputs("ot3", C, T2)
            residual("wo3", T2, "nf_1")
            root("nf_1", R["nf_1"], T2, D)
            high_parts(X0["nf_1"], T2, x_hi(T2))
            ffn(1)
            root("nfin", R["nfin"], T2, D)

        @block.vector
        def _(dve):
            steps = [0]

            def then(ins):
                steps[0] = steps[0] + 1
                ins.then_inc(dve_step, 1)
                dve.wait_ge(dve_step, steps[0])

            def parts(src, hi, lo):
                then(dve.tensor_copy(hi, src))
                return dve.tensor_tensor(lo, src, hi.bitcast(F32), ALU.subtract)

            def reciprocal_root(r, t):
                dve.wait_ge(lin_free, r + 1)
                then(dve.reciprocal(TS[:, 2, 0:t], TS[:, 2, 0:t]))

            def normed(gain, count0, t, hi, lo, used):
                if used:
                    dve.wait_ge(unit_used, used)
                for c in range(C + 1):
                    if c < C:
                        if count0 + c >= 2:
                            dve.wait_ge(x_ready, count0 + c - 1)
                        dve.scalar_tensor_tensor(out=TS[:, c % 2, 0:t], in0=H[:, c, T1 - t:T1], scalar=vec(gain, c), in1=TS[:, 2, 0:t],
                                                 op0=ALU.mult, op1=ALU.mult).then_inc(y_ready, 1)
                    if c:
                        dve.wait_ge(hi_ready, count0 + c)
                        dve.tensor_tensor(lo(c - 1), TS[:, (c - 1) % 2, 0:t], hi(c - 1).bitcast(F32), ALU.subtract).then_inc(x_ready, 1)

            def normed_in_place(gain, root_):
                for c in range(C):
                    dve.scalar_tensor_tensor(out=H[:, c, META:T1], in0=H[:, c, META:T1], scalar=vec(gain, c), in1=root_,
                                             op0=ALU.mult, op1=ALU.mult).then_inc(h_ready, 1)

            def x_hi(t):
                return lambda c: XH[:, c, T1 - t:T1]

            def x_lo(t):
                return lambda c: XL[:, c, T1 - t:T1]

            def residual(name, t, norm):
                def add_squares(c):
                    dve.wait_ge(sq_ready, SQ0[norm] + c + 1)
                    if c > 1:
                        dve.wait_ge(sq_added, ADD0[norm] + c - 1)
                    dve.tensor_tensor(SQ[:, 0, 0:t], SQ[:, 0, 0:t], SQ[:, 1, 0:t], ALU.add).then_inc(sq_added, 1)

                for c in range(C):
                    dve.wait_ge(lin_free, R[name] + c + 1)
                    h = H[:, c, T1 - t:T1]
                    dve.tensor_tensor(h, h, staged(E0[name] + c, t), ALU.add).then_inc(ev_used, 1)
                    if c >= 2:
                        add_squares(c - 1)

            def attention(kind):
                body, lag = len(ITEMS[kind]), LAG[kind]
                nsa = kind in ("nsa0", "nsa1")

                def step(i, n):
                    if exists(kind, i, n - lag - 3):
                        a = number(kind, i, n - lag - 3)
                        c, m = home(kind, i, n - lag - 3)
                        half, t = ITEMS[kind][m][0:2]
                        rows = META if kind == "fox" and t == 0 else P
                        o = outs(kind, m)[0:rows, 0:HD]
                        if nsa and m % 3 == 2:
                            dve.wait_ge(o_done, a + 1)
                            g = 2 * int(kind[3]) + half
                            dve.tensor_scalar(OT2[:, t, bass.ds(at(c, HD, g * 4 * HD), HD)], o, vec("one"), None, ALU.mult).then_inc(o_ready, 1)
                        if not nsa:
                            dve.wait_ge(o_done, a + 1)
                            dve.wait_ge(sum_inverted, a + 1)
                            ot, stride, base = (OT1, P, half * HD) if kind == "fox" else (OT3, HD, half * 8 * HD)
                            dve.tensor_scalar(ot[0:rows, t, bass.ds(at(c, stride, base), HD)], o, stat[0:rows, 2, m:m + 1], None, ALU.mult)\
                               .then_inc(o_ready, 1)
                    if exists(kind, i, n):
                        a = number(kind, i, n)
                        half, t = ITEMS[kind][n][0:2]
                        keys = keys_of(kind, i, n)[1]
                        s = scores(kind, n)
                        width = META if kind == "fox" and t == 0 else P
                        own = s[:, keys - width:keys]
                        dve.wait_ge(s_done, a + 1)
                        if kind == "fox":
                            dve.tensor_tensor(own, own, const("causal", width), ALU.add).then_inc(masked, 1)
                        elif kind == "swa":
                            dve.tensor_tensor(s[:, 0:keys], s[:, 0:keys], const("causal") if t == 0 else const("band"), ALU.add)\
                               .then_inc(masked, 1)
                            dve.tensor_copy(s[:, keys:keys + 1], vecs[:, bass.ds(at(i, 1, V0["sink"] + half * 8), 1)]).then_inc(masked, 1)
                        elif ITEMS[kind][n][2] == 0:
                            dve.tensor_tensor(s[:, 0:NC], s[:, 0:NC], const("cmask", NC, start=t * NC), ALU.add).then_inc(masked, 1)
                        else:
                            dve.tensor_tensor(own, own, const("causal"), ALU.add).then_inc(masked, 1)
                    if exists(kind, i, n - 2):
                        a = number(kind, i, n - 2)
                        c, m = home(kind, i, n - 2)
                        dve.wait_ge(p_ready, a + 1)
                        dve.reciprocal(stat[:, 2, m:m + 1], stat[:, 1, m:m + 1]).then_inc(sum_inverted, 1)
                    if exists(kind, i, n):
                        per = MASKS[kind]
                        dve.wait_ge(masked, number(kind, i, n, per, M0) + per)
                        seen = keys + (kind == "swa")
                        dve.tensor_reduce(stat[:, 0, n:n + 1], s[:, 0:seen], AX, ALU.max, negate=True).then_inc(max_ready, 1)
                    if nsa and exists(kind, i, n - 2):
                        a = number(kind, i, n - 2)
                        c, m = home(kind, i, n - 2)
                        half, t, b = ITEMS[kind][m]
                        dve.wait_ge(sum_inverted, a + 1)
                        if exists(kind, i, n - 2 - 4):
                            dve.wait_ge(t_done, a + -3)
                        gate = gate48[:, t, bass.ds(at(c, 3, (2 * int(kind[3]) + half) * 12 + b), 1)]
                        dve.tensor_scalar(weights(m), ident, stat[:, 2, m:m + 1], gate, ALU.mult, ALU.mult).then_inc(weigh_ready, 1)

                for n in range(body):
                    step(0, n)
                with dve.Fori(1, CHUNKS[kind]) as i:
                    for n in range(body):
                        step(i, n)
                for n in range(body, body + lag + 3):
                    step(CHUNKS[kind] - 1, n)

            def zero_other_heads():
                dve.memset(QSTAGE[HD:P, 0, :], 0.0).then_inc(zeros_written, 1)
                dve.memset(QSTAGE[0:HD, 1, :], 0.0).then_inc(zeros_written, 1)

            def feature_parts(stage_, count, t, first):
                for c in range(count):
                    dve.wait_ge(lin_free, R[stage_] + c + 1)
                    parts(staged(E0[stage_] + c, t), o_hi(first + c, t), o_lo(first + c, t)).then_inc(ev_used, 1)

            def rotated(stage_, count, dest):
                r0, e0 = R[stage_], E0[stage_]
                for c in range(count):
                    at = 2 * c - (1 if c else 0)
                    rot = 2 * c + 2 if c < count - 1 else 2 * count - 1
                    dve.wait_ge(lin_free, r0 + rot + 1)
                    if ROPE0[stage_] + c:
                        dve.wait_ge(rope_ready, ROPE0[stage_] + c)
                    dve.tensor_tensor(TS[:, 0, 0:T2], staged(e0 + at, T2), const("cosq"), ALU.mult).then_inc(ev_used, 1)
                    dve.tensor_tensor(TS[:, 1, 0:T2], staged(e0 + rot, T2), const("sinq"), ALU.mult).then_inc(ev_used, 1)
                    dve.wait_ge(ev_used, e0 + 2 * c + 2)
                    dve.tensor_tensor(dest(c), TS[:, 0, 0:T2], TS[:, 1, 0:T2], ALU.add).then_inc(rope_ready, 1)

            def ffn(layer):
                r0, e0 = R[f"ffn{layer}_in"], E0[f"ffn{layer}_in"]
                w0 = V0[f"fw{layer}"]
                before, per = steps[0], 2 * 6
                with dve.Fori(0, FC // 2) as i:
                    steps[0] = i * per + before
                    for j in range(2):
                        for m in (2 * j, 2 * j + 1):
                            slot = (e0 + m) % EV_SLOTS
                            w = [vecs[:, bass.ds(i * 16 + (w0 + 4 * m + q), 1)] for q in range(4)]
                            y = SQ[:, j, 0:T2] if m == 2 * j else TS[:, j, 0:T2]
                            dve.wait_ge(lin_free, r0 + i * 4 + m + 1)
                            then(dve.tensor_scalar(y, EV[:, slot, 2:2 + T2], w[2], w[3], ALU.mult, ALU.add))
                            then(dve.scalar_tensor_tensor(out=y, in0=EV[:, slot, 1:1 + T2], scalar=w[1], in1=y, op0=ALU.mult, op1=ALU.add))
                            dve.scalar_tensor_tensor(out=y, in0=EV[:, slot, 0:T2], scalar=w[0], in1=y, op0=ALU.mult, op1=ALU.add)\
                               .then_inc(ev_used, 1)
                        dve.wait_ge(act_done, DONE0[f"ffn{layer}"] + i * 2 + j + 1)
                        dve.wait_ge(ev_used, e0 + i * 4 + 2 * j + 2)
                        y = TS[:, j, 0:T2]
                        then(dve.tensor_tensor(y, y, SQ[:, j, 0:T2], ALU.mult))
                        parts(y, HIDH[:, bass.ds(i * (2 * SEQ) + j * SEQ, SEQ)], HIDL[:, bass.ds(i * (2 * SEQ) + j * SEQ, SEQ)])\
                            .then_inc(hid_ready, 1)
                steps[0] = before + per * (FC // 2)
                residual(f"ffn{layer}_out", T2, ("na1", "nfin")[layer])

            dve.wait_ge(consts_loaded, 32)
            for loaded in x_loaded:
                dve.wait_ge(loaded, 16)
            dve.wait_ge(pads_zeroed, 7)
            reciprocal_root(R["n1"], T1)
            normed("norm1", X0["n1"], T1, x_hi(T1), x_lo(T1), 0)
            a, b = 16, 16 + T1
            dve.wait_ge(inv_loaded, 16)
            dve.wait_ge(lin_free, R["in1"] + 2)
            then(dve.tensor_tensor(sum2[:, :, a:b], apad[:, :, a:b], apad[:, :, a - 1:b - 1], ALU.add))
            then(dve.tensor_tensor(sum4[:, :, a:b], sum2[:, :, a:b], sum2[:, :, a - 2:b - 2], ALU.add))
            then(dve.tensor_tensor(sum8[:, a:b], sum4[:, 1, a:b], sum4[:, 1, a - 4:b - 4], ALU.add))
            then(dve.tensor_tensor(sum2[:, 1, a:b], sum8[:, a:b], sum8[:, a - 8:b - 8], ALU.add))
            for c, (low_, high) in enumerate(((sum2[0:HD, 0, a:b], sum4[HD:P, 0, a:b]), (sum8[0:HD, a:b], sum2[HD:P, 1, a:b]))):
                then(dve.tensor_tensor(TS[0:HD, c, :], low_, inv[0:HD, c, :], ALU.mult))
                then(dve.tensor_tensor(TS[HD:P, c, :], high, inv[HD:P, c, :], ALU.mult))
                dve.tensor_tensor(TS[:, c, :], TS[:, c, :], apad[:, c, a:b], ALU.subtract).then_inc(dve_ready, 1)
            dve.wait_ge(lin_free, R["in1"] + 6)
            g0 = KS - 1
            then(dve.tensor_tensor(glu[:, :, g0:g0 + T1], glu[:, :, g0:g0 + T1], sig[:, :, :], ALU.mult))
            for c in range(2):
                y = sig[:, c, :]
                then(dve.tensor_scalar(y, glu[:, c, 0:T1], vec("conv_w", c * KS), vec("conv_b", c), ALU.mult, ALU.add))
                for k in range(1, KS):
                    ins = dve.scalar_tensor_tensor(out=y, in0=glu[:, c, k:k + T1], scalar=vec("conv_w", c * KS + k), in1=y,
                                                   op0=ALU.mult, op1=ALU.add)
                    if k < KS - 1:
                        then(ins)
                ins.then_inc(dve_ready, 1)
            dve.wait_ge(act_done, DONE0["fg"] + 1)
            z, soft, total = (staged(e, T1)[0:FOX_H, :] for e in (0, 1, 2))
            then(dve.tensor_scalar(z, z, 0.0, None, ALU.min))
            then(dve.tensor_tensor(soft, soft, z, ALU.subtract))
            then(dve.tensor_tensor_scan(total, consts[0:FOX_H, C0["ones"]:C0["ones"] + 1].to_broadcast([FOX_H, T1]), soft, 0.0,
                                        ALU.mult, ALU.add))
            parts(total, z.bitcast(F32R), soft.bitcast(F32R)).then_inc(dve_ready, 1)
            dve.tensor_copy(ones2[:, :], const("ones", rows=2)).then_inc(dve_ready, 1)
            for c in range(2):
                dve.wait_ge(lin_free, R["pool"] + c + 1)
                then(dve.tensor_scalar(apad[:, c, a:b], apad[:, c, a:b], vec("pool_s", c), None, ALU.mult))
                parts(apad[:, c, a:b], o_hi(c, T1), o_lo(c, T1)).then_inc(hid_ready, 1)
            dve.wait_ge(lin_free, R["ln"] + 1)
            for c in range(2):
                dve.tensor_tensor(sig[:, c, :], sig[:, c, :], TS[:, 2, :], ALU.add).then_inc(act_asked, 1)
            reciprocal_root(R["lnv"], T1)
            zero_other_heads()
            for c in range(2):
                dve.scalar_tensor_tensor(out=sig[:, c, :], in0=sig[:, c, :], scalar=vec("ln_g", c), in1=TS[:, 2, :],
                                         op0=ALU.mult, op1=ALU.mult).then_inc(act_asked, 1)
            for c in range(2):
                dve.wait_ge(act_done, DONE0["ln"] + c + 1)
                parts(sig[:, c, :], o_hi(2 + c, T1), o_lo(2 + c, T1)).then_inc(hid_ready, 1)

            attention("fox")
            feature_parts("ot1", 4, T1, 4)
            with dve.Fori(0, 4) as i:
                for m in range(2):
                    r, e = R["merge"] + 6 * m, E0["merge"] + 6 * m
                    dve.wait_ge(hid_ready, HID0["merge"] + i * 2 + m)
                    for g in range(3):
                        dve.wait_ge(lin_free, r + i * 12 + 4 + g)
                        dve.tensor_tensor(TS[:, g, :], staged(e + g, T1), staged(e + 3 + g, T1), ALU.mult).then_inc(ev_used, 1)
                    dve.wait_ge(ev_used, e + i * 12 + 3)
                    dve.tensor_tensor(TS[:, 0, :], TS[:, 0, :], TS[:, 1, :], ALU.add).then_inc(ev_used, 1)
                    dve.wait_ge(ev_used, e + i * 12 + 4)
                    dve.tensor_tensor(TS[:, 0, :], TS[:, 0, :], TS[:, 2, :], ALU.add).then_inc(ev_used, 1)
                    dve.wait_ge(ev_used, e + i * 12 + 5)
                    hi = HIDH[:, bass.ds(i * (2 * T1) + (C + m) * T1, T1)]
                    lo = HIDL[:, bass.ds(i * (2 * T1) + (low - (C - m) * T1), T1)]
                    dve.tensor_copy(hi, TS[:, 0, :]).then_inc(ev_used, 1)
                    dve.wait_ge(ev_used, e + i * 12 + 6)
                    dve.tensor_tensor(lo, TS[:, 0, :], hi.bitcast(F32), ALU.subtract).then_inc(hid_ready, 1)
            residual("wo1", T1, "n2")
            reciprocal_root(R["n2"], T1)
            normed("norm2", X0["n2"], T1, x_hi(T1), x_lo(T1), U["router"])
            dve.wait_ge(lin_free, R["routerT"] + 1)
            NTT = QT + 1

            def wide(ap, n=4):
                return ap.unsqueeze(2).to_broadcast([P, NTT, n])

            def vec_rows(name, a, n):
                return vecs[:, V0[name] + a:V0[name] + a + n].unsqueeze(1).to_broadcast([P, NTT, n])

            glog, elog = route[:, 0, :, 0:4], route[:, 1, :, :]
            val = [route[:, 2, :, k] for k in range(10)]
            less, ex = route[:, 3, :, :], route[:, 4, :, :]
            prio = vec_rows("prio", 0, 4)

            def first_of(out_, src, top, best):
                then(dve.tensor_tensor(out_, src, wide(top), ALU.is_equal))
                then(dve.tensor_tensor(out_, out_, prio, ALU.mult))
                then(dve.tensor_reduce(best, out_, AX, ALU.max))
                then(dve.tensor_tensor(out_, out_, wide(best), ALU.is_equal))

            group, top1, top2, rest, w = (route[:, k, :, 0:4] for k in (5, 7, 8, 9, 10))
            then(dve.tensor_tensor(glog, glog, vec_rows("rbias", 0, 4), ALU.add))
            then(dve.tensor_tensor(elog, elog, vec_rows("rbias", 4, 16), ALU.add))
            then(dve.tensor_reduce(val[0], glog, AX, ALU.max))
            then(dve.tensor_tensor(less[:, :, 0:4], glog, wide(val[0]), ALU.subtract))
            first_of(group, glog, val[0], val[1])
            grid = route[:, 6, :, :].rearrange("p t (g e) -> p t g e", g=N_GRP)
            then(dve.tensor_tensor(grid, elog.rearrange("p t (g e) -> p t g e", g=N_GRP),
                                   group.unsqueeze(3).to_broadcast([P, NTT, N_GRP, PER_GRP]), ALU.mult))
            then(dve.tensor_reduce(rest, route[:, 6, :, :].rearrange("p t (g e) -> p t e g", g=N_GRP), AX, ALU.add))
            then(dve.tensor_reduce(val[2], rest, AX, ALU.max))
            dve.tensor_tensor(less[:, :, 4:8], rest, wide(val[2]), ALU.subtract).then_inc(act_asked, 1)
            dve.wait_ge(act_done, DONE0["router"] + 1)
            then(dve.tensor_reduce(val[3], ex[:, :, 0:4], AX, ALU.add))
            then(dve.tensor_reduce(val[4], ex[:, :, 4:8], AX, ALU.max))
            first_of(top1, ex[:, :, 4:8], val[4], val[5])
            then(dve.scalar_tensor_tensor(out=rest, in0=top1, scalar=-2.0, in1=ex[:, :, 4:8], op0=ALU.mult, op1=ALU.add))
            then(dve.tensor_reduce(val[6], rest, AX, ALU.max))
            first_of(top2, rest, val[6], val[7])
            then(dve.tensor_tensor(val[8], val[4], val[6], ALU.add))
            then(dve.tensor_tensor(val[8], val[8], val[3], ALU.mult))
            then(dve.reciprocal(val[9], val[8]))
            then(dve.tensor_tensor(w, top1, top2, ALU.add))
            then(dve.tensor_tensor(w, w, ex[:, :, 4:8], ALU.mult))
            then(dve.tensor_tensor(w, w, wide(val[9]), ALU.mult))
            dve.tensor_tensor(route[:, 11, :, :].rearrange("p t (g e) -> p t g e", g=N_GRP),
                              w.unsqueeze(2).to_broadcast([P, NTT, N_GRP, PER_GRP]),
                              group.unsqueeze(3).to_broadcast([P, NTT, N_GRP, PER_GRP]), ALU.mult).then_inc(dve_ready, 1)
            dve.wait_ge(lin_free, R["cb"] + N_EXP)
            before, per = steps[0], 8
            with dve.Fori(0, N_GRP) as i:
                steps[0] = i * per + before
                r, e = R["moe"] - HEAD, E0["moe"]
                for j in range(C):
                    y = TS[:, j % 2, :]
                    dve.wait_ge(lin_free, r + i * 24 + 2 * j + 2)
                    dve.tensor_tensor(y, staged(e + 2 * j, T1), staged(e + 2 * j + 1, T1), ALU.mult).then_inc(ev_used, 1)
                    dve.wait_ge(ev_used, e + i * 24 + 2 * j + 1)
                    dve.tensor_tensor(y, y, CB[:, i * PER_GRP + j // 2, :], ALU.mult).then_inc(ev_used, 1)
                    dve.wait_ge(ev_used, e + i * 24 + 2 * j + 2)
                    if j == 0:
                        dve.wait_ge(unit_used, U["moe"] + i * 24)
                    parts(y, o_hi(j, T1), o_lo(j, T1)).then_inc(hid_ready, 1)
                for j in range(C):
                    dve.wait_ge(lin_free, r + i * 24 + 16 + j + 1)
                    dve.tensor_tensor(H[:, j, :], H[:, j, :], staged(e + 16 + j, T1), ALU.add).then_inc(ev_used, 1)
            steps[0] = before + per * N_GRP
            reciprocal_root(R["nf1"], T1)
            normed_in_place("final1", TS[:, 2, META:T1])
            reciprocal_root(R["na0"], T2)
            normed("attn0", X0["na0"], T2, x_hi(T2), x_lo(T2), U["kc"])
            zero_other_heads()
            dve.wait_ge(lin_free, R["tok2"] + 3)
            for t in range(QT):
                g = gate48[:, t, 0:3 * NH:3]
                ins = dve.tensor_scalar(g, g, vec("cvalid", t), None, ALU.mult)
                then(ins)
            dve.wait_ge(pairs_moved, 64)
            for kv in range(2):
                if kv:
                    dve.wait_ge(dve_ready, 8)
                for b in range(CMP_B // 2):
                    ins = dve.tensor_scalar(BLK[:, b, :].rearrange("p (g n) -> p g n", g=A_G),
                                            PAIR[:, 2 * kv:2 * kv + 2, :, b:b + 8 * (NC - 1) + 1:8].rearrange("p q g n -> p (q g) n"),
                                            vec("cpos", kv * (CMP_B // 2) + b), None, ALU.add)
                    if b == CMP_B // 2 - 1:
                        then(ins)
                if kv:
                    dve.wait_ge(unit_used, U["cmp"] + 4)
                parts(BLK[:, :, :], BLKH[:, :, :], BLKL[:, :, :]).then_inc(dve_ready, 1)
            dve.wait_ge(lin_free, R["cmp"] + 7)
            k_, kr = (staged(E0["cmp"] + x, 2 * NC).rearrange("p (g n) -> p g n", g=2) for x in range(2))
            cosc, sinc = (const(x).unsqueeze(1).to_broadcast([P, 2, NC]) for x in ("cosc", "sinc"))
            ta, tb = (TS[:, x, 0:2 * NC].rearrange("p (g n) -> p g n", g=2) for x in range(2))
            dve.tensor_tensor(ta, k_, cosc, ALU.mult).then_inc(ev_used, 1)
            dve.tensor_tensor(tb, kr, sinc, ALU.mult).then_inc(ev_used, 1)
            dve.wait_ge(ev_used, E0["cmp"] + 2)
            dve.tensor_tensor(KCMP[:, :, 0:NC], ta, tb, ALU.add).then_inc(rope_ready, 1)
            rotated("rope2", 12, lambda c: KSEL[:, c, :] if c < 2 else KWIN[:, c - 2, :] if c < 4 else Q2[:, c - 4, :])

            attention("nsa0")
            attention("nsa1")
            feature_parts("ot2", C, T2, 0)
            residual("wo2", T2, "nf0")
            reciprocal_root(R["nf0"], T2)
            normed("ffn0", X0["nf0"], T2, x_hi(T2), x_lo(T2), U["wo2"])
            ffn(0)
            reciprocal_root(R["na1"], T2)
            normed("kv", X0["kv"], T2, lambda c: o_hi(c, T2), lambda c: o_lo(c, T2), U["k3"])
            normed("attn1", X0["na1"], T2, x_hi(T2), x_lo(T2), U["k3"])
            zero_other_heads()
            dve.wait_ge(x_ready, X0["nf_1"])
            dve.wait_ge(lin_free, R["kv3"] + 3)
            e = E0["k3"]
            dve.tensor_tensor(TS[:, 0, 0:T2], staged(e, T2), const("cosq"), ALU.mult).then_inc(ev_used, 1)
            dve.tensor_tensor(TS[:, 1, 0:T2], staged(e + 1, T2), const("sinq"), ALU.mult).then_inc(ev_used, 1)
            dve.wait_ge(ev_used, e + 2)
            dve.tensor_tensor(K3[:, :], TS[:, 0, 0:T2], TS[:, 1, 0:T2], ALU.add).then_inc(rope_ready, 1)
            rotated("q3", 8, lambda c: Q3[:, c, :])

            attention("swa")
            feature_parts("ot3", C, T2, 0)
            residual("wo3", T2, "nf_1")
            reciprocal_root(R["nf_1"], T2)
            normed("ffn1", X0["nf_1"], T2, x_hi(T2), x_lo(T2), U["wo3"])
            ffn(1)
            reciprocal_root(R["nfin"], T2)
            normed_in_place("final2", TS[:, 2, 0:T2])


def units_of(w):
    rows, cols = w.shape
    w = w.reshape(rows // UNIT, KC, P, cols // P, P).transpose(3, 0, 2, 1, 4)
    return w.reshape(-1, P, UNIT)


def padded(w, cols):
    out = np.zeros((w.shape[0], cols), np.float32)
    out[:, :w.shape[1]] = w
    return out


def lay_stream(a):
    w = np.asarray(a["w_in"])[0]
    cut = np.cumsum([POOL_W, CONV_W, CONV_W, FOX_W, FOX_W, FOX_W, FOX_H])
    pool, bv, bg, q, k, v, fg, gates = np.split(w, cut, axis=1)
    seq = [units_of(x) for x in (pool, bv, bg, padded(fg, P), q, v, k)]
    branch = units_of(np.concatenate([np.asarray(a[n])[0] for n in ("w_out_a", "w_out_b", "w_out_c")], axis=0))
    gate = units_of(gates).reshape(3, C, P, UNIT)
    seq.append(np.concatenate([gate, branch[None]], axis=0).transpose(1, 0, 2, 3).reshape(-1, P, UNIT))
    seq.append(units_of(np.asarray(a["w_o"])[0]))
    seq.append(units_of(padded(np.concatenate([np.asarray(a["router_g"])[0], np.asarray(a["router_e"])[0]], axis=1), P)))
    w1, w3, w2 = (np.asarray(a[n])[0] for n in ("exp_w1", "exp_w3", "exp_w2"))
    for g in range(N_GRP):
        for e in range(g * PER_GRP, (g + 1) * PER_GRP):
            seq.append(np.stack([units_of(w1[e]), units_of(w3[e])], axis=1).reshape(-1, P, UNIT))
        seq.append(units_of(w2[g * PER_GRP:(g + 1) * PER_GRP].reshape(PER_GRP * EXP_HID, D)))
    w = np.asarray(a["a_w_in_2"])[0]
    q, kc, vc, ks, vs, kw, vw, gl = np.split(w, np.cumsum([NH * HD] + [A_G * HD] * 6), axis=1)
    q = q.reshape(D, 2, 2, 4, HD).transpose(0, 1, 3, 2, 4).reshape(D, D)
    seq += [units_of(x) for x in (kc, vc, padded(gl, P), vs, vw)]
    c1 = np.asarray(a["a_cmp_w1_2"])[0]
    seq += [units_of(c1[0]), units_of(c1[1])]
    seq += [units_of(x) for x in (ks, kw, q, np.asarray(a["a_w_out_2"])[0])]

    def ffn(layer):
        w = units_of(np.asarray(a["ffn_w_in_2"])[layer]).reshape(2, FC, P, UNIT).transpose(1, 0, 2, 3).reshape(-1, P, UNIT)
        o = np.zeros((3 * UNIT, D), np.float32)
        o[:DFF] = np.asarray(a["ffn_w_out_2"])[layer]
        return [w, units_of(o)]

    seq += ffn(0)
    k, v = np.split(np.asarray(a["b_w_kv_2"]), 2, axis=1)
    q = np.asarray(a["b_w_q_2"])[0].reshape(D, B_G, 8, HD).transpose(0, 2, 1, 3).reshape(D, D)
    seq += [units_of(x) for x in (k, v, q, np.asarray(a["b_w_out_2"])[0])]
    seq += ffn(1)
    out = np.concatenate(seq, axis=0)
    assert out.shape == (N_UNITS, P, UNIT), out.shape
    return np.ascontiguousarray(out)


def lay_vecs(a):
    def cols(x):
        return np.asarray(x).reshape(-1, P).T

    def rows(x):
        return np.tile(np.asarray(x).reshape(1, -1), (P, 1))

    out = {"norm1": cols(a["norm1_g"]), "norm2": cols(a["norm2_g"]), "final1": cols(a["final_g"]),
           "attn0": cols(np.asarray(a["norm_attn_2"])[0]), "attn1": cols(np.asarray(a["norm_attn_2"])[1]),
           "ffn0": cols(np.asarray(a["norm_ffn_2"])[0]), "ffn1": cols(np.asarray(a["norm_ffn_2"])[1]),
           "kv": cols(a["kv_norm_2"]), "final2": cols(a["final_norm_2"]), "pool_b": cols(a["pool_b"]), "pool_s": cols(a["pool_scale"]),
           "conv_b": cols(a["conv_b"]), "ln_g": cols(a["conv_ln_g"]), "ln_b": cols(a["conv_ln_b"]),
           "conv_w": np.asarray(a["conv_w"])[0].T.reshape(2, P, KS).transpose(1, 0, 2).reshape(P, 2 * KS),
           "bforget": np.concatenate([np.asarray(a["b_forget"]).reshape(-1, 1), np.zeros((P - FOX_H, 1), np.float32)]),
           "sink": rows(a["b_sinks_2"]),
           "rbias": np.concatenate([rows(a["router_g_b"]), rows(a["router_e_b"])], axis=1),
           "prio": rows(np.arange(4, 0, -1, dtype=np.float32)), "eps": np.full((P, 1), EPS), "one": np.ones((P, 1)),
           "cpos": np.asarray(a["a_cmp_pos_2"])[0].reshape(2, CMP_B // 2, P).transpose(2, 0, 1).reshape(P, -1)}
    valid = (np.arange(SEQ) >= CMP_B - 1).astype(np.float32)
    out["cvalid"] = valid.reshape(QT, P).T
    for layer in range(2):
        w = np.concatenate([np.asarray(a["ffn_conv_w_2"])[layer], np.asarray(a["ffn_conv_b_2"])[layer][None]], axis=0)
        out[f"fw{layer}"] = w.reshape(4, 2, FC, P).transpose(3, 2, 1, 0).reshape(P, -1)
    return np.ascontiguousarray(np.concatenate([out[n].astype(np.float32) for n, _ in VECS], axis=1))


def lay_consts(a):
    f = np.float32
    rot = np.zeros((P, P), f)
    half = HD // 2
    for h in range(2):
        for d in range(half):
            rot[h * HD + d + half, h * HD + d] = -1.0
            rot[h * HD + d, h * HD + d + half] = 1.0
    i, j = np.arange(P)[:, None], np.arange(P)[None, :]
    causal = np.where(j <= i, 0.0, NEG)
    band = np.concatenate([np.where(j > i, 0.0, NEG), causal], axis=1)
    ends = np.arange(NC) * CMP_S + CMP_B - 1
    cmask = np.where(ends[None, :] <= np.arange(SEQ)[:, None], 0.0, NEG).reshape(QT, P, NC).transpose(1, 0, 2).reshape(P, -1)
    angle = f(10000.0) ** (-np.arange(half, dtype=f) / f(half))

    def table(fn, pos):
        t = fn((pos.astype(f)[:, None] * angle[None, :]).astype(f)).T
        return np.concatenate([t] * 4, axis=0)

    pw = np.asarray(a["pool_w"])[0]
    poolw = np.zeros((P, 2 * P), f)
    for g in range(4):
        lo = HD * (g % 2)
        poolw[lo:lo + HD, (g // 2) * P + lo:(g // 2) * P + lo + HD] = pw[g]
    w2 = np.asarray(a["a_cmp_w2_2"])[0].reshape(2, 2, P, HD)
    w2k = np.zeros((P, 2, 2, P), f)
    for j in range(2):
        w2k[:, j, 0, 0:HD] = w2[0, j]
        w2k[:, j, 1, HD:P] = w2[0, j]
    pos = np.arange(SEQ)
    out = {"ident": np.eye(P), "ones": np.ones((P, P)), "rot": rot, "causal": causal, "band": band, "poolw": poolw,
           "cosq": table(np.cos, pos), "sinq": table(np.sin, pos), "cosc": table(np.cos, ends), "sinc": table(np.sin, ends),
           "cmask": cmask, "w2k": w2k.reshape(P, -1), "w2v": w2[1].transpose(1, 0, 2).reshape(P, -1)}
    return np.ascontiguousarray(np.concatenate([out[n].astype(f) for n, _ in CONSTS], axis=1))


def lay_inverse_counts():
    out = np.zeros((P, 2, T1), np.float32)
    for g, window in enumerate((2, 4, 8, 16)):
        lo = HD * (g % 2)
        out[lo:lo + HD, g // 2, :] = 1.0 / np.minimum(np.arange(T1) + 1, window)
    return out


def kernel(**inputs):
    import concourse.bacc as bacc
    from concourse.bass_utils import run_bass_kernel_spmd

    h = np.concatenate([np.asarray(inputs["meta"]), np.asarray(inputs["x"])[0]], axis=0)
    arrays = {"stream": lay_stream(inputs), "x_fm": np.ascontiguousarray(h.T.reshape(C, P, T1).transpose(1, 0, 2)),
              "vecs_in": lay_vecs(inputs), "consts_in": lay_consts(inputs), "inv_counts": lay_inverse_counts()}
    nc = bacc.Bacc("TRN2", target_bir_lowering=False, num_devices=1)
    aps = [nc.dram_tensor(n, x.shape, F32, kind="ExternalInput").ap() for n, x in arrays.items()]
    out = nc.dram_tensor("out_fm", [P, C, SEQ], F32, kind="ExternalOutput").ap()
    build(nc, *aps, out)
    got = run_bass_kernel_spmd(nc, [arrays], core_ids=[0]).results[0]["out_fm"]
    return np.ascontiguousarray(got.transpose(1, 0, 2).reshape(D, SEQ).T)[None]
```

```python
from contextlib import ExitStack

import numpy as np
import concourse.bass as bass
from concourse import mybir

F32 = mybir.dt.float32
F32R = mybir.dt.float32r
ALU = mybir.AluOpType
ACT = mybir.ActivationFunctionType
AX = mybir.AxisListType.X

P = 128
D = 1024
C = D // P
SEQ, META = 512, 16
T1, T2 = SEQ + META, SEQ
HALF = T1 // 2
QT = SEQ // P
HD = 64
EPS = 1e-6
NEG = -1e30
KC = 8
UNIT = KC * P
POOL_W, CONV_W, FOX_H, KS = 256, 256, 8, 31
FOX_W = FOX_H * HD
N_GRP, PER_GRP = 4, 4
N_EXP, EXP_HID = 16, 256
NH, A_G, B_G = 16, 4, 2
CMP_B, CMP_S, CMP_HID = 32, 16, 256
NC = SEQ // CMP_S - CMP_B // CMP_S + 1
WIN_B = 128
DFF = 2816
FC = DFF // P
SCALE = HD ** -0.5

CMP_UNITS = 8
PARTS = [("pool", 2), ("bv", 2), ("bg", 2), ("fg", 1), ("q1", 4), ("v1", 4), ("k1", 4),
         ("merge", 32), ("wo1", 8), ("router", 1), ("moe", 96),
         ("kc", 2), ("vc", 2), ("gl", 1), ("vs", 2), ("vw", 2), ("cmp", CMP_UNITS), ("ks", 2), ("kw", 2), ("q2", 8), ("wo2", 8),
         ("ffn0_in", 2 * FC), ("ffn0_out", 24),
         ("q3", 8), ("k3", 1), ("v3", 1), ("wo3", 8), ("ffn1_in", 2 * FC), ("ffn1_out", 24)]
U = {}
N_UNITS = 0
for _name, _count in PARTS:
    U[_name] = N_UNITS
    N_UNITS += _count
RAW, SPLIT = 4, 2

VECS = [("norm1", 8), ("norm2", 8), ("final1", 8), ("attn0", 8), ("ffn0", 8), ("kv", 8), ("attn1", 8), ("ffn1", 8),
        ("final2", 8), ("pool_b", 2), ("pool_s", 2), ("conv_b", 2), ("ln_g", 2), ("ln_b", 2), ("conv_w", 2 * KS),
        ("bforget", 1), ("fw0", 2 * FC * 4), ("fw1", 2 * FC * 4), ("sink", NH), ("rbias", N_GRP + N_EXP),
        ("prio", 4), ("eps", 1), ("one", 1), ("cvalid", QT), ("cpos", 2 * CMP_B // 2)]
V0 = {}
N_VEC = 0
for _name, _count in VECS:
    V0[_name] = N_VEC
    N_VEC += _count

CONSTS = [("ident", P), ("ones", P), ("rot", P), ("causal", P), ("band", 2 * P), ("poolw", 2 * P),
          ("cosq", SEQ), ("sinq", SEQ), ("cosc", NC), ("sinc", NC), ("cmask", QT * NC), ("w2k", 4 * P), ("w2v", 2 * HD)]
C0 = {}
N_CONST = 0
for _name, _count in CONSTS:
    C0[_name] = N_CONST
    N_CONST += _count

HEAD = 5
STAGES = [("n1", 1), ("in1", 11), ("pool", 2), ("v1", 8), ("ln", 1), ("k1a", 1), ("lnv", 1), ("k1b", 3), ("ot1", 4), ("merge", 48), ("wo1", 8),
          ("n2", 1), ("router", 1), ("moe_a", 1), ("routerT", 1), ("moe_b", HEAD - 1), ("combT", 1), ("cb", N_EXP), ("moe", 96 - HEAD),
          ("kc", 2), ("nf1", 1), ("vc", 2), ("tok2", 10), ("cmp", 7), ("rope2", 24), ("wo2", 8),
          ("nf0", 1), ("ffn0_in", 2 * FC), ("ffn0_out", 8), ("na1", 1), ("q3", 16), ("kv3", 4), ("wo3", 8),
          ("nf_1", 1), ("ffn1_in", 2 * FC), ("ffn1_out", 8), ("nfin", 1)]
R = {}
N_RES = 0
for _name, _count in STAGES:
    R[_name] = N_RES
    N_RES += _count
PAIRS = 4

STAGED = [("ot1", 4), ("merge", 48), ("wo1", 8), ("moe", 96), ("cmp", 2), ("rope2", 24), ("wo2", 8), ("ffn0_in", 2 * FC),
          ("ffn0_out", 8), ("q3", 16), ("k3", 2), ("wo3", 8), ("ffn1_in", 2 * FC), ("ffn1_out", 8)]
E0 = {}
N_EV = 0
for _name, _count in STAGED:
    E0[_name] = N_EV
    N_EV += _count
EV_SLOTS = 4

FOX_ITEMS = [(half, t) for half in range(2) for t in range(QT + 1)]
NSA_ITEMS = [(half, t, b) for half in range(2) for t in reversed(range(QT)) for b in (1, 0, 2)]
SWA_ITEMS = [(half, t) for half in range(2) for t in range(QT)]
ITEMS = {"fox": FOX_ITEMS, "nsa0": NSA_ITEMS, "nsa1": NSA_ITEMS, "swa": SWA_ITEMS}
CHUNKS = {"fox": 4, "nsa0": 4, "nsa1": 4, "swa": 8}
DEPTH = {"fox": 3, "nsa0": 4, "nsa1": 4, "swa": 4}
LAG = {"fox": 3, "nsa0": 4, "nsa1": 4, "swa": 4}
FOX_BANK = [0, 1, 2, 3, 0, 2, 3, 0, 1, 2]
FOX_PROBS = [0, 1, 2, 0, 1, 2, 0, 1, 2, 3]
MASKS = {"fox": 1, "nsa0": 1, "nsa1": 1, "swa": 1}
A0, Q0, O0, M0 = {}, {}, {}, {}
W0 = {"nsa0": 0, "nsa1": 4 * len(NSA_ITEMS), "swa": 8 * len(NSA_ITEMS)}
_a = _q = _o = _m = 0
for _name, _items in ITEMS.items():
    A0[_name], Q0[_name], O0[_name], M0[_name] = _a, _q, _o, _m
    _n = len(_items) * CHUNKS[_name]
    _a, _q, _m = _a + _n, _q + CHUNKS[_name], _m + _n * MASKS[_name]
    _o += _n // 3 if _items is NSA_ITEMS else _n


def at(i, stride, base=0):
    return i * stride + base


ALONE = [("pool", 2), ("v1", 4), ("ln", 1), ("ot1", 4), ("merge", 16), ("routerT", 1), ("combT", 1), ("cb", N_EXP), ("tok2", 5), ("cmp", 3),
         ("rope2", 12), ("q3", 8), ("k3", 1), ("v3", 1)]
L0 = {}
N_ALONE = 0
for _name, _count in ALONE:
    L0[_name] = N_ALONE
    N_ALONE += _count

X0 = {"n1": 0, "n2": C, "na0": 2 * C, "nf0": 3 * C, "na1": 4 * C, "kv": 5 * C, "nf_1": 6 * C}
HID0 = {"pool": 0, "conv": 2, "merge": 4, "moe": 12, "ffn0": 44, "ffn1": 44 + FC}
SQ0 = {"n1": 0, "ln": C, "n2": C + 2, "nf1": 2 * C + 2, "nf0": 3 * C + 2, "na1": 4 * C + 2, "nf_1": 5 * C + 2, "nfin": 6 * C + 2}
SUMS = {"n1": 2, "ln": 2, "n2": 2, "nf1": 2, "nf0": 2, "na1": 2, "nf_1": 2, "nfin": 2}
S0 = {_name: sum(list(SUMS.values())[:_i]) for _i, _name in enumerate(SUMS)}
ADD0 = {_name: _i * (C - 2) for _i, _name in enumerate(("n1", "n2", "nf0", "na1", "nf_1", "nfin"))}
ROPE0 = {"rope2": 1, "q3": 13, "k3": 21}
DONE0 = {"fg": 0, "ln": 1, "router": 3, "nf1": 4, "ffn0": 6, "ffn1": 6 + FC}


def build(nc, stream, x_in, vecs_in, consts_in, invcnt_in, out):
    with ExitStack() as ctx:
        def sb(name, shape, dt=F32):
            return ctx.enter_context(nc.sbuf_tensor(name, shape, dt))

        def sem(name):
            return ctx.enter_context(nc.semaphore(name))

        arena_at = (nc.sbuf_base + 31) // 32 * 32
        sb("arena", [P, 2 * FC * SEQ])
        HIDH = nc.alloc_sbuf_tensor_at("hid_hi", [P, FC * SEQ], F32R, offset=arena_at)
        HIDL = nc.alloc_sbuf_tensor_at("hid_lo", [P, FC * SEQ], F32R, offset=arena_at + FC * SEQ * 4)
        SPARE = nc.alloc_sbuf_tensor_at("spare", [P, C * T1], F32, offset=arena_at)
        raw = sb("raw", [P, RAW, UNIT])
        w_hi = sb("w_hi", [P, SPLIT, UNIT], F32R)
        w_lo = sb("w_lo", [P, SPLIT, UNIT], F32R)
        XH = sb("x_hi", [P, C, T1], F32R)
        XL = sb("x_lo", [P, C, T1], F32R)
        H = sb("resid", [P, C, T1])
        EV = sb("staged", [P, EV_SLOTS, 2 + T1])
        TS = sb("scratch", [P, 3, T1])
        SQ = sb("squares", [P, 2, T1])
        vecs = sb("vecs", [P, N_VEC])
        consts = sb("consts", [P, N_CONST])
        gate48 = sb("gate48", [P, QT, 3 * NH])
        route = sb("route", [P, 12, QT, 16])
        ones2 = sb("ones_r", [P, P], F32R)
        gain_sq = sb("gain_squares", [P, C])
        one_root = sb("one_root", [P, 1])
        one_exp = sb("one_exp", [P, 1])
        stat = sb("stat", [P, 3, len(NSA_ITEMS)])
        o_bytes, end_bytes = C * T1 * 4, 2 * FC * SEQ * 4 - C * T1 * 4
        low = FC * SEQ - C * T1
        cursor = [o_bytes]

        def over(name, shape, dt=F32, at=None):
            size = 4
            for s in shape[1:]:
                size *= s
            start = cursor[0] if at is None else at
            if at is None:
                cursor[0] += -(-size // 32) * 32
            assert start + size <= end_bytes, (name, start + size, end_bytes)
            return nc.alloc_sbuf_tensor_at(name, shape, dt, offset=arena_at + start)

        Q1 = over("q1", [P, 4, T1])
        K1 = over("k1", [P, 4, T1])
        V1 = over("v1", [P, QT + 1, FOX_W])
        nf_at = cursor[0]
        NF = over("neg_cum_logf", [P, FOX_H, T1], F32R)
        OT1 = over("o_tok1", [P, QT + 1, FOX_W])
        cursor[0] = nf_at
        apad = over("a_pad", [P, 2, 16 + T1])
        sum2 = over("sum2", [P, 2, 16 + T1])
        sum4 = over("sum4", [P, 2, 16 + T1])
        sum8 = over("sum8", [P, 16 + T1])
        glu = over("glu", [P, 2, KS - 1 + T1])
        sig = over("sig", [P, 2, T1])
        inv = over("inv_count", [P, 2, T1])
        cursor[0] = o_bytes
        CB = over("comb_rows", [P, N_EXP, T2])
        cursor[0] = o_bytes
        q2_at = cursor[0]
        Q2 = over("q2", [P, 8, SEQ])
        ks_at = cursor[0]
        KSEL = over("k_sel", [P, 2, SEQ])
        KWIN = over("k_win", [P, 2, SEQ])
        VSEL = over("v_sel", [P, QT, 2 * P])
        VWIN = over("v_win", [P, QT, 2 * P])
        KCMP = over("k_cmp", [P, 2, 32])
        VCMP = over("v_cmp", [P, A_G, HD])
        HIDC = over("cmp_hidden", [P, 2, A_G * NC])
        EO = over("kv_even_odd", [P, 4, 2, SEQ // 2])
        PAIR = over("kv_pairs", [P, 4, 2, SEQ // 2])
        COSR2 = over("cos_over_roots", [P, SEQ])
        SINR2 = over("sin_over_roots", [P, SEQ])
        BLK = over("cmp_blocks", [P, CMP_B // 2, A_G * NC], at=ks_at)
        BLKH = over("cmp_blocks_hi", [P, CMP_B // 2, A_G * NC], F32R, at=q2_at)
        BLKL = over("cmp_blocks_lo", [P, CMP_B // 2, A_G * NC], F32R, at=q2_at + CMP_B // 2 * A_G * NC * 4)
        cursor[0] = o_bytes
        Q3 = over("q3", [P, 8, SEQ])
        K3 = over("k3", [P, SEQ])
        V3 = over("v3", [P, QT, P])
        IDR = over("ident_r", [P, P], F32R)
        BANDR = over("band_r", [P, 2 * P], F32R)
        COSR = over("cos_over_root", [P, SEQ])
        SINR = over("sin_over_root", [P, SEQ])
        VFM = over("v_feature_major", [P, SEQ])

        PS = ctx.enter_context(nc.psum_tensor("psum", [P, 8, 512], F32))

        raw_loaded = [sem(f"raw_loaded{s}") for s in range(RAW)]
        vecs_loaded = sem("vecs_loaded")
        ones_loaded = sem("ones_loaded")
        consts_loaded = sem("consts_loaded")
        x_loaded = [sem(f"x_loaded{i}") for i in range(4)]
        inv_loaded = sem("inv_loaded")
        pairs_moved = sem("pairs_moved")
        stored = sem("stored")
        pads_zeroed = sem("pads_zeroed")
        hi_split = sem("hi_split")
        split_ready = sem("split_ready")
        unit_used = sem("unit_used")
        lin_done = sem("lin_done")
        lin_free = sem("lin_free")
        ev_used = sem("ev_used")
        y_ready = sem("y_ready")
        hi_ready = sem("hi_ready")
        x_ready = sem("x_ready")
        two_added = sem("two_added")
        scaled = sem("scaled")
        silu_done = sem("silu_done")
        h_ready = sem("h_ready")
        hid_ready = sem("hid_ready")
        sq_ready = sem("sq_ready")
        sq_added = sem("sq_added")
        sq_used = sem("sq_used")
        act_asked = sem("act_asked")
        act_done = sem("act_done")
        dve_step = sem("dve_step")
        act_step = sem("act_step")
        dve_ready = sem("dve_ready")
        rope_ready = sem("rope_ready")
        q_staged = sem("q_staged")
        zeros_written = sem("zeros_written")
        rows_moved = sem("rows_moved")
        mask_ready = sem("mask_ready")
        masked = sem("masked")
        sum_inverted = sem("sum_inverted")
        weigh_ready = sem("weigh_ready")
        s_done = sem("s_done")
        max_ready = sem("max_ready")
        p_ready = sem("p_ready")
        t_done = sem("t_done")
        pt_ready = sem("pt_ready")
        o_done = sem("o_done")
        o_hi_ready = sem("o_hi_ready")
        o_ready = sem("o_ready")

        def const(name, width=None, rows=P, start=0):
            a = C0[name] + start
            return consts[0:rows, a:a + (width if width else dict(CONSTS)[name])]

        def vec(name, i=0):
            return vecs[:, V0[name] + i:V0[name] + i + 1]

        ident = const("ident")

        def pair(r):
            return PS[:, 2 * (r % PAIRS):2 * (r % PAIRS) + 2, :]

        def halves(ap):
            return ap.rearrange("p (a n) -> p a n", a=2)

        def staged(e, width, shift=2):
            return EV[:, e % EV_SLOTS, shift:shift + width]

        def o_hi(c, t):
            return HIDH[:, c * T1:c * T1 + t]

        def o_lo(c, t):
            return HIDL[:, low + c * T1:low + c * T1 + t]

        def spare(c, t):
            return SPARE[:, c * T1:c * T1 + t]

        def m_hi(c, t):
            return HIDH[:, (C + c) * T1:(C + c) * T1 + t]

        def m_lo(c, t):
            return HIDL[:, low - (C - c) * T1:low - (C - c) * T1 + t]

        QSTAGE = SQ

        def home(kind, i, n):
            return (i, n) if n >= 0 else (i - 1 if isinstance(i, int) else i + -1, n + len(ITEMS[kind]))

        def exists(kind, i, n):
            return n < len(ITEMS[kind]) and (n >= 0 or not isinstance(i, int) or i > 0)

        def number(kind, i, n, per=1, count=A0):
            return at(i, len(ITEMS[kind]) * per, count[kind] + n * per)

        def chunk_queries(kind, i):
            if kind == "fox":
                return Q1[:, i, :]
            if kind == "swa":
                return Q3[:, i, :]
            return Q2[:, at(i, 1, 4 * int(kind[3])), :]

        def queries(kind, n):
            half, t = ITEMS[kind][n][0:2]
            q0 = P * t if kind != "fox" else META + P * (t - 1) if t else 0
            return QSTAGE[:, half, q0:q0 + P]

        def keys_of(kind, i, n):
            half, t = ITEMS[kind][n][0:2]
            if kind == "fox":
                return K1[:, i, 0:META + P * t], META + P * t
            if kind == "swa":
                first = max(t - 1, 0)
                return K3[:, first * P:(t + 1) * P], P * (t + 1 - first)
            gp, b = int(kind[3]), ITEMS[kind][n][2]
            if b == 0:
                return KCMP[:, gp, 0:NC], NC
            return (KSEL if b == 1 else KWIN)[:, gp, 0:P * (t + 1)], P * (t + 1)

        def key_tiles(kind, n):
            t = ITEMS[kind][n][1]
            if kind == "fox":
                return [(META + P * j, P, P * j, j + 1) for j in range(t)] + [(0, META, None, 0)]
            if kind == "swa":
                first = max(t - 1, 0)
                return [(P * (j - first), P, P * (j - first), j) for j in range(first, t + 1)]
            if ITEMS[kind][n][2] == 0:
                return [(0, NC, 0, 0)]
            return [(P * j, P, P * j, j) for j in range(t + 1)]

        def values(kind, i, n, width, j):
            half = ITEMS[kind][n][0]
            if kind == "fox":
                return V1[0:width, j, bass.ds(at(i, P, half * HD), HD)]
            if kind == "swa":
                return V3[:, j, half * HD:(half + 1) * HD]
            g, b = 2 * int(kind[3]) + half, ITEMS[kind][n][2]
            return VCMP[0:NC, g, :] if b == 0 else (VSEL if b == 1 else VWIN)[:, j, g * HD:(g + 1) * HD]

        def scores(kind, n):
            if kind == "fox":
                return PS[:, 0:4, :].rearrange("p a n -> p (a n)")[:, 512 * FOX_BANK[n]:512 * FOX_BANK[n] + (T1 if FOX_ITEMS[n][1] == QT else 512)]
            return PS[:, n % 4, :]

        def probs(kind, n):
            return EV[:, FOX_PROBS[n] if kind == "fox" else n % 4, 2:2 + T1]

        def turned(n):
            return PS[:, 4 + n % 2, :]

        def meta_turned(n):
            t = FOX_ITEMS[n][1]
            return turned(n)[0:META, t * P:(t + 1) * P] if t < QT else PS[0:META, FOX_BANK[n] + 1, P:2 * P]

        def outs(kind, n):
            return PS[:, 6 + (n // 3 if kind in ("nsa0", "nsa1") else n) % 2, :]

        KV_CHUNKS = [0, 1, 3, 4, 6, 7, 8, 8, 8]

        def kv_chunks(c):
            return range(KV_CHUNKS[c], KV_CHUNKS[c + 1])

        def out_place(kind, i, n):
            half, t = ITEMS[kind][n][0:2]
            first = 4 * int(kind[3]) if kind != "swa" else 0
            return slice(half * HD, (half + 1) * HD), at(i, T1, first * T1 + t * P)

        def turned_copy(n, rows, col):
            return TS[:, 2, (n % 2) * P:(n % 2) * P + rows] if col is None else TS[:, n % 2, col:col + rows]

        def weights(n):
            return TS[:, 2, (n % 4) * P:(n % 4 + 1) * P]

        def token_tiles1():
            return [(0, 1, 0, META)] + [(META + P * i, 0, P * i, P) for i in range(QT)]

        def first_squares(c):
            return SQ[:, 0, :] if c == 0 else (SQ[:, 1, :], TS[:, 0, :], TS[:, 1, :])[(c - 1) % 3]

        def turning_order(count):
            order = [(0, False)]
            for c in range(1, count):
                order += [(c, False), (c - 1, True)]
            return order + [(count - 1, True)]

        block = ctx.enter_context(nc.Block())

        @block.sync
        def _(sp):
            sp.dma_start(vecs[:, :], vecs_in).then_inc(vecs_loaded, 16)
            sp.dma_start(consts[:, 0:2 * P], consts_in[:, 0:2 * P]).then_inc(ones_loaded, 16)
            for i in range(4):
                sp.dma_start(H[:, 2 * i:2 * i + 2, :], x_in[:, 2 * i:2 * i + 2, :]).then_inc(x_loaded[i], 16)
            for s in range(RAW):
                sp.dma_start(raw[:, s, :], stream[s, :, :]).then_inc(raw_loaded[s], 16)
            sp.dma_start(inv[:, :, :], invcnt_in).then_inc(inv_loaded, 16)
            sp.dma_start(consts[:, 2 * P:], consts_in[:, 2 * P:]).then_inc(consts_loaded, 16)
            with sp.Fori(1, N_UNITS // RAW) as i:
                for s in range(RAW):
                    sp.wait_ge(split_ready, i * RAW + (s + 1 - RAW))
                    sp.dma_start(raw[:, s, :], stream[i * RAW + s, :, :]).then_inc(raw_loaded[s], 16)
            for n in range(N_UNITS // RAW * RAW, N_UNITS):
                sp.wait_ge(split_ready, n + 1 - RAW)
                sp.dma_start(raw[:, n % RAW, :], stream[n, :, :]).then_inc(raw_loaded[n % RAW], 16)
            for c in range(0, C, 2):
                sp.wait_ge(h_ready, C + c + 2)
                sp.dma_start(out[:, c:c + 2, :], H[:, c:c + 2, META:T1]).then_inc(stored, 16)
            sp.wait_ge(stored, 16 * C // 2)

        @block.gpsimd
        def _(pool):
            pool.memset(apad[:, :, 0:16], 0.0).then_inc(pads_zeroed, 1)
            pool.memset(sum2[:, :, 0:16], 0.0).then_inc(pads_zeroed, 1)
            pool.memset(sum4[:, :, 0:16], 0.0).then_inc(pads_zeroed, 1)
            pool.memset(sum8[:, 0:16], 0.0).then_inc(pads_zeroed, 1)
            pool.memset(glu[:, :, 0:KS - 1], 0.0).then_inc(pads_zeroed, 1)
            pool.memset(EV[:, :, 0:2], 0.0).then_inc(pads_zeroed, 1)
            pool.memset(route[:, :, :, :], 0.0).then_inc(pads_zeroed, 1)

            def split_unit(slot, n, loads, free, low=True):
                pool.wait_ge(raw_loaded[slot], 16 * loads)
                if free:
                    pool.wait_ge(unit_used, n - (SPLIT - 1))
                pool.tensor_tensor(w_hi[:, slot % SPLIT, :], raw[:, slot, :], vec("one").to_broadcast([P, UNIT]), ALU.mult).then_inc(hi_split, 1)
                if low:
                    pool.wait_ge(hi_split, n + 1)
                    if isinstance(n, int) and n == U["cmp"] + CMP_UNITS:
                        pool.wait_ge(split_ready, n)
                    pool.tensor_tensor(w_lo[:, slot % SPLIT, :], raw[:, slot, :], w_hi[:, slot % SPLIT, :].bitcast(F32),
                                       ALU.subtract).then_inc(split_ready, 1)

            def split_units(first, last):
                for n in range(first, last):
                    split_unit(n % RAW, n, n // RAW + 1, n >= SPLIT, not U["cmp"] <= n < U["cmp"] + CMP_UNITS)

            pool.wait_ge(vecs_loaded, 16)
            split_units(0, RAW)
            before, after = U["cmp"] // RAW, -(-(U["cmp"] + CMP_UNITS + 1) // RAW)
            with pool.Fori(1, before) as i:
                for s in range(RAW):
                    split_unit(s, i * RAW + s, i + 1, True)
            split_units(before * RAW, after * RAW)
            with pool.Fori(after, N_UNITS // RAW) as i:
                for s in range(RAW):
                    split_unit(s, i * RAW + s, i + 1, True)
            split_units(N_UNITS // RAW * RAW, N_UNITS)

        @block.tensor
        def _(pe):
            def take_pair(r):
                if not isinstance(r, int) or r >= PAIRS:
                    pe.wait_ge(lin_free, r - (PAIRS - 1))

            def three(outs_, slot, k, moving, start, stop):
                for p, (wt, part) in enumerate(((w_hi, 0), (w_hi, 1), (w_lo, 0))):
                    for o, m in zip(outs_, moving):
                        last = pe.matmul(o, wt[:, slot, k * P:(k + 1) * P], m[part], start=start and p == 0, stop=stop and p == 2,
                                         skip_group_check=True)
                return last

            def moving_of(hi, lo, t):
                if t == T1:
                    return [(hi[:, 0:HALF], lo[:, 0:HALF]), (hi[:, HALF:T1], lo[:, HALF:T1])]
                return [(hi, lo)]

            def out_of(rslot, t):
                return [PS[:, 2 * rslot, 0:HALF], PS[:, 2 * rslot + 1, 0:HALF]] if t == T1 else [PS[:, 2 * rslot, :]]

            def unit(n, slot, r, rslot, t, src, ready=None, chunks=range(KC), first=True, last=True, ends=True):
                pe.wait_ge(split_ready, n + 1)
                if first:
                    take_pair(r)
                chunks = list(chunks)
                for j, k in enumerate(chunks):
                    if ready is not None:
                        pe.wait_ge(ready[0], ready[1] + (j + 1) * (ready[2] if len(ready) > 2 else 1))
                    hi, lo = src(j)
                    mm = three(out_of(rslot, t), slot, k, moving_of(hi, lo, t), first and j == 0, last and j == len(chunks) - 1)
                mm.then_inc(unit_used if ends else lin_done, 1)

            def two_units(n, r, t, src, ready):
                pe.wait_ge(split_ready, n + 2)
                take_pair(r)
                take_pair(r + 1)
                for k in range(KC):
                    pe.wait_ge(ready[0], ready[1] + k + 1)
                    hi, lo = src(k)
                    for u in range(2):
                        mm = three(out_of((r + u) % PAIRS, t), (n + u) % SPLIT, k, moving_of(hi, lo, t), k == 0, k == KC - 1)
                        if k == KC - 1:
                            mm.then_inc(unit_used, 1)

            def x_of(t):
                return lambda k: (XH[:, k, T1 - t:T1], XL[:, k, T1 - t:T1])

            def turn(r, source, t):
                take_pair(r)
                tiles = token_tiles1() if t == T1 else [(P * i, 0, P * i, P) for i in range(QT)]
                for first, bank, col, rows in tiles:
                    mm = pe.transpose(pair(r)[0:rows, bank, col:col + P], source[:, first:first + rows], ident)
                mm.then_inc(lin_done, 1)

            def token_units(n0, r0, count, t, src, spare0, scaled0=None):
                for x, (c, turned_) in enumerate(turning_order(count)):
                    r = r0 + x
                    if turned_:
                        if scaled0 is None:
                            pe.wait_ge(lin_free, r0 + turning_order(count).index((c, False)) + 1)
                        else:
                            pe.wait_ge(scaled, scaled0 + c + 1)
                        turn(r, spare(spare0 + c, t), t)
                    else:
                        unit(n0 + c, (n0 + c) % SPLIT, r, r % PAIRS, t, src)

            def norm_sum(stage, r, t, chunks=C):
                take_pair(r)
                for c in range(chunks):
                    s = SQ0[stage] + c
                    pe.wait_ge(sq_ready, s + 1)
                    for o, a in ((0, 0), (1, HALF)) if t == T1 else ((0, 0),):
                        w = HALF if t == T1 else T2
                        mm = pe.matmul(pair(r)[:, o, 0:w], const("ones"), SQ[:, s % 2, a:a + w],
                                       start=c == 0, stop=c == chunks - 1, skip_group_check=True)
                    mm.then_inc(sq_used, 1)

            def rotate(e, r, width=T2):
                take_pair(r)
                pe.matmul(pair(r)[:, 0, 0:width], const("rot"), staged(e, width), start=True, stop=True).then_inc(lin_done, 1)

            def rope_chunks(n0, r0, e0, count, src, ready=None, summed=None):
                for c in range(count + 1):
                    if ready is not None and c < 2:
                        if c == 0:
                            unit(n0, n0 % SPLIT, r0, r0 % PAIRS, T2, src, ready)
                            gathered_sum(summed, T2)
                            unit(n0 + 1, (n0 + 1) % SPLIT, r0 + 1, (r0 + 1) % PAIRS, T2, src)
                    elif c < count:
                        r = r0 + 2 * c - (1 if c else 0)
                        unit(n0 + c, (n0 + c) % SPLIT, r, r % PAIRS, T2, src)
                    if c:
                        before = 2 * (c - 1) - (1 if c > 1 else 0)
                        pe.wait_ge(lin_free, r0 + before + 1)
                        rotate(e0 + before, r0 + 2 * c if c < count else r0 + 2 * count - 1)

            def attention(kind, results):
                body, depth, lag = len(ITEMS[kind]), DEPTH[kind], LAG[kind]
                nsa, fox = kind in ("nsa0", "nsa1"), kind == "fox"

                def step(i, n):
                    if exists(kind, i, n):
                        a = number(kind, i, n)
                        q = queries(kind, n)
                        k, keys = keys_of(kind, i, n)
                        if n % (body // 2) == 0:
                            pe.wait_ge(q_staged, at(i, 2, 2 * Q0[kind] + 1 + n // (body // 2)))
                        if exists(kind, i, n - depth):
                            pe.wait_ge(p_ready, a + (1 - depth))
                        if kind == "fox" and ITEMS[kind][n][1] == QT - 1 and exists(kind, i, n - QT):
                            pe.wait_ge(pt_ready, a + (1 - QT))
                        if kind == "swa":
                            pe.matmul(scores(kind, n)[:, 0:keys], IDR[:, :], BANDR[:, 2 * P - keys:], start=True, stop=False,
                                      skip_group_check=True)
                        for c in range(0, keys, 512):
                            w = min(512, keys - c)
                            mm = pe.matmul(scores(kind, n)[:, c:c + w], q, k[:, c:c + w], start=kind != "swa", stop=kind != "fox",
                                           skip_group_check=kind in ("fox", "swa"))
                            if kind == "fox":
                                mm = pe.matmul(scores(kind, n)[:, c:c + w], ones2[:, :], NF[:, at(i, 2, ITEMS[kind][n][0]), c:c + w],
                                               start=False, stop=True, skip_group_check=True)
                        mm.then_inc(s_done, 1)
                    if exists(kind, i, n - lag):
                        a = number(kind, i, n - lag)
                        _, m = home(kind, i, n - lag)
                        pe.wait_ge(p_ready, a + 1)
                        if exists(kind, i, n - lag - 2):
                            pe.wait_ge(pt_ready, a + -1)
                        by = ident
                        if not fox:
                            pe.wait_ge(weigh_ready, number(kind, i, n - lag + 1, 1, W0))
                            by = weights(m)
                        for col, width, dst, _ in key_tiles(kind, m):
                            o = meta_turned(m) if dst is None else turned(m)[0:width, dst:dst + P]
                            e = probs(kind, m)[:, col:col + width]
                            mm = pe.transpose(o, e, by) if fox else pe.matmul(o, e, by, start=True, stop=True)
                        mm.then_inc(t_done, 1)
                    meta = kind == "fox" and exists(kind, i, n - lag - 1) and ITEMS[kind][home(kind, i, n - lag - 1)[1]][1] == 0
                    if exists(kind, i, n - lag - 1) and not (meta and exists(kind, i, n - lag)):
                        a = number(kind, i, n - lag - 1)
                        c, m = home(kind, i, n - lag - 1)
                        pe.wait_ge(pt_ready, a + 1)
                        if nsa and m % 3 == 0 and exists(kind, i, n - lag - 1 - 6):
                            pe.wait_ge(o_ready, at(i, body // 3, O0[kind] + (n - lag - 1) // 3 - 1))
                        if not nsa and exists(kind, i, n - lag - 3):
                            pe.wait_ge(o_ready, number(kind, i, n - lag - 2, 1, O0))

                        def output(c, m, j, first, last):
                            _, width, src, tile = key_tiles(kind, m)[j]
                            e, v = turned_copy(m, P, src)[0:width, :], values(kind, c, m, width, tile)
                            if fox:
                                return pe.matmul(outs(kind, m)[:, 0:HD], e, v, start=first, stop=last)
                            return pe.matmul(outs(kind, m)[out_place(kind, 0, m)[0], 0:P], v, e, start=first, stop=last, skip_group_check=nsa)

                        tiles = len(key_tiles(kind, m))
                        for j in range(tiles):
                            if kind == "fox" and ITEMS[kind][m][1] == 1 and j == 1 and exists(kind, i, n - lag - 2):
                                output(*home(kind, i, n - lag - 2), 0, True, True).then_inc(o_done, 1)
                            mm = output(c, m, j, j == 0 and not (nsa and m % 3), j == tiles - 1 and not (nsa and m % 3 < 2))
                        mm.then_inc(o_done, 1)

                pe.wait_ge(lin_free, results)
                for n in range(body):
                    step(0, n)
                with pe.Fori(1, CHUNKS[kind]) as i:
                    for n in range(body):
                        step(i, n)
                for n in range(body, body + lag + 1):
                    step(CHUNKS[kind] - 1, n)
                pe.wait_ge(o_ready, O0[kind] + CHUNKS[kind] * body // (3 if nsa else 1))

            def turn_outputs(r0, count, ot):
                for c in range(count):
                    take_pair(r0 + c)
                    for i in range(QT):
                        mm = pe.transpose(pair(r0 + c)[:, 0, i * P:(i + 1) * P], ot[:, i, c * P:(c + 1) * P], ident)
                    mm.then_inc(lin_done, 1)

            def residual(name, t, src, ready):
                n0, r0 = U[name], R[name]
                for c in range(C):
                    unit(n0 + c, (n0 + c) % SPLIT, r0 + c, (r0 + c) % PAIRS, t, src, None if c else ready)

            def gathered_sum(stage, t):
                take_pair(R[stage])
                for x in range(2):
                    if x == 0:
                        pe.wait_ge(sq_added, ADD0[stage] + C - 2)
                    else:
                        pe.wait_ge(sq_ready, SQ0[stage] + C)
                    for o, a in ((0, 0), (1, HALF)) if t == T1 else ((0, 0),):
                        w = HALF if t == T1 else T2
                        mm = pe.matmul(pair(R[stage])[:, o, 0:w], const("ones"), SQ[:, x, a:a + w],
                                       start=x == 0, stop=x == 1, skip_group_check=True)
                    mm.then_inc(sq_used, 1)

            def hidden_of(part):
                return lambda k: (HIDH[:, (part * KC + k) * SEQ:(part * KC + k + 1) * SEQ],
                                  HIDL[:, (part * KC + k) * SEQ:(part * KC + k + 1) * SEQ])

            def ffn(layer, norm):
                n0, r0 = U[f"ffn{layer}_in"], R[f"ffn{layer}_in"]
                unit(n0, n0 % SPLIT, r0, r0 % PAIRS, T2, x_of(T2), (x_ready, X0[norm]))
                gathered_sum(norm, T2)
                for j in range(1, 4):
                    unit(n0 + j, (n0 + j) % SPLIT, r0 + j, (r0 + j) % PAIRS, T2, x_of(T2))
                with pe.Fori(1, FC // 2) as i:
                    for j in range(4):
                        unit(n0 + i * 4 + j, (n0 + j) % SPLIT, r0 + i * 4 + j, (r0 + j) % PAIRS, T2, x_of(T2))
                n0, r0 = U[f"ffn{layer}_out"], R[f"ffn{layer}_out"]
                with pe.Fori(0, 2) as i:
                    for j in range(4):
                        for part in range(3):
                            m = 3 * j + part
                            pe.wait_ge(hid_ready, HID0[f"ffn{layer}"] + min(FC, (part + 1) * KC))
                            unit(n0 + i * 12 + m, (n0 + m) % SPLIT, r0 + i * 4 + j, (r0 + j) % PAIRS, T2, hidden_of(part),
                                 chunks=range(min(KC, FC - part * KC)), first=part == 0, last=part == 2)

            pe.wait_ge(ones_loaded, 16)
            gathered_sum("n1", T1)
            r = R["in1"]
            two_units(U["pool"], r, T1, x_of(T1), (x_ready, X0["n1"]))
            for n in range(U["bv"], U["v1"]):
                unit(n, n % SPLIT, r + n - U["pool"], (r + n - U["pool"]) % PAIRS, T1, x_of(T1))
            for c in range(2):
                r = R["pool"] + c
                take_pair(r)
                pe.wait_ge(consts_loaded, 16)
                pe.wait_ge(dve_ready, c + 1)
                for o in range(2):
                    mm = pe.matmul(pair(r)[:, o, 0:HALF], const("poolw", P, start=c * P), TS[:, c, o * HALF:(o + 1) * HALF],
                                   start=True, stop=True)
                mm.then_inc(lin_done, 1)
            token_units(U["v1"], R["v1"], 4, T1, x_of(T1), 4)
            take_pair(R["ln"])
            for c in range(2):
                pe.wait_ge(dve_ready, 3 + c)
                for o in range(2):
                    mm = pe.matmul(pair(R["ln"])[:, o, 0:HALF], const("ones"), sig[:, c, o * HALF:(o + 1) * HALF],
                                   start=c == 0, stop=c == 1, skip_group_check=True)
            mm.then_inc(lin_done, 1)
            unit(U["k1"], U["k1"] % SPLIT, R["k1a"], R["k1a"] % PAIRS, T1, x_of(T1))
            norm_sum("ln", R["lnv"], T1, chunks=2)
            for c in range(1, 4):
                n, r = U["k1"] + c, R["k1b"] + c - 1
                unit(n, n % SPLIT, r, r % PAIRS, T1, x_of(T1))
            pe.wait_ge(rows_moved, 32)
            pe.wait_ge(dve_ready, 6)
            attention("fox", R["ot1"])
            turn_outputs(R["ot1"], 4, OT1[:, 1:QT + 1, :])
            with pe.Fori(0, 4) as i:
                for m in range(2):
                    n, r = U["merge"] + 4 * m, R["merge"] + 6 * m
                    for g in range(3):
                        unit(n + i * 8 + g, (n + g) % SPLIT, r + i * 12 + g, (r + g) % PAIRS, T2, x_of(T2))
                    pe.wait_ge(hid_ready, HID0["merge"])
                    pe.wait_ge(ev_used, E0["merge"])
                    for b, (k0, k1) in enumerate(((0, 2), (2, 4), (4, 8))):
                        unit(n + i * 8 + 3, (n + 3) % SPLIT, r + i * 12 + 3 + b, (r + 3 + b) % PAIRS, T2,
                             lambda k: (o_hi(k0 + k, T2), o_lo(k0 + k, T2)), chunks=range(k0, k1), ends=b == 2)
            residual("wo1", T2, lambda k: (m_hi(k, T2), m_lo(k, T2)), (hid_ready, HID0["merge"]))
            n, r = U["router"], R["router"]
            unit(n, n % SPLIT, r, r % PAIRS, T2, x_of(T2), (x_ready, X0["n2"]))
            gathered_sum("n2", T2)
            n, r = U["moe"], R["moe_a"]
            unit(n, n % SPLIT, r, r % PAIRS, T2, x_of(T2))
            pe.wait_ge(scaled, 1)
            turn(R["routerT"], spare(0, T2), T2)
            for j in range(1, HEAD):
                n, r = U["moe"] + j, R["moe_b"] + j - 1
                unit(n, n % SPLIT, r, r % PAIRS, T2, x_of(T2))
            take_pair(R["combT"])
            pe.wait_ge(dve_ready, 7)
            for i in range(QT):
                mm = pe.transpose(pair(R["combT"])[0:N_EXP, 0, i * P:(i + 1) * P], route[:, 11, i, :], ident)
            mm.then_inc(lin_done, 1)
            pe.wait_ge(scaled, 2)
            for e in range(N_EXP):
                r = R["cb"] + e
                take_pair(r)
                pe.matmul(pair(r)[:, 0, :], ident[0:N_EXP, e:e + 1].to_broadcast([N_EXP, P]), SQ[0:N_EXP, 0, 0:T2],
                          start=True, stop=True).then_inc(lin_done, 1)

            def group_units(i, first):
                n, r = U["moe"], R["moe"] - HEAD
                for j in range(first, 16):
                    unit(n + i * 24 + j, (n + j) % SPLIT, r + i * 24 + j, (r + j) % PAIRS, T2, x_of(T2))
                for j in range(16, 24):
                    unit(n + i * 24 + j, (n + j) % SPLIT, r + i * 24 + j, (r + j) % PAIRS, T2,
                         lambda k: (o_hi(k, T2), o_lo(k, T2)), ready=(hid_ready, i * C + HID0["moe"]) if j == 16 else None)

            group_units(0, HEAD)
            with pe.Fori(1, N_GRP) as i:
                group_units(i, 0)
            for c in range(2):
                n, r = U["kc"] + c, R["kc"] + c
                unit(n, n % SPLIT, r, r % PAIRS, T2, x_of(T2), None if c else (x_ready, X0["na0"]))
            take_pair(R["nf1"])
            pe.wait_ge(two_added, 2 * C - 1)
            for o, sums in enumerate((SQ[:, 0, 0:T2], TS[:, 2, 0:T2])):
                pe.matmul(pair(R["nf1"])[:, o, 0:T2], const("ones"), sums, start=True, stop=True).then_inc(sq_used, 1)
            for c in range(2):
                n, r = U["vc"] + c, R["vc"] + c
                unit(n, n % SPLIT, r, r % PAIRS, T2, x_of(T2))
            token_units(U["gl"], R["tok2"], 5, T2, x_of(T2), 0, 6)
            for kv in range(2):
                pe.wait_ge(dve_ready, 8 + kv)
                r = R["cmp"] + 3 * kv
                for m in range(2):
                    take_pair(r + m)
                    for part in range(2):
                        n = U["cmp"] + 4 * kv + 2 * m + part
                        pe.wait_ge(split_ready, n + 1)
                        for k in range(KC):
                            b = part * KC + k
                            mm = three([pair(r + m)[:, 0, 0:A_G * NC]], n % SPLIT, k, [(BLKH[:, b, :], BLKL[:, b, :])],
                                       part == 0 and k == 0, part == 1 and k == KC - 1)
                        mm.then_inc(unit_used, 1)
                take_pair(r + 2)
                pe.wait_ge(lin_free, r + 2)
                if kv == 0:
                    for gp in range(2):
                        for odd in range(2):
                            g = 2 * gp + odd
                            for j in range(2):
                                mm = pe.matmul(pair(r + 2)[:, 0, gp * NC:(gp + 1) * NC], const("w2k", P, start=(2 * j + odd) * P),
                                               HIDC[:, j, g * NC:(g + 1) * NC], start=odd == 0 and j == 0, stop=odd == 1 and j == 1)
                else:
                    for g in range(A_G):
                        for j in range(2):
                            mm = pe.matmul(pair(r + 2)[0:NC, 0, g * HD:(g + 1) * HD], HIDC[:, j, g * NC:(g + 1) * NC],
                                           const("w2v", HD, start=j * HD), start=j == 0, stop=j == 1)
                mm.then_inc(lin_done, 1)
            rotate(E0["cmp"], R["cmp"] + 6, 2 * NC)
            rope_chunks(U["ks"], R["rope2"], E0["rope2"], 12, x_of(T2))
            pe.wait_ge(rope_ready, ROPE0["rope2"] + 4)
            attention("nsa0", R["wo2"])
            attention("nsa1", R["wo2"])
            residual("wo2", T2, lambda k: (o_hi(k, T2), o_lo(k, T2)), (o_ready, O0["nsa0"], 2 * QT))
            ffn(0, "nf0")
            rope_chunks(U["q3"], R["q3"], E0["q3"], 8, x_of(T2), (x_ready, X0["na1"]), "na1")
            r = R["kv3"]
            pe.wait_ge(x_ready, X0["kv"] + C)
            for x, n in enumerate((U["k3"], U["v3"])):
                unit(n, n % SPLIT, r + x, (r + x) % PAIRS, T2, lambda k: (o_hi(k, T2), o_lo(k, T2)))
            pe.wait_ge(lin_free, r + 1)
            rotate(E0["k3"], r + 2)
            pe.wait_ge(scaled, 12)
            turn(r + 3, VFM[:, :], T2)
            pe.wait_ge(rope_ready, ROPE0["k3"] + 1)
            pe.wait_ge(mask_ready, 4)
            attention("swa", R["wo3"])
            residual("wo3", T2, lambda k: (o_hi(k, T2), o_lo(k, T2)), (o_ready, O0["swa"], 2 * QT))
            ffn(1, "nf_1")
            gathered_sum("nfin", T2)

        @block.scalar
        def _(act):
            def by_unit(n):
                act.wait_ge(unit_used, n + 1)

            def alone(l):
                act.wait_ge(lin_done, l + 1)

            def result(rslot, t):
                return PS[:, 2 * rslot:2 * rslot + 2, 0:HALF] if t == T1 else PS[:, 2 * rslot, :]

            def shaped(ap, t):
                return halves(ap) if t == T1 else ap

            def evacuate(rslot, dst, t, func=ACT.Copy, **more):
                act.activation(shaped(dst, t), result(rslot, t), func, **more).then_inc(lin_free, 1)

            def stage(rslot, e, eslot, t, func=ACT.Copy, back=EV_SLOTS - 1, **more):
                if not isinstance(e, int) or e - back > 0:
                    act.wait_ge(ev_used, e - back)
                evacuate(rslot, EV[:, eslot, 2:2 + t], t, func, **more)

            def squares(stage_, src, ready, count=C):
                for c in range(count):
                    s = SQ0[stage_] + c
                    if ready is not None:
                        act.wait_ge(ready[0], ready[1] + c + 1)
                    if s >= 2:
                        act.wait_ge(sq_used, S0[stage_] + c - 1)
                    ap = src(c)
                    act.activation(SQ[:, s % 2, 0:ap.shape[1]], ap, ACT.Square).then_inc(sq_ready, 1)

            def root_table():
                act.activation(one_root[:, :], vec("one"), ACT.Sqrt)

            def exp_table():
                act.activation(one_exp[:, :], vec("one"), ACT.Exp)

            def root(stage_, r, t, width):
                act.wait_ge(sq_used, S0[stage_] + SUMS[stage_])
                act.activation(shaped(TS[:, 2, 0:t], t), result(r % PAIRS, t), ACT.Sqrt, bias=vec("eps"), scale=1.0 / width)\
                   .then_inc(lin_free, 1)

            def high_parts(count0, t, hi):
                for c in range(C):
                    act.wait_ge(y_ready, count0 + c + 1)
                    act.activation(hi(c), TS[:, c % 2, 0:t], ACT.Copy).then_inc(hi_ready, 1)

            def x_hi(t):
                return lambda c: XH[:, c, T1 - t:T1]

            def token_results(n0, r0, l0, count, t, spare0, keep):
                for x, (c, turned_) in enumerate(turning_order(count)):
                    if turned_:
                        alone(l0 + c)
                        keep(c, pair(r0 + x))
                    else:
                        by_unit(n0 + c)
                        evacuate((r0 + x) % PAIRS, spare(spare0 + c, t), t)

            def stage_queries(kind, i, half):
                body = len(ITEMS[kind])
                if exists(kind, i, -1) or kind == "nsa1":
                    act.wait_ge(s_done, number(kind, i, half * body // 2 - body // 2))
                q = chunk_queries(kind, i)
                rows = slice(half * HD, (half + 1) * HD)
                act.activation(QSTAGE[rows, half, 0:q.shape[-1]], q[rows, :], ACT.Copy).then_inc(q_staged, 1)

            def attention(kind, following=None):
                body, depth, lag = len(ITEMS[kind]), DEPTH[kind], LAG[kind]
                extra = 1 if kind == "swa" else 0

                last = CHUNKS[kind] - 1

                def step(i, n):
                    if n == body // 2 - 2:
                        stage_queries(kind, i, 1)
                    if n == body // 2 + 1 and not (isinstance(i, int) and i == last):
                        stage_queries(kind, i + 1, 0)
                    if n == body // 2 + 1 and isinstance(i, int) and i == last and following:
                        stage_queries(following, 0, 0)
                    if exists(kind, i, n - 1):
                        a = number(kind, i, n - 1)
                        c, m = home(kind, i, n - 1)
                        keys = keys_of(kind, c, m)[1]
                        act.wait_ge(max_ready, a + 1)
                        if exists(kind, i, n - 1 - depth):
                            act.wait_ge(t_done, a + (1 - depth))
                        act.activation(probs(kind, m)[:, 0:keys + extra], scores(kind, m)[:, 0:keys + extra], ACT.Exp,
                                       bias=stat[:, 0, m:m + 1], accum_out=stat[:, 1, m:m + 1]).then_inc(p_ready, 1)
                    if exists(kind, i, n - lag):
                        a = number(kind, i, n - lag)
                        _, m = home(kind, i, n - lag)
                        act.wait_ge(t_done, a + 1)
                        if exists(kind, i, n - lag - 2):
                            act.wait_ge(o_done, a + -1)
                        tiles = key_tiles(kind, m)
                        if tiles[-1][2] is None:
                            cp = act.activation(turned_copy(m, P, None)[0:META, :], meta_turned(m), ACT.Copy)
                            tiles = tiles[:-1]
                        if tiles:
                            height, wide = tiles[0][1], len(tiles) * P
                            cp = act.activation(turned_copy(m, wide, 0)[0:height, :], turned(m)[0:height, 0:wide], ACT.Copy)
                        cp.then_inc(pt_ready, 1)
                    if kind != "fox" and exists(kind, i, n - lag - 2):
                        a = number(kind, i, n - lag - 2)
                        c, m = home(kind, i, n - lag - 2)
                        if kind == "swa" or m % 3 == 2:
                            rows, col = out_place(kind, c, m)
                            act.wait_ge(o_done, a + 1)
                            act.activation(HIDH[rows, bass.ds(col, P)], outs(kind, m)[rows, 0:P], ACT.Copy).then_inc(o_hi_ready, 1)

                for n in range(body):
                    step(0, n)
                with act.Fori(1, last) as i:
                    for n in range(body):
                        step(i, n)
                for n in range(body + lag + 2):
                    step(last, n)

            def turned_outputs(stage_, count):
                for c in range(count):
                    r, e = R[stage_] + c, E0[stage_] + c
                    alone(L0[stage_] + c)
                    if e >= EV_SLOTS:
                        act.wait_ge(ev_used, e - (EV_SLOTS - 1))
                    act.activation(staged(e, T2), pair(r)[:, 0, :], ACT.Copy).then_inc(lin_free, 1)

            def residual(name, t, norm, units=1, scaled=False):
                root_table()
                for c in range(C):
                    by_unit(U[name] + units * c + units - 1)
                    stage((R[name] + c) % PAIRS, E0[name] + c, (E0[name] + c) % EV_SLOTS, t)
                    act.wait_ge(ev_used, E0[name] + c + 1)
                    if c >= 2:
                        act.wait_ge(sq_added, ADD0[norm] + c - 1)
                    act.activation(SQ[:, min(c, 1), 0:t], H[:, c, T1 - t:T1], ACT.Square).then_inc(sq_ready, 1)
                    if scaled:
                        act.wait_ge(y_ready, X0[norm] + c + 1)
                        act.activation(XH[:, c, T1 - t:T1], TS[:, c % 2, 0:t], ACT.Copy).then_inc(hi_ready, 1)

            def ffn(layer):
                e0 = E0[f"ffn{layer}_in"]
                with act.Fori(0, FC // 2) as i:
                    for j in range(2):
                        act.wait_ge(ev_used, e0 + i * 4 + 2 * j + 1)
                        act.activation(SQ[:, j, 0:T2], SQ[:, j, 0:T2], ACT.Silu).then_inc(act_done, 1)
                residual(f"ffn{layer}_out", T2, ("na1", "nfin")[layer], 3, scaled=layer == 0)

            def rope_results(name, n0, count, scale_from, between=None):
                r0, e0 = R[name], E0[name]
                order = [(0, False)]
                for c in range(1, count):
                    order += [(c, False), (c - 1, True)]
                order.append((count - 1, True))
                for n, (c, turned_) in enumerate(order):
                    if turned_:
                        alone(L0[name] + c)
                        stage((r0 + n) % PAIRS, e0 + n, (e0 + n) % EV_SLOTS, T2, back=3 if c < count - 1 else 2)
                        if between:
                            between(c)
                    else:
                        by_unit(n0 + c)
                        stage((r0 + n) % PAIRS, e0 + n, (e0 + n) % EV_SLOTS, T2, back=1 if n else 0,
                              scale=SCALE if c >= scale_from else 1.0)

            act.wait_ge(vecs_loaded, 16)
            act.wait_ge(pads_zeroed, 7)
            root_table()
            for c in range(C):
                act.wait_ge(x_loaded[c // 2], 16)
                if c > 3:
                    act.wait_ge(sq_added, ADD0["n1"] + c - 3)
                act.activation(first_squares(c), H[:, c, :], ACT.Square).then_inc(sq_ready, 1)
            root("n1", R["n1"], T1, D)
            high_parts(X0["n1"], T1, x_hi(T1))
            r, n = R["in1"], U["pool"]
            for c in range(6):
                by_unit(n + c)
                if c < 2:
                    evacuate((r + c) % PAIRS, apad[:, c, 16:16 + T1], T1)
                elif c < 4:
                    evacuate((r + c) % PAIRS, glu[:, c - 2, KS - 1:KS - 1 + T1], T1)
                else:
                    evacuate((r + c) % PAIRS, sig[:, c - 4, :], T1, ACT.Sigmoid)
            by_unit(U["fg"])
            act.activation(halves(staged(0, T1)[0:FOX_H, :]), pair(r + 6)[0:FOX_H, :, 0:HALF], ACT.Identity,
                           bias=vec("bforget")[0:FOX_H, :]).then_inc(lin_free, 1)
            act.wait_ge(lin_free, r + 7)
            act.activation(staged(1, T1)[0:FOX_H, :], staged(0, T1)[0:FOX_H, :], ACT.Abs).then_inc(act_step, 1)
            act.wait_ge(act_step, 1)
            act.activation(staged(3, T1)[0:FOX_H, :], staged(1, T1)[0:FOX_H, :], ACT.Exp, scale=-1.0).then_inc(act_step, 1)
            act.wait_ge(act_step, 2)
            act.activation(staged(1, T1)[0:FOX_H, :], staged(3, T1)[0:FOX_H, :], ACT.Ln, bias=vec("one")[0:FOX_H, :])\
               .then_inc(act_done, 1)
            for c in range(4):
                by_unit(U["q1"] + c)
                evacuate((r + 7 + c) % PAIRS, Q1[:, c, :], T1, scale=SCALE)
            for c in range(2):
                alone(L0["pool"] + c)
                evacuate((R["pool"] + c) % PAIRS, apad[:, c, 16:16 + T1], T1, ACT.Identity, bias=vec("pool_b", c))

            def keep_v1(c, ps):
                act.activation(V1[0:META, 0, c * P:(c + 1) * P], ps[0:META, 1, 0:P], ACT.Copy)
                act.activation(V1[:, 1:QT + 1, c * P:(c + 1) * P], ps[:, 0, :].rearrange("p (i n) -> p i n", i=QT), ACT.Copy)\
                   .then_inc(lin_free, 1)

            token_results(U["v1"], R["v1"], L0["v1"], 4, T1, 4, keep_v1)
            alone(L0["ln"])
            evacuate(R["ln"] % PAIRS, TS[:, 2, :], T1, scale=-1.0 / CONV_W)
            squares("ln", lambda c: sig[:, c, :], (act_asked, 0), 2)
            by_unit(U["k1"])
            evacuate(R["k1a"] % PAIRS, K1[:, 0, :], T1)
            root("ln", R["lnv"], T1, CONV_W)
            by_unit(U["k1"] + 1)
            evacuate(R["k1b"] % PAIRS, K1[:, 1, :], T1)
            for c in range(2):
                act.wait_ge(act_asked, 3 + c)
                act.activation(sig[:, c, :], sig[:, c, :], ACT.Silu, bias=vec("ln_b", c)).then_inc(act_done, 1)
            act.wait_ge(hid_ready, HID0["merge"])
            act.wait_ge(dve_ready, 5)
            act.wait_ge(zeros_written, 1)
            for part in range(2):
                act.dma_start(NF[part:part + 1, :, :].bitcast(F32), staged(part, T1)[0:FOX_H, :]).then_inc(rows_moved, 16)
            exp_table()
            act.wait_ge(zeros_written, 3)
            stage_queries("fox", 0, 0)
            for c in range(2, 4):
                by_unit(U["k1"] + c)
                evacuate((R["k1b"] + c - 1) % PAIRS, K1[:, c, :], T1)
            attention("fox")
            turned_outputs("ot1", 4)
            with act.Fori(0, 4) as i:
                n, r, e = U["merge"], R["merge"], E0["merge"]
                for j in range(12):
                    m, k = j // 6, j % 6
                    if k in (3, 4):
                        alone(L0["merge"] + i * 4 + 2 * m + k - 3)
                    else:
                        by_unit(n + i * 8 + 4 * m + min(k, 3))
                    stage((r + j) % PAIRS, e + i * 12 + j, (e + j) % EV_SLOTS, T2, ACT.Sigmoid if k < 3 else ACT.Copy)
            residual("wo1", T2, "n2", scaled=True)
            root("n2", R["n2"], T2, D)
            by_unit(U["router"])
            evacuate(R["router"] % PAIRS, spare(0, T2), T2)

            def stage_expert(i, j, r0):
                e = E0["moe"]
                if j < 16 and j % 2 == 0:
                    act.wait_ge(lin_free, r0 + i * 24 + j + 1)
                    gate = EV[:, (e + j) % EV_SLOTS, 2:2 + T2]
                    act.activation(gate, gate, ACT.Silu).then_inc(silu_done, 1)
                else:
                    by_unit(U["moe"] + i * 24 + j)
                    stage((r0 + j) % PAIRS, e + i * 24 + j, (e + j) % EV_SLOTS, T2)

            stage_expert(0, 0, R["moe_a"])
            alone(L0["routerT"])
            r = R["routerT"]
            for slot, a, w in ((0, 0, N_GRP), (1, N_GRP, N_EXP)):
                cp = act.activation(route[:, slot, :, 0:w],
                                    pair(r)[:, 0, :].rearrange("p (i n) -> p i n", i=QT)[:, :, a:a + w], ACT.Copy)
            cp.then_inc(lin_free, 1)
            stage_expert(0, 1, R["moe_b"] - 1)
            act.wait_ge(act_asked, 5)
            act.activation(route[:, 4, :, 0:8], route[:, 3, :, 0:8], ACT.Exp).then_inc(act_done, 1)
            for j in range(2, HEAD):
                stage_expert(0, j, R["moe_b"] - 1)
            r = R["combT"]
            alone(L0["combT"])
            act.activation(SQ[0:N_EXP, 0, 0:T2], pair(r)[0:N_EXP, 0, :], ACT.Copy).then_inc(lin_free, 1)
            for e in range(N_EXP):
                alone(L0["cb"] + e)
                evacuate((R["cb"] + e) % PAIRS, CB[:, e, :], T2)
            for j in range(HEAD, 24):
                stage_expert(0, j, R["moe"] - HEAD)
            with act.Fori(1, N_GRP - 1) as i:
                for j in range(24):
                    stage_expert(i, j, R["moe"] - HEAD)
            for j in range(24):
                stage_expert(N_GRP - 1, j, R["moe"] - HEAD)
                if j >= 16:
                    c = j - 16
                    if c == 0:
                        root_table()
                    act.wait_ge(ev_used, E0["moe"] + (N_GRP - 1) * 24 + 16 + c + 1)
                    if c >= 2:
                        act.wait_ge(two_added, 2 * c - 1)
                    act.activation(SQ[:, min(c, 1), 0:T2], H[:, c, META:T1], ACT.Square).then_inc(sq_ready, 1)
                    act.wait_ge(y_ready, X0["na0"] + c + 1)
                    act.activation(XH[:, c, META:T1], TS[:, c % 2, 0:T2], ACT.Copy).then_inc(hi_ready, 1)
            for c in range(4):
                r = R["kc"] + c if c < 2 else R["vc"] + c - 2
                if c == 2:
                    act.wait_ge(sq_used, S0["nf1"] + 2)
                    act.activation(TS[:, 2, 0:T2], pair(R["nf1"])[:, 0, :], ACT.Sqrt, bias=vec("eps"), scale=1.0 / D).then_inc(act_done, 1)
                    act.wait_ge(act_asked, 6)
                    act.activation(TS[:, 0, 0:T2], TS[:, 0, 0:T2], ACT.Sqrt, bias=vec("eps")).then_inc(act_done, 1)
                by_unit(U["kc"] + c)
                act.activation(EO[:, c, :, :], pair(r)[:, 0, :].rearrange("p (n a) -> p a n", a=2), ACT.Copy).then_inc(lin_free, 1)
            act.wait_ge(scaled, 6)
            for par in range(2):
                for g2 in range(2):
                    act.dma_start(PAIR[par * HD:(par + 1) * HD, :, g2, :], EO[g2 * HD:(g2 + 1) * HD, :, par, :])\
                       .then_inc(pairs_moved, 16)

            def keep_tok2(c, ps):
                tiles = ps[:, 0, :].rearrange("p (i n) -> p i n", i=QT)
                if c == 0:
                    act.activation(gate48[:, :, :], tiles[:, :, 0:3 * NH], ACT.Sigmoid).then_inc(lin_free, 1)
                else:
                    v, half = (VSEL, VWIN)[(c - 1) // 2], (c - 1) % 2
                    act.activation(v[:, :, half * P:(half + 1) * P], tiles, ACT.Copy).then_inc(lin_free, 1)

            token_results(U["gl"], R["tok2"], L0["tok2"], 5, T2, 0, keep_tok2)
            for kv in range(2):
                r = R["cmp"] + 3 * kv
                for m in range(2):
                    by_unit(U["cmp"] + 4 * kv + 2 * m + 1)
                    act.activation(HIDC[:, m, :], pair(r + m)[:, 0, 0:A_G * NC], ACT.Gelu_apprx_tanh).then_inc(lin_free, 1)
                alone(L0["cmp"] + kv)
                if kv == 0:
                    act.wait_ge(ev_used, E0["cmp"])
                    act.activation(staged(E0["cmp"], 2 * NC), pair(r + 2)[:, 0, 0:2 * NC], ACT.Copy).then_inc(lin_free, 1)
                else:
                    act.activation(VCMP[0:NC, :, :], pair(r + 2)[0:NC, 0, 0:A_G * HD].rearrange("p (g d) -> p g d", g=A_G), ACT.Copy)\
                       .then_inc(lin_free, 1)
            alone(L0["cmp"] + 2)
            act.activation(staged(E0["cmp"] + 1, 2 * NC), pair(R["cmp"] + 6)[:, 0, 0:2 * NC], ACT.Copy).then_inc(lin_free, 1)
            exp_table()
            rope_results("rope2", U["ks"], 12, 4)
            act.wait_ge(zeros_written, 5)
            act.wait_ge(rope_ready, ROPE0["rope2"] + 4 + CHUNKS["nsa0"] + 1)
            stage_queries("nsa0", 0, 0)
            attention("nsa0", "nsa1")
            act.wait_ge(rope_ready, ROPE0["q3"])
            attention("nsa1")
            residual("wo2", T2, "nf0", scaled=True)
            root("nf0", R["nf0"], T2, D)
            ffn(0)
            root("na1", R["na1"], T2, D)

            def kv_high(c):
                for x in kv_chunks(c):
                    act.wait_ge(y_ready, X0["kv"] + x + 1)
                    act.activation(o_hi(x, T2), TS[:, x % 2, 0:T2], ACT.Copy).then_inc(hi_ready, 1)

            exp_table()
            rope_results("q3", U["q3"], 8, 0, kv_high)
            r, e = R["kv3"], E0["k3"]
            by_unit(U["k3"])
            stage(r % PAIRS, e, e % EV_SLOTS, T2, back=0)
            alone(L0["k3"])
            stage((r + 2) % PAIRS, e + 1, (e + 1) % EV_SLOTS, T2, back=1)
            act.wait_ge(zeros_written, 7)
            act.wait_ge(rope_ready, ROPE0["q3"] + 8)
            stage_queries("swa", 0, 0)
            alone(L0["v3"])
            act.activation(V3[:, :, :], pair(r + 3)[:, 0, :].rearrange("p (i n) -> p i n", i=QT), ACT.Copy).then_inc(lin_free, 2)
            attention("swa")
            residual("wo3", T2, "nf_1", scaled=True)
            root("nf_1", R["nf_1"], T2, D)
            ffn(1)
            root("nfin", R["nfin"], T2, D)

        @block.vector
        def _(dve):
            steps = [0]

            def then(ins):
                steps[0] = steps[0] + 1
                ins.then_inc(dve_step, 1)
                dve.wait_ge(dve_step, steps[0])

            def parts(src, hi, lo):
                then(dve.tensor_copy(hi, src))
                return dve.tensor_tensor(lo, src, hi.bitcast(F32), ALU.subtract)

            def reciprocal_root(r, t):
                dve.wait_ge(lin_free, r + 1)
                then(dve.reciprocal(TS[:, 2, 0:t], TS[:, 2, 0:t]))

            def normed(gain, count0, t, hi, lo, used):
                if used:
                    dve.wait_ge(unit_used, used)
                for c in range(C + 1):
                    if c < C:
                        if count0 + c >= 2:
                            dve.wait_ge(x_ready, count0 + c - 1)
                        dve.scalar_tensor_tensor(out=TS[:, c % 2, 0:t], in0=H[:, c, T1 - t:T1], scalar=vec(gain, c), in1=TS[:, 2, 0:t],
                                                 op0=ALU.mult, op1=ALU.mult).then_inc(y_ready, 1)
                    if c:
                        dve.wait_ge(hi_ready, count0 + c)
                        dve.tensor_tensor(lo(c - 1), TS[:, (c - 1) % 2, 0:t], hi(c - 1).bitcast(F32), ALU.subtract).then_inc(x_ready, 1)

            def normed_in_place(gain, root_, chunks=range(C)):
                for c in chunks:
                    dve.scalar_tensor_tensor(out=H[:, c, META:T1], in0=H[:, c, META:T1], scalar=vec(gain, c), in1=root_,
                                             op0=ALU.mult, op1=ALU.mult).then_inc(h_ready, 1)

            def x_hi(t):
                return lambda c: XH[:, c, T1 - t:T1]

            def x_lo(t):
                return lambda c: XL[:, c, T1 - t:T1]

            def residual(name, t, norm, gain=None):
                if gain:
                    dve.wait_ge(unit_used, U[name])
                def add_squares(c):
                    dve.wait_ge(sq_ready, SQ0[norm] + c + 1)
                    if c > 1:
                        dve.wait_ge(sq_added, ADD0[norm] + c - 1)
                    dve.tensor_tensor(SQ[:, 0, 0:t], SQ[:, 0, 0:t], SQ[:, 1, 0:t], ALU.add).then_inc(sq_added, 1)

                for c in range(C):
                    dve.wait_ge(lin_free, R[name] + c + 1)
                    h = H[:, c, T1 - t:T1]
                    dve.tensor_tensor(h, h, staged(E0[name] + c, t), ALU.add).then_inc(ev_used, 1)
                    if c >= 2:
                        add_squares(c - 1)
                    if gain:
                        x = X0[norm] + c
                        dve.wait_ge(ev_used, E0[name] + c + 1)
                        dve.wait_ge(x_ready, x - 1)
                        dve.tensor_scalar(TS[:, c % 2, 0:t], h, vec(gain, c), None, ALU.mult).then_inc(y_ready, 1)
                        dve.wait_ge(hi_ready, x + 1)
                        dve.tensor_tensor(XL[:, c, T1 - t:T1], TS[:, c % 2, 0:t], XH[:, c, T1 - t:T1].bitcast(F32),
                                          ALU.subtract).then_inc(x_ready, 1)

            def attention(kind):
                body, lag = len(ITEMS[kind]), LAG[kind]
                nsa = kind in ("nsa0", "nsa1")
                late = lag + (2 if kind == "fox" else 3)

                def step(i, n):
                    if exists(kind, i, n - late):
                        a = number(kind, i, n - late)
                        c, m = home(kind, i, n - late)
                        half, t = ITEMS[kind][m][0:2]
                        if kind == "fox":
                            rows = META if t == 0 else P
                            dve.wait_ge(o_done, a + 1)
                            dve.wait_ge(sum_inverted, a + 1)
                            dve.tensor_scalar(OT1[0:rows, t, bass.ds(at(c, P, half * HD), HD)], outs(kind, m)[0:rows, 0:HD],
                                              stat[0:rows, 2, m:m + 1], None, ALU.mult).then_inc(o_ready, 1)
                        elif kind == "swa" or m % 3 == 2:
                            rows, col = out_place(kind, c, m)
                            per = len(ITEMS[kind]) if kind == "swa" else len(ITEMS[kind]) // 3
                            dve.wait_ge(o_hi_ready, at(c, per, O0[kind] - O0["nsa0"] + (m if kind == "swa" else m // 3) + 1))
                            dve.tensor_tensor(HIDL[rows, bass.ds(col + low, P)], outs(kind, m)[rows, 0:P],
                                              HIDH[rows, bass.ds(col, P)].bitcast(F32), ALU.subtract).then_inc(o_ready, 1)
                    if exists(kind, i, n):
                        a = number(kind, i, n)
                        half, t = ITEMS[kind][n][0:2]
                        keys = keys_of(kind, i, n)[1]
                        s = scores(kind, n)
                        width = META if kind == "fox" and t == 0 else P
                        own = s[:, keys - width:keys]
                        dve.wait_ge(s_done, a + 1)
                        if kind == "fox":
                            dve.tensor_tensor(own, own, const("causal", width), ALU.add).then_inc(masked, 1)
                        elif kind == "swa":
                            dve.tensor_scalar(s[:, keys:keys + 1], vecs[:, bass.ds(at(i, 1, V0["sink"] + half * 8), 1)], vec("one"), None, ALU.mult)\
                               .then_inc(masked, 1)
                        elif ITEMS[kind][n][2] == 0:
                            dve.tensor_tensor(s[:, 0:NC], s[:, 0:NC], const("cmask", NC, start=t * NC), ALU.add).then_inc(masked, 1)
                        else:
                            dve.tensor_tensor(own, own, const("causal"), ALU.add).then_inc(masked, 1)
                    if exists(kind, i, n - 2):
                        a = number(kind, i, n - 2)
                        c, m = home(kind, i, n - 2)
                        dve.wait_ge(p_ready, a + 1)
                        dve.reciprocal(stat[:, 2, m:m + 1], stat[:, 1, m:m + 1]).then_inc(sum_inverted, 1)
                    if exists(kind, i, n):
                        per = MASKS[kind]
                        dve.wait_ge(masked, number(kind, i, n, per, M0) + per)
                        seen = keys + (kind == "swa")
                        dve.tensor_reduce(stat[:, 0, n:n + 1], s[:, 0:seen], AX, ALU.max, negate=True).then_inc(max_ready, 1)
                    if kind != "fox" and exists(kind, i, n - 2):
                        a = number(kind, i, n - 2)
                        c, m = home(kind, i, n - 2)
                        dve.wait_ge(sum_inverted, a + 1)
                        if exists(kind, i, n - 2 - 4):
                            dve.wait_ge(t_done, a + -3)
                        gate = None
                        if nsa:
                            half, t, b = ITEMS[kind][m]
                            gate = gate48[:, t, bass.ds(at(c, 3, (2 * int(kind[3]) + half) * 12 + b), 1)]
                        dve.tensor_scalar(weights(m), ident, stat[:, 2, m:m + 1], gate, ALU.mult, *([ALU.mult] if nsa else []))\
                           .then_inc(weigh_ready, 1)

                for n in range(body):
                    step(0, n)
                with dve.Fori(1, CHUNKS[kind]) as i:
                    for n in range(body):
                        step(i, n)
                for n in range(body, body + lag + 3):
                    step(CHUNKS[kind] - 1, n)

            def zero_other_heads():
                dve.memset(QSTAGE[HD:P, 0, :], 0.0).then_inc(zeros_written, 1)
                dve.memset(QSTAGE[0:HD, 1, :], 0.0).then_inc(zeros_written, 1)

            def feature_parts(stage_, count, t, first):
                for c in range(count):
                    dve.wait_ge(lin_free, R[stage_] + c + 1)
                    parts(staged(E0[stage_] + c, t), o_hi(first + c, t), o_lo(first + c, t)).then_inc(ev_used, 1)

            def rotated(stage_, count, dest, cos, sin, between=None):
                r0, e0 = R[stage_], E0[stage_]
                for c in range(count):
                    at = 2 * c - (1 if c else 0)
                    rot = 2 * c + 2 if c < count - 1 else 2 * count - 1
                    dve.wait_ge(lin_free, r0 + rot + 1)
                    dve.wait_ge(rope_ready, ROPE0[stage_] + c)
                    if between and c:
                        dve.wait_ge(x_ready, X0["kv"] + KV_CHUNKS[c])
                    dve.tensor_tensor(TS[:, 0, 0:T2], staged(e0 + at, T2), cos, ALU.mult).then_inc(ev_used, 1)
                    dve.tensor_tensor(TS[:, 1, 0:T2], staged(e0 + rot, T2), sin, ALU.mult).then_inc(ev_used, 1)
                    dve.wait_ge(ev_used, e0 + 2 * c + 2)
                    dve.tensor_tensor(dest(c), TS[:, 0, 0:T2], TS[:, 1, 0:T2], ALU.add).then_inc(rope_ready, 1)
                    if between:
                        between(c)

            def ffn(layer):
                n0, r0, e0 = U[f"ffn{layer}_in"], R[f"ffn{layer}_in"], E0[f"ffn{layer}_in"]
                w0 = V0[f"fw{layer}"]
                before, per = steps[0], 2 * 6
                with dve.Fori(0, FC // 2) as i:
                    steps[0] = i * per + before
                    for j in range(2):
                        for m in (2 * j, 2 * j + 1):
                            slot = (e0 + m) % EV_SLOTS
                            w = [vecs[:, bass.ds(i * 16 + (w0 + 4 * m + q), 1)] for q in range(4)]
                            y = SQ[:, j, 0:T2] if m == 2 * j else TS[:, j, 0:T2]
                            dve.wait_ge(unit_used, n0 + i * 4 + m + 1)
                            dve.wait_ge(ev_used, e0 + i * 4 + m - 3)
                            dve.tensor_tensor(EV[:, slot, 2:2 + T2], PS[:, 2 * ((r0 + m) % PAIRS), :], TS[:, 2, 0:T2], ALU.mult)\
                               .then_inc(lin_free, 1)
                            dve.wait_ge(lin_free, r0 + i * 4 + m + 1)
                            then(dve.tensor_scalar(y, EV[:, slot, 2:2 + T2], w[2], w[3], ALU.mult, ALU.add))
                            then(dve.scalar_tensor_tensor(out=y, in0=EV[:, slot, 1:1 + T2], scalar=w[1], in1=y, op0=ALU.mult, op1=ALU.add))
                            dve.scalar_tensor_tensor(out=y, in0=EV[:, slot, 0:T2], scalar=w[0], in1=y, op0=ALU.mult, op1=ALU.add)\
                               .then_inc(ev_used, 1)
                        dve.wait_ge(act_done, DONE0[f"ffn{layer}"] + i * 2 + j + 1)
                        dve.wait_ge(ev_used, e0 + i * 4 + 2 * j + 2)
                        y = TS[:, j, 0:T2]
                        then(dve.tensor_tensor(y, y, SQ[:, j, 0:T2], ALU.mult))
                        parts(y, HIDH[:, bass.ds(i * (2 * SEQ) + j * SEQ, SEQ)], HIDL[:, bass.ds(i * (2 * SEQ) + j * SEQ, SEQ)])\
                            .then_inc(hid_ready, 1)
                steps[0] = before + per * (FC // 2)
                residual(f"ffn{layer}_out", T2, ("na1", "nfin")[layer], ("attn1", None)[layer])

            dve.wait_ge(vecs_loaded, 16)
            for loaded in x_loaded:
                dve.wait_ge(loaded, 16)
            dve.wait_ge(ones_loaded, 16)
            dve.wait_ge(pads_zeroed, 7)
            g1 = vecs[:, V0["final1"]:V0["final1"] + C]
            then(dve.tensor_tensor(gain_sq[:, :], g1, g1, ALU.mult))
            for c in range(1, C - 1):
                dve.wait_ge(sq_ready, SQ0["n1"] + c + 1)
                if c > 1:
                    dve.wait_ge(sq_added, ADD0["n1"] + c - 1)
                dve.tensor_tensor(SQ[:, 0, :], SQ[:, 0, :], first_squares(c), ALU.add).then_inc(sq_added, 1)
            reciprocal_root(R["n1"], T1)
            normed("norm1", X0["n1"], T1, x_hi(T1), x_lo(T1), 0)
            a, b = 16, 16 + T1
            dve.wait_ge(inv_loaded, 16)
            dve.wait_ge(lin_free, R["in1"] + 2)
            then(dve.tensor_tensor(sum2[:, :, a:b], apad[:, :, a:b], apad[:, :, a - 1:b - 1], ALU.add))
            then(dve.tensor_tensor(sum4[:, :, a:b], sum2[:, :, a:b], sum2[:, :, a - 2:b - 2], ALU.add))
            then(dve.tensor_tensor(sum8[:, a:b], sum4[:, 1, a:b], sum4[:, 1, a - 4:b - 4], ALU.add))
            then(dve.tensor_tensor(sum2[:, 1, a:b], sum8[:, a:b], sum8[:, a - 8:b - 8], ALU.add))
            for c, (low_, high) in enumerate(((sum2[0:HD, 0, a:b], sum4[HD:P, 0, a:b]), (sum8[0:HD, a:b], sum2[HD:P, 1, a:b]))):
                then(dve.tensor_tensor(TS[0:HD, c, :], low_, inv[0:HD, c, :], ALU.mult))
                then(dve.tensor_tensor(TS[HD:P, c, :], high, inv[HD:P, c, :], ALU.mult))
                dve.tensor_tensor(TS[:, c, :], TS[:, c, :], apad[:, c, a:b], ALU.subtract).then_inc(dve_ready, 1)
            dve.wait_ge(lin_free, R["in1"] + 6)
            g0 = KS - 1
            then(dve.tensor_tensor(glu[:, :, g0:g0 + T1], glu[:, :, g0:g0 + T1], sig[:, :, :], ALU.mult))
            for c in range(2):
                y = sig[:, c, :]
                then(dve.tensor_scalar(y, glu[:, c, 0:T1], vec("conv_w", c * KS), vec("conv_b", c), ALU.mult, ALU.add))
                for k in range(1, KS):
                    ins = dve.scalar_tensor_tensor(out=y, in0=glu[:, c, k:k + T1], scalar=vec("conv_w", c * KS + k), in1=y,
                                                   op0=ALU.mult, op1=ALU.add)
                    if k < KS - 1:
                        then(ins)
                ins.then_inc(dve_ready, 1)
            dve.wait_ge(act_done, DONE0["fg"] + 1)
            z, soft, total = (staged(e, T1)[0:FOX_H, :] for e in (0, 1, 2))
            then(dve.tensor_scalar(z, z, 0.0, None, ALU.min))
            then(dve.tensor_tensor(soft, soft, z, ALU.subtract))
            then(dve.tensor_tensor_scan(total, consts[0:FOX_H, C0["ones"]:C0["ones"] + 1].to_broadcast([FOX_H, T1]), soft, 0.0,
                                        ALU.mult, ALU.add))
            parts(total, z.bitcast(F32R), soft.bitcast(F32R)).then_inc(dve_ready, 1)
            dve.tensor_copy(ones2[:, :], const("ones")).then_inc(dve_ready, 1)
            for c in range(2):
                dve.wait_ge(lin_free, R["pool"] + c + 1)
                then(dve.tensor_scalar(apad[:, c, a:b], apad[:, c, a:b], vec("pool_s", c), None, ALU.mult))
                parts(apad[:, c, a + META:b], o_hi(c, T2), o_lo(c, T2)).then_inc(hid_ready, 1)
            dve.wait_ge(lin_free, R["ln"] + 1)
            for c in range(2):
                dve.tensor_tensor(sig[:, c, :], sig[:, c, :], TS[:, 2, :], ALU.add).then_inc(act_asked, 1)
            dve.wait_ge(hid_ready, 2)
            dve.memset(NF[:, :, :].bitcast(F32), 0.0).then_inc(zeros_written, 1)
            reciprocal_root(R["lnv"], T1)
            zero_other_heads()
            for c in range(2):
                dve.scalar_tensor_tensor(out=sig[:, c, :], in0=sig[:, c, :], scalar=vec("ln_g", c), in1=TS[:, 2, :],
                                         op0=ALU.mult, op1=ALU.mult).then_inc(act_asked, 1)
            for c in range(2):
                dve.wait_ge(act_done, DONE0["ln"] + c + 1)
                parts(sig[:, c, META:T1], o_hi(2 + c, T2), o_lo(2 + c, T2)).then_inc(hid_ready, 1)

            dve.wait_ge(consts_loaded, 16)
            attention("fox")
            feature_parts("ot1", 4, T2, 4)
            with dve.Fori(0, 4) as i:
                for m in range(2):
                    r, e = R["merge"] + 6 * m, E0["merge"] + 6 * m
                    dve.wait_ge(hid_ready, HID0["merge"] + i * 2 + m)
                    for g in range(3):
                        dve.wait_ge(lin_free, r + i * 12 + 4 + g)
                        dve.tensor_tensor(TS[:, g, 0:T2], staged(e + g, T2), staged(e + 3 + g, T2), ALU.mult).then_inc(ev_used, 1)
                    dve.wait_ge(ev_used, e + i * 12 + 3)
                    dve.tensor_tensor(TS[:, 0, 0:T2], TS[:, 0, 0:T2], TS[:, 1, 0:T2], ALU.add).then_inc(ev_used, 1)
                    dve.wait_ge(ev_used, e + i * 12 + 4)
                    dve.tensor_tensor(TS[:, 0, 0:T2], TS[:, 0, 0:T2], TS[:, 2, 0:T2], ALU.add).then_inc(ev_used, 1)
                    dve.wait_ge(ev_used, e + i * 12 + 5)
                    hi = HIDH[:, bass.ds(i * (2 * T1) + (C + m) * T1, T2)]
                    lo = HIDL[:, bass.ds(i * (2 * T1) + (low - (C - m) * T1), T2)]
                    dve.tensor_copy(hi, TS[:, 0, 0:T2]).then_inc(ev_used, 1)
                    dve.wait_ge(ev_used, e + i * 12 + 6)
                    dve.tensor_tensor(lo, TS[:, 0, 0:T2], hi.bitcast(F32), ALU.subtract).then_inc(hid_ready, 1)
            residual("wo1", T2, "n2", "norm2")
            reciprocal_root(R["n2"], T2)

            def expert_gate(i, j, r0):
                e = E0["moe"]
                dve.wait_ge(unit_used, U["moe"] + i * 24 + 2 * j + 1)
                dve.wait_ge(ev_used, e + i * 24 + 2 * j - 3)
                rslot = (r0 + 2 * j) % PAIRS
                dve.tensor_tensor(staged(e + 2 * j, T2), PS[:, 2 * rslot, :], TS[:, 2, 0:T2], ALU.mult)\
                   .then_inc(lin_free, 1)

            dve.wait_ge(lin_free, R["router"] + 1)
            dve.tensor_tensor(spare(0, T2), spare(0, T2), TS[:, 2, 0:T2], ALU.mult).then_inc(scaled, 1)
            expert_gate(0, 0, R["moe_a"])
            dve.wait_ge(lin_free, R["routerT"] + 1)
            NTT = QT

            def wide(ap, n=4):
                return ap.unsqueeze(2).to_broadcast([P, NTT, n])

            def vec_rows(name, a, n):
                return vecs[:, V0[name] + a:V0[name] + a + n].unsqueeze(1).to_broadcast([P, NTT, n])

            glog, elog = route[:, 0, :, 0:4], route[:, 1, :, :]
            val = [route[:, 2, :, k] for k in range(10)]
            less, ex = route[:, 3, :, :], route[:, 4, :, :]
            prio = vec_rows("prio", 0, 4)

            def first_of(out_, src, top, best):
                then(dve.tensor_tensor(out_, src, wide(top), ALU.is_equal))
                then(dve.tensor_tensor(out_, out_, prio, ALU.mult))
                then(dve.tensor_reduce(best, out_, AX, ALU.max))
                then(dve.tensor_tensor(out_, out_, wide(best), ALU.is_equal))

            group, top1, top2, rest, w = (route[:, k, :, 0:4] for k in (5, 7, 8, 9, 10))
            then(dve.tensor_tensor(glog, glog, vec_rows("rbias", 0, 4), ALU.add))
            then(dve.tensor_tensor(elog, elog, vec_rows("rbias", 4, 16), ALU.add))
            then(dve.tensor_reduce(val[0], glog, AX, ALU.max))
            then(dve.tensor_tensor(less[:, :, 0:4], glog, wide(val[0]), ALU.subtract))
            first_of(group, glog, val[0], val[1])
            grid = route[:, 6, :, :].rearrange("p t (g e) -> p t g e", g=N_GRP)
            then(dve.tensor_tensor(grid, elog.rearrange("p t (g e) -> p t g e", g=N_GRP),
                                   group.unsqueeze(3).to_broadcast([P, NTT, N_GRP, PER_GRP]), ALU.mult))
            then(dve.tensor_reduce(rest, route[:, 6, :, :].rearrange("p t (g e) -> p t e g", g=N_GRP), AX, ALU.add))
            then(dve.tensor_reduce(val[2], rest, AX, ALU.max))
            dve.tensor_tensor(less[:, :, 4:8], rest, wide(val[2]), ALU.subtract).then_inc(act_asked, 1)
            dve.wait_ge(x_ready, X0["n2"] + C)
            dve.wait_ge(silu_done, 1)
            dve.wait_ge(lin_free, R["moe_b"] + 1)
            dve.tensor_tensor(TS[:, 0, 0:T2], staged(E0["moe"], T2), staged(E0["moe"] + 1, T2), ALU.mult).then_inc(ev_used, 1)
            dve.wait_ge(act_done, DONE0["router"] + 1)
            then(dve.tensor_reduce(val[3], ex[:, :, 0:4], AX, ALU.add))
            then(dve.tensor_reduce(val[4], ex[:, :, 4:8], AX, ALU.max))
            first_of(top1, ex[:, :, 4:8], val[4], val[5])
            then(dve.scalar_tensor_tensor(out=rest, in0=top1, scalar=-2.0, in1=ex[:, :, 4:8], op0=ALU.mult, op1=ALU.add))
            then(dve.tensor_reduce(val[6], rest, AX, ALU.max))
            first_of(top2, rest, val[6], val[7])
            then(dve.tensor_tensor(val[8], val[4], val[6], ALU.add))
            then(dve.tensor_tensor(val[8], val[8], val[3], ALU.mult))
            then(dve.reciprocal(val[9], val[8]))
            then(dve.tensor_tensor(w, top1, top2, ALU.add))
            then(dve.tensor_tensor(w, w, ex[:, :, 4:8], ALU.mult))
            then(dve.tensor_tensor(w, w, wide(val[9]), ALU.mult))
            dve.tensor_tensor(route[:, 11, :, :].rearrange("p t (g e) -> p t g e", g=N_GRP),
                              w.unsqueeze(2).to_broadcast([P, NTT, N_GRP, PER_GRP]),
                              group.unsqueeze(3).to_broadcast([P, NTT, N_GRP, PER_GRP]), ALU.mult).then_inc(dve_ready, 1)
            for j in range(1, (HEAD + 1) // 2):
                if j > 1:
                    dve.wait_ge(lin_free, R["moe_b"] + 2 * j - 1)
                expert_gate(0, j, R["moe_b"] - 1)
            dve.wait_ge(lin_free, R["combT"] + 1)
            dve.tensor_tensor(SQ[0:N_EXP, 0, 0:T2], SQ[0:N_EXP, 0, 0:T2], TS[0:N_EXP, 2, 0:T2], ALU.mult).then_inc(scaled, 1)
            dve.wait_ge(lin_free, R["cb"] + N_EXP)
            before, per = steps[0], 8

            def expert_group(i, outputs, head=0, gates=0):
                steps[0] = i * per + before
                r, e = R["moe"] - HEAD, E0["moe"]
                for j in range(C):
                    y = TS[:, j % 2, 0:T2]
                    if j >= gates:
                        expert_gate(i, j, r)
                    if j >= head:
                        dve.wait_ge(silu_done, i * C + j + 1)
                        dve.wait_ge(lin_free, r + i * 24 + 2 * j + 2)
                        dve.tensor_tensor(y, staged(e + 2 * j, T2), staged(e + 2 * j + 1, T2), ALU.mult).then_inc(ev_used, 1)
                    dve.wait_ge(ev_used, e + i * 24 + 2 * j + 1)
                    dve.tensor_tensor(y, y, CB[:, i * PER_GRP + j // 2, :], ALU.mult).then_inc(ev_used, 1)
                    dve.wait_ge(ev_used, e + i * 24 + 2 * j + 2)
                    if j == 0:
                        dve.wait_ge(unit_used, U["moe"] + i * 24)
                    parts(y, o_hi(j, T2), o_lo(j, T2)).then_inc(hid_ready, 1)
                for j in range(C):
                    dve.wait_ge(lin_free, r + i * 24 + 16 + j + 1)
                    dve.tensor_tensor(H[:, j, META:T1], H[:, j, META:T1], staged(e + 16 + j, T2), ALU.add).then_inc(ev_used, 1)
                    outputs(j)

            def next_input(c):
                if c:
                    add_both(c - 1)
                dve.wait_ge(ev_used, E0["moe"] + (N_GRP - 1) * 24 + 16 + c + 1)
                if c == 0:
                    dve.wait_ge(hid_ready, HID0["moe"] + N_GRP * C)
                    dve.wait_ge(unit_used, U["moe"] + (N_GRP - 1) * 24 + 16)
                x = X0["na0"] + c
                dve.wait_ge(x_ready, x - 1)
                dve.tensor_scalar(TS[:, c % 2, 0:T2], H[:, c, META:T1], vec("final1", c), vec("attn0", c), ALU.mult, ALU.mult)\
                   .then_inc(y_ready, 1)
                dve.wait_ge(hi_ready, x + 1)
                dve.tensor_tensor(XL[:, c, META:T1], TS[:, c % 2, 0:T2], XH[:, c, META:T1].bitcast(F32), ALU.subtract).then_inc(x_ready, 1)

            def add_both(c):
                dve.wait_ge(sq_ready, SQ0["nf1"] + c + 1)
                g = gain_sq[:, c:c + 1]
                if c == 0:
                    dve.tensor_scalar(TS[:, 2, 0:T2], SQ[:, 0, 0:T2], g, None, ALU.mult).then_inc(two_added, 1)
                    return
                dve.wait_ge(two_added, 2 * c - 1)
                dve.tensor_tensor(SQ[:, 0, 0:T2], SQ[:, 0, 0:T2], SQ[:, 1, 0:T2], ALU.add).then_inc(two_added, 1)
                dve.scalar_tensor_tensor(out=TS[:, 2, 0:T2], in0=SQ[:, 1, 0:T2], scalar=g, in1=TS[:, 2, 0:T2], op0=ALU.mult, op1=ALU.add)\
                   .then_inc(two_added, 1)

            expert_group(0, lambda j: None, 1, (HEAD + 1) // 2)
            with dve.Fori(1, N_GRP - 1) as i:
                expert_group(i, lambda j: None)
            expert_group(N_GRP - 1, next_input)
            add_both(C - 1)
            steps[0] = before + per * N_GRP
            dve.wait_ge(act_done, DONE0["nf1"] + 1)
            root1, both = TS[:, 2, 0:T2], SQ[:, 0, 0:T2]
            then(dve.reciprocal(root1, root1))
            dve.wait_ge(x_ready, X0["na0"] + C)
            dve.scalar_tensor_tensor(out=TS[:, 0, 0:T2], in0=pair(R["nf1"])[:, 1, :], scalar=1.0 / D, in1=root1, op0=ALU.mult, op1=ALU.mult)\
               .then_inc(lin_free, 1)
            dve.wait_ge(lin_free, R["nf1"] + 1)
            dve.tensor_tensor(TS[:, 0, 0:T2], TS[:, 0, 0:T2], root1, ALU.mult).then_inc(act_asked, 1)
            dve.wait_ge(act_done, DONE0["nf1"] + 2)
            then(dve.reciprocal(TS[:, 0, 0:T2], TS[:, 0, 0:T2]))
            then(dve.tensor_tensor(both, TS[:, 0, 0:T2], root1, ALU.mult))
            for c in range(4):
                dve.wait_ge(lin_free, R["kc"] + c + 1 if c < 2 else R["vc"] + c - 1)
                eo = EO[:, c, :, :]
                dve.tensor_tensor(eo, eo, both.rearrange("p (n a) -> p a n", a=2), ALU.mult).then_inc(scaled, 1)

            def over_roots(c):
                dve.wait_ge(lin_free, R["tok2"] + turning_order(5).index((c, False)) + 1)
                dve.tensor_tensor(spare(c, T2), spare(c, T2), both, ALU.mult).then_inc(scaled, 1)

            def blocks(kv):
                for b in range(CMP_B // 2):
                    ins = dve.tensor_scalar(BLK[:, b, :].rearrange("p (g n) -> p g n", g=A_G),
                                            PAIR[:, 2 * kv:2 * kv + 2, :, b:b + 8 * (NC - 1) + 1:8].rearrange("p q g n -> p (q g) n"),
                                            vec("cpos", kv * (CMP_B // 2) + b), None, ALU.add)
                    if b == CMP_B // 2 - 1:
                        then(ins)

            def low_part(m):
                n = U["cmp"] + m
                dve.wait_ge(hi_split, n + 1)
                dve.wait_ge(split_ready, n)
                dve.tensor_tensor(w_lo[:, n % SPLIT, :], raw[:, n % RAW, :], w_hi[:, n % SPLIT, :].bitcast(F32),
                                  ALU.subtract).then_inc(split_ready, 1)

            over_roots(0)
            normed_in_place("final1", root1, range(0, C // 2))
            over_roots(1)
            normed_in_place("final1", root1, range(C // 2, C))
            then(dve.tensor_tensor(COSR2[:, :], const("cosq"), both, ALU.mult))
            then(dve.tensor_tensor(SINR2[:, :], const("sinq"), both, ALU.mult))
            over_roots(2)
            dve.wait_ge(lin_free, R["tok2"] + 3)
            for t in range(QT):
                g = gate48[:, t, 0:3 * NH:3]
                ins = dve.tensor_scalar(g, g, vec("cvalid", t), None, ALU.mult)
                then(ins)
            dve.wait_ge(pairs_moved, 64)
            blocks(0)
            over_roots(3)
            parts(BLK[:, :, :], BLKH[:, :, :], BLKL[:, :, :]).then_inc(dve_ready, 1)
            low_part(0)
            over_roots(4)
            low_part(1)
            dve.wait_ge(dve_ready, 8)
            blocks(1)
            for m in range(2, 5):
                low_part(m)
            dve.wait_ge(unit_used, U["cmp"] + 4)
            parts(BLK[:, :, :], BLKH[:, :, :], BLKL[:, :, :]).then_inc(dve_ready, 1)
            for m in range(5, CMP_UNITS):
                low_part(m)
            dve.wait_ge(scaled, 11)
            zero_other_heads()
            dve.wait_ge(lin_free, R["cmp"] + 7)
            k_, kr = (staged(E0["cmp"] + x, 2 * NC).rearrange("p (g n) -> p g n", g=2) for x in range(2))
            cosc, sinc = (const(x).unsqueeze(1).to_broadcast([P, 2, NC]) for x in ("cosc", "sinc"))
            ta, tb = (TS[:, x, 0:2 * NC].rearrange("p (g n) -> p g n", g=2) for x in range(2))
            dve.tensor_tensor(ta, k_, cosc, ALU.mult).then_inc(ev_used, 1)
            dve.tensor_tensor(tb, kr, sinc, ALU.mult).then_inc(ev_used, 1)
            dve.wait_ge(ev_used, E0["cmp"] + 2)
            dve.tensor_tensor(KCMP[:, :, 0:NC], ta, tb, ALU.add).then_inc(rope_ready, 1)
            rotated("rope2", 12, lambda c: KSEL[:, c, :] if c < 2 else KWIN[:, c - 2, :] if c < 4 else Q2[:, c - 4, :],
                    COSR2[:, :], SINR2[:, :])

            attention("nsa0")
            attention("nsa1")
            residual("wo2", T2, "nf0", "ffn0")
            reciprocal_root(R["nf0"], T2)
            ffn(0)
            reciprocal_root(R["na1"], T2)
            dve.tensor_tensor(COSR[:, :], const("cosq"), TS[:, 2, 0:T2], ALU.mult).then_inc(mask_ready, 1)
            dve.tensor_tensor(SINR[:, :], const("sinq"), TS[:, 2, 0:T2], ALU.mult).then_inc(mask_ready, 1)
            zero_other_heads()
            dve.tensor_copy(IDR[:, :], ident).then_inc(mask_ready, 1)
            dve.tensor_copy(BANDR[:, :], const("band")).then_inc(mask_ready, 1)
            dve.wait_ge(mask_ready, 2)
            dve.wait_ge(unit_used, U["q3"])

            def kv_input(c):
                for x in kv_chunks(c):
                    dve.wait_ge(rope_ready, ROPE0["q3"] + c + 1)
                    dve.wait_ge(x_ready, X0["kv"] + x)
                    dve.tensor_scalar(TS[:, x % 2, 0:T2], H[:, x, META:T1], vec("kv", x), None, ALU.mult).then_inc(y_ready, 1)
                    dve.wait_ge(hi_ready, X0["kv"] + x + 1)
                    dve.tensor_tensor(o_lo(x, T2), TS[:, x % 2, 0:T2], o_hi(x, T2).bitcast(F32), ALU.subtract).then_inc(x_ready, 1)

            rotated("q3", 8, lambda c: Q3[:, c, :], COSR[:, :], SINR[:, :], kv_input)
            dve.wait_ge(unit_used, U["v3"] + 1)
            dve.tensor_tensor(VFM[:, :], pair(R["kv3"] + 1)[:, 0, :], TS[:, 2, 0:T2], ALU.mult).then_inc(scaled, 1)
            dve.wait_ge(lin_free, R["kv3"] + 2)
            dve.wait_ge(rope_ready, ROPE0["k3"])
            e = E0["k3"]
            dve.tensor_tensor(TS[:, 0, 0:T2], staged(e, T2), COSR[:, :], ALU.mult).then_inc(ev_used, 1)
            dve.tensor_tensor(TS[:, 1, 0:T2], staged(e + 1, T2), SINR[:, :], ALU.mult).then_inc(ev_used, 1)
            dve.wait_ge(ev_used, e + 2)
            dve.tensor_tensor(K3[:, :], TS[:, 0, 0:T2], TS[:, 1, 0:T2], ALU.add).then_inc(rope_ready, 1)

            attention("swa")
            residual("wo3", T2, "nf_1", "ffn1")
            reciprocal_root(R["nf_1"], T2)
            ffn(1)
            reciprocal_root(R["nfin"], T2)
            normed_in_place("final2", TS[:, 2, 0:T2])


def units_of(w):
    rows, cols = w.shape
    w = w.reshape(rows // UNIT, KC, P, cols // P, P).transpose(3, 0, 2, 1, 4)
    return w.reshape(-1, P, UNIT)


def padded(w, cols):
    out = np.zeros((w.shape[0], cols), np.float32)
    out[:, :w.shape[1]] = w
    return out


def lay_stream(a):
    w = np.asarray(a["w_in"])[0]
    cut = np.cumsum([POOL_W, CONV_W, CONV_W, FOX_W, FOX_W, FOX_W, FOX_H])
    pool, bv, bg, q, k, v, fg, gates = np.split(w, cut, axis=1)
    seq = [units_of(x) for x in (pool, bv, bg, padded(fg, P), q, v, k)]
    branch = units_of(np.concatenate([np.asarray(a[n])[0] for n in ("w_out_a", "w_out_b", "w_out_c")], axis=0))
    gate = units_of(gates).reshape(3, C, P, UNIT)
    seq.append(np.concatenate([gate, branch[None]], axis=0).transpose(1, 0, 2, 3).reshape(-1, P, UNIT))
    seq.append(units_of(np.asarray(a["w_o"])[0]))
    seq.append(units_of(padded(np.concatenate([np.asarray(a["router_g"])[0], np.asarray(a["router_e"])[0]], axis=1), P)))
    w1, w3, w2 = (np.asarray(a[n])[0] for n in ("exp_w1", "exp_w3", "exp_w2"))
    for g in range(N_GRP):
        for e in range(g * PER_GRP, (g + 1) * PER_GRP):
            seq.append(np.stack([units_of(w1[e]), units_of(w3[e])], axis=1).reshape(-1, P, UNIT))
        seq.append(units_of(w2[g * PER_GRP:(g + 1) * PER_GRP].reshape(PER_GRP * EXP_HID, D)))
    w = np.asarray(a["a_w_in_2"])[0]
    q, kc, vc, ks, vs, kw, vw, gl = np.split(w, np.cumsum([NH * HD] + [A_G * HD] * 6), axis=1)
    q = q.reshape(D, 2, 2, 4, HD).transpose(0, 1, 3, 2, 4).reshape(D, D)
    seq += [units_of(x) for x in (kc, vc, padded(gl, P), vs, vw)]
    c1 = np.asarray(a["a_cmp_w1_2"])[0]
    seq += [units_of(c1[0]), units_of(c1[1])]
    wo = np.asarray(a["a_w_out_2"])[0].reshape(2, 2, 4, HD, D).transpose(0, 2, 1, 3, 4).reshape(D, D)
    seq += [units_of(x) for x in (ks, kw, q, wo)]

    def ffn(layer):
        w = units_of(np.asarray(a["ffn_w_in_2"])[layer]).reshape(2, FC, P, UNIT).transpose(1, 0, 2, 3).reshape(-1, P, UNIT)
        o = np.zeros((3 * UNIT, D), np.float32)
        o[:DFF] = np.asarray(a["ffn_w_out_2"])[layer]
        return [w, units_of(o)]

    seq += ffn(0)
    k, v = np.split(np.asarray(a["b_w_kv_2"]), 2, axis=1)
    q = np.asarray(a["b_w_q_2"])[0].reshape(D, B_G, 8, HD).transpose(0, 2, 1, 3).reshape(D, D)
    wo = np.asarray(a["b_w_out_2"])[0].reshape(B_G, 8, HD, D).transpose(1, 0, 2, 3).reshape(D, D)
    seq += [units_of(x) for x in (q, k, v, wo)]
    seq += ffn(1)
    out = np.concatenate(seq, axis=0)
    assert out.shape == (N_UNITS, P, UNIT), out.shape
    return np.ascontiguousarray(out)


def lay_vecs(a):
    def cols(x):
        return np.asarray(x).reshape(-1, P).T

    def rows(x):
        return np.tile(np.asarray(x).reshape(1, -1), (P, 1))

    out = {"norm1": cols(a["norm1_g"]), "norm2": cols(a["norm2_g"]), "final1": cols(a["final_g"]),
           "attn0": cols(np.asarray(a["norm_attn_2"])[0]), "attn1": cols(np.asarray(a["norm_attn_2"])[1]),
           "ffn0": cols(np.asarray(a["norm_ffn_2"])[0]), "ffn1": cols(np.asarray(a["norm_ffn_2"])[1]),
           "kv": cols(a["kv_norm_2"]), "final2": cols(a["final_norm_2"]), "pool_b": cols(a["pool_b"]), "pool_s": cols(a["pool_scale"]),
           "conv_b": cols(a["conv_b"]), "ln_g": cols(a["conv_ln_g"]), "ln_b": cols(a["conv_ln_b"]),
           "conv_w": np.asarray(a["conv_w"])[0].T.reshape(2, P, KS).transpose(1, 0, 2).reshape(P, 2 * KS),
           "bforget": np.concatenate([np.asarray(a["b_forget"]).reshape(-1, 1), np.zeros((P - FOX_H, 1), np.float32)]),
           "sink": rows(a["b_sinks_2"]),
           "rbias": np.concatenate([rows(a["router_g_b"]), rows(a["router_e_b"])], axis=1),
           "prio": rows(np.arange(4, 0, -1, dtype=np.float32)), "eps": np.full((P, 1), EPS), "one": np.ones((P, 1)),
           "cpos": np.asarray(a["a_cmp_pos_2"])[0].reshape(2, CMP_B // 2, P).transpose(2, 0, 1).reshape(P, -1)}
    valid = (np.arange(SEQ) >= CMP_B - 1).astype(np.float32)
    out["cvalid"] = valid.reshape(QT, P).T
    for layer in range(2):
        w = np.concatenate([np.asarray(a["ffn_conv_w_2"])[layer], np.asarray(a["ffn_conv_b_2"])[layer][None]], axis=0)
        out[f"fw{layer}"] = w.reshape(4, 2, FC, P).transpose(3, 2, 1, 0).reshape(P, -1)
    return np.ascontiguousarray(np.concatenate([out[n].astype(np.float32) for n, _ in VECS], axis=1))


def lay_consts(a):
    f = np.float32
    rot = np.zeros((P, P), f)
    half = HD // 2
    for h in range(2):
        for d in range(half):
            rot[h * HD + d + half, h * HD + d] = -1.0
            rot[h * HD + d, h * HD + d + half] = 1.0
    i, j = np.arange(P)[:, None], np.arange(P)[None, :]
    causal = np.where(j <= i, 0.0, NEG)
    band = np.concatenate([np.where(j > i, 0.0, NEG), causal], axis=1)
    ends = np.arange(NC) * CMP_S + CMP_B - 1
    cmask = np.where(ends[None, :] <= np.arange(SEQ)[:, None], 0.0, NEG).reshape(QT, P, NC).transpose(1, 0, 2).reshape(P, -1)
    angle = f(10000.0) ** (-np.arange(half, dtype=f) / f(half))

    def table(fn, pos):
        t = fn((pos.astype(f)[:, None] * angle[None, :]).astype(f)).T
        return np.concatenate([t] * 4, axis=0)

    pw = np.asarray(a["pool_w"])[0]
    poolw = np.zeros((P, 2 * P), f)
    for g in range(4):
        lo = HD * (g % 2)
        poolw[lo:lo + HD, (g // 2) * P + lo:(g // 2) * P + lo + HD] = pw[g]
    w2 = np.asarray(a["a_cmp_w2_2"])[0].reshape(2, 2, P, HD)
    w2k = np.zeros((P, 2, 2, P), f)
    for j in range(2):
        w2k[:, j, 0, 0:HD] = w2[0, j]
        w2k[:, j, 1, HD:P] = w2[0, j]
    pos = np.arange(SEQ)
    out = {"ident": np.eye(P), "ones": np.ones((P, P)), "rot": rot, "causal": causal, "band": band, "poolw": poolw,
           "cosq": table(np.cos, pos), "sinq": table(np.sin, pos), "cosc": table(np.cos, ends), "sinc": table(np.sin, ends),
           "cmask": cmask, "w2k": w2k.reshape(P, -1), "w2v": w2[1].transpose(1, 0, 2).reshape(P, -1)}
    return np.ascontiguousarray(np.concatenate([out[n].astype(f) for n, _ in CONSTS], axis=1))


def lay_inverse_counts():
    out = np.zeros((P, 2, T1), np.float32)
    for g, window in enumerate((2, 4, 8, 16)):
        lo = HD * (g % 2)
        out[lo:lo + HD, g // 2, :] = 1.0 / np.minimum(np.arange(T1) + 1, window)
    return out


def kernel(**inputs):
    import concourse.bacc as bacc
    from concourse.bass_utils import run_bass_kernel_spmd

    h = np.concatenate([np.asarray(inputs["meta"]), np.asarray(inputs["x"])[0]], axis=0)
    arrays = {"stream": lay_stream(inputs), "x_fm": np.ascontiguousarray(h.T.reshape(C, P, T1).transpose(1, 0, 2)),
              "vecs_in": lay_vecs(inputs), "consts_in": lay_consts(inputs), "inv_counts": lay_inverse_counts()}
    nc = bacc.Bacc("TRN2", target_bir_lowering=False, num_devices=1)
    aps = [nc.dram_tensor(n, x.shape, F32, kind="ExternalInput").ap() for n, x in arrays.items()]
    out = nc.dram_tensor("out_fm", [P, C, SEQ], F32, kind="ExternalOutput").ap()
    build(nc, *aps, out)
    got = run_bass_kernel_spmd(nc, [arrays], core_ids=[0]).results[0]["out_fm"]
    return np.ascontiguousarray(got.transpose(1, 0, 2).reshape(D, SEQ).T)[None]
```
